# Optimizing a Trainium2 kernel written in Bass

```python
import math
import jax, jax.numpy as jnp
from jax import lax
import numpy as np

D_MODEL = 1024
BATCH = 1
SEQ = 512
DEPTH = 1

SB_HEADS = 8
SB_HEAD_DIM = 64
SB_WIDTH = SB_HEADS * SB_HEAD_DIM
Q_BLOCK = 128
CONV_WIDTH = D_MODEL // 2
CONV_K = 3
MEM_LEN = 256
MEM_HEADS = 4
MEM_HEAD_DIM = D_MODEL // MEM_HEADS
FFN_HIDDEN = -(-8 * D_MODEL // (3 * 256)) * 256
EPS = 1e-6

IN_SPLITS = (SB_WIDTH, SB_WIDTH, SB_WIDTH, CONV_WIDTH, CONV_WIDTH, CONV_WIDTH, D_MODEL, D_MODEL)
IN_WIDTH = sum(IN_SPLITS)


def rms_norm(x, g):
    xf = x.astype(jnp.float32)
    var = jnp.mean(xf * xf, axis=-1, keepdims=True)
    return (xf * lax.rsqrt(var + EPS) * g.astype(jnp.float32)).astype(x.dtype)

def stick_breaking_attention(q, k, v):
    seq = q.shape[2]
    scale = 1.0 / math.sqrt(q.shape[-1])
    outs = []
    for blk in range(seq // Q_BLOCK):
        t0 = blk * Q_BLOCK
        n_keys = t0 + Q_BLOCK
        qb = q[:, :, t0:n_keys].astype(jnp.float32)
        kb = k[:, :, :n_keys].astype(jnp.float32)
        vb = v[:, :, :n_keys].astype(jnp.float32)
        z = jnp.einsum('bhqd,bhkd->bhqk', qb, kb) * scale
        q_pos = t0 + jnp.arange(Q_BLOCK)[:, None]
        k_pos = jnp.arange(n_keys)[None, :]
        mask = k_pos < q_pos
        log_fail = jnp.where(mask, jax.nn.log_sigmoid(-z), 0.0)
        log_later = lax.cumsum(log_fail, axis=3, reverse=True) - log_fail
        weights = jnp.where(mask, jnp.exp(jax.nn.log_sigmoid(z) + log_later), 0.0)
        outs.append(jnp.einsum('bhqk,bhkd->bhqd', weights, vb))
    return jnp.concatenate(outs, axis=2).astype(v.dtype)

def causal_depthwise_conv(u, w):
    c = u.shape[-1]
    return lax.conv_general_dilated(
        u, w[:, None, :].astype(u.dtype), window_strides=(1,), padding=((CONV_K - 1, 0),),
        dimension_numbers=('NWC', 'WIO', 'NWC'), feature_group_count=c)

def memory_cross_attention(h, m, w_q, w_kv, w_o):
    b, s, _ = h.shape
    mlen = m.shape[1]
    q = (h @ w_q).reshape(b, s, MEM_HEADS, MEM_HEAD_DIM)
    kv = (m @ w_kv).reshape(b, mlen, 2, MEM_HEADS, MEM_HEAD_DIM)
    k, v = kv[:, :, 0], kv[:, :, 1]
    scores = jnp.einsum('bshd,bmhd->bhsm', q.astype(jnp.float32), k.astype(jnp.float32))
    probs = jax.nn.softmax(scores / math.sqrt(MEM_HEAD_DIM), axis=-1)
    o = jnp.einsum('bhsm,bmhd->bshd', probs, v.astype(jnp.float32)).astype(h.dtype)
    return o.reshape(b, s, D_MODEL) @ w_o

def first_inputs(seed: int = 0) -> dict:
    key = jax.random.key(seed)
    ks = jax.random.split(key, 20)
    f32 = jnp.float32

    def w(k, shape, fan_in):
        return jax.random.normal(k, shape, f32) * (fan_in ** -0.5)

    def gain(k, shape):
        return 1.0 + 0.05 * jax.random.normal(k, shape, f32)

    return {
        "x": jax.random.normal(ks[0], (BATCH, SEQ, D_MODEL), f32),
        "mem": jax.random.normal(ks[1], (BATCH, MEM_LEN, D_MODEL), f32),
        "norm_mix": gain(ks[2], (DEPTH, D_MODEL)),
        "w_in": w(ks[3], (DEPTH, D_MODEL, IN_WIDTH), D_MODEL),
        "conv_w": w(ks[4], (DEPTH, CONV_K, CONV_WIDTH), CONV_K),
        "w_branch_a": w(ks[5], (DEPTH, SB_WIDTH, D_MODEL), SB_WIDTH),
        "w_branch_b": w(ks[6], (DEPTH, CONV_WIDTH, D_MODEL), CONV_WIDTH),
        "w_mix_out": w(ks[7], (DEPTH, D_MODEL, D_MODEL), D_MODEL),
        "norm_mem_q": gain(ks[8], (DEPTH, D_MODEL)),
        "norm_mem_kv": gain(ks[9], (DEPTH, D_MODEL)),
        "w_mem_q": w(ks[10], (DEPTH, D_MODEL, D_MODEL), D_MODEL),
        "w_mem_kv": w(ks[11], (DEPTH, D_MODEL, 2 * D_MODEL), D_MODEL),
        "w_mem_o": w(ks[12], (DEPTH, D_MODEL, D_MODEL), D_MODEL),
        "norm_ffn": gain(ks[13], (DEPTH, D_MODEL)),
        "w_ffn_in": w(ks[14], (DEPTH, D_MODEL, 2 * FFN_HIDDEN), D_MODEL),
        "w_ffn_out": w(ks[15], (DEPTH, FFN_HIDDEN, D_MODEL), FFN_HIDDEN),
        "norm_final": gain(ks[16], (D_MODEL,)),
    }

def first_block(x, mem, norm_mix, w_in, conv_w, w_branch_a, w_branch_b, w_mix_out,
              norm_mem_q, norm_mem_kv, w_mem_q, w_mem_kv, w_mem_o,
              norm_ffn, w_ffn_in, w_ffn_out, norm_final):
    b, s, _ = x.shape
    split_points = list(np.cumsum(IN_SPLITS)[:-1])
    for l in range(DEPTH):
        h = rms_norm(x, norm_mix[l])
        proj = h @ w_in[l]
        q_a, k_a, v_a, u_b, gate_b, gate_c, g_a, g_b = jnp.split(proj, split_points, axis=-1)

        def heads(t):
            return t.reshape(b, s, SB_HEADS, SB_HEAD_DIM).transpose(0, 2, 1, 3)

        o_a = stick_breaking_attention(heads(q_a), heads(k_a), heads(v_a))
        o_a = o_a.transpose(0, 2, 1, 3).reshape(b, s, SB_WIDTH)
        y_b = gate_b * causal_depthwise_conv(gate_c * u_b, conv_w[l])

        branch_a = o_a @ w_branch_a[l]
        branch_b = y_b @ w_branch_b[l]
        merged = jax.nn.sigmoid(g_a) * branch_a + jax.nn.sigmoid(g_b) * branch_b
        x = x + merged @ w_mix_out[l]

        x = x + memory_cross_attention(rms_norm(x, norm_mem_q[l]), rms_norm(mem, norm_mem_kv[l]),
                                       w_mem_q[l], w_mem_kv[l], w_mem_o[l])

        hf = rms_norm(x, norm_ffn[l])
        gate, up = jnp.split(hf @ w_ffn_in[l], 2, axis=-1)
        x = x + (jax.nn.silu(gate) * up) @ w_ffn_out[l]
    return rms_norm(x, norm_final)


GRID_W = 64
CTX_LEN = 256
N_MIXERS = 2
N_MOD = 6
NORM_EPS = 1e-6

NA_HEADS = 16
NA_HEAD_DIM = D_MODEL // NA_HEADS
NA_WIN_H = 8
NA_WIN_W = 16

HY_FILTER_WIDTH = 64
HY_EMB_DIM = 33
HY_BANDS = (HY_EMB_DIM - 1) // 2
HY_SHORT_WIDTH = 3
HY_DECAY_TARGET = 1e-2
HY_SHORT_DECAY_PCT = 0.3
HY_LONG_DECAY_PCT = 1.5

D_FF = 2816
FFN_CONV_WIDTH = 3


def rms_norm_2(x, gain):
    xf = x.astype(jnp.float32)
    y = xf * lax.rsqrt(jnp.mean(xf * xf, axis=-1, keepdims=True) + NORM_EPS)
    return (y * gain.astype(jnp.float32)).astype(x.dtype)

def adaln(cond, w_mod, b_mod):
    return jnp.split(jax.nn.silu(cond) @ w_mod + b_mod, N_MOD, axis=-1)

def modulate(h, shift, scale):
    return h * (1.0 + scale) + shift

def dwconv_centred(x, w, b):
    k = w.shape[0]
    L = x.shape[1]
    pad = k // 2
    xp = jnp.pad(x, ((0, 0), (pad, k - 1 - pad), (0, 0)))
    out = xp[:, 0:L] * w[0]
    for i in range(1, k):
        out = out + xp[:, i:i + L] * w[i]
    return out + b

def split_heads(t):
    return t.reshape(t.shape[0], t.shape[1], NA_HEADS, NA_HEAD_DIM)

def neighbourhood_attention(q, k, v, k_ctx, v_ctx, rpb):
    B, L, H, Dh = q.shape
    rows = L // GRID_W
    kh = min(NA_WIN_H, rows)
    kw = NA_WIN_W
    scale = Dh ** -0.5
    cols = np.arange(GRID_W)
    col_idx = (np.clip(cols - kw // 2, 0, GRID_W - kw)[:, None] + np.arange(kw)[None, :]).astype(np.int32)
    dc_idx = (col_idx - cols[:, None] + (NA_WIN_W - 1)).astype(np.int32)
    qg = jnp.moveaxis(q.reshape(B, rows, GRID_W, H, Dh), 1, 0)
    kg = k.reshape(B, rows, GRID_W, H, Dh)
    vg = v.reshape(B, rows, GRID_W, H, Dh)

    def one_row(args):
        r, q_row = args
        r0 = jnp.clip(r - kh // 2, 0, rows - kh)
        k_win = lax.dynamic_slice_in_dim(kg, r0, kh, axis=1)[:, :, col_idx]
        v_win = lax.dynamic_slice_in_dim(vg, r0, kh, axis=1)[:, :, col_idx]
        dr_idx = r0 + jnp.arange(kh, dtype=jnp.int32) - r + (NA_WIN_H - 1)
        bias = rpb[:, dr_idx[:, None, None], dc_idx[None, :, :]]
        s_loc = jnp.einsum('bqhd,biqjhd->bhqij', q_row, k_win) * scale + jnp.transpose(bias, (0, 2, 1, 3))[None]
        s_ctx = jnp.einsum('bqhd,bkhd->bhqk', q_row, k_ctx) * scale
        s = jnp.concatenate([s_loc.reshape(B, H, GRID_W, kh * kw), s_ctx], axis=-1)
        p = jax.nn.softmax(s.astype(jnp.float32), axis=-1).astype(v.dtype)
        p_loc = p[..., :kh * kw].reshape(B, H, GRID_W, kh, kw)
        return (jnp.einsum('bhqij,biqjhd->bqhd', p_loc, v_win)
                + jnp.einsum('bhqk,bkhd->bqhd', p[..., kh * kw:], v_ctx))

    out = lax.map(one_row, (jnp.arange(rows, dtype=jnp.int32), qg))
    return jnp.moveaxis(out, 0, 1).reshape(B, L, H * Dh)

def context_attention(q, k, v):
    s = jnp.einsum('bqhd,bkhd->bhqk', q, k) * (q.shape[-1] ** -0.5)
    p = jax.nn.softmax(s.astype(jnp.float32), axis=-1).astype(v.dtype)
    o = jnp.einsum('bhqk,bkhd->bqhd', p, v)
    return o.reshape(o.shape[0], o.shape[1], -1)

def hyena_filters(L, w1, b1, w2, b2, w3, b3, w_out, sin_freq):
    f32 = jnp.float32
    t = jnp.linspace(0.0, 1.0, L, dtype=f32)[:, None]
    w = (2.0 * math.pi / L) * jnp.arange(L, dtype=f32)[:, None]
    bands = jnp.linspace(1e-4, HY_BANDS - 1, HY_BANDS, dtype=f32)[None, :]
    z = jnp.concatenate([t, jnp.cos(bands * w), -jnp.sin(bands * w)], axis=-1)
    freq = sin_freq.astype(f32)
    hdn = jnp.sin(freq * (z @ w1.astype(f32) + b1.astype(f32)))
    hdn = jnp.sin(freq * (hdn @ w2.astype(f32) + b2.astype(f32)))
    hdn = jnp.sin(freq * (hdn @ w3.astype(f32) + b3.astype(f32)))
    h = (hdn @ w_out.astype(f32)).reshape(L, 2, D_MODEL)
    deltas = jnp.abs(jnp.linspace(math.log(HY_DECAY_TARGET) / HY_SHORT_DECAY_PCT,
                                  math.log(HY_DECAY_TARGET) / HY_LONG_DECAY_PCT, D_MODEL, dtype=f32))
    h = h * jnp.exp(-t * deltas)[:, None, :]
    h = h * lax.rsqrt(jnp.sum(h * h, axis=(0, 1), keepdims=True) + NORM_EPS)
    return jnp.concatenate([h[:, 0], jnp.zeros((1, D_MODEL), f32), h[:0:-1, 1]], axis=0)

def hyena_mixer(h, w_in, b_in, short_w, short_b, f_w1, f_b1, f_w2, f_b2, f_w3, f_b3, f_wout, f_freq,
                d_bias, w_out, b_out):
    L = h.shape[1]
    u = dwconv_centred(h @ w_in + b_in, short_w, short_b)
    x0, x1, v = jnp.split(u, 3, axis=-1)
    filt = hyena_filters(L, f_w1, f_b1, f_w2, f_b2, f_w3, f_b3, f_wout, f_freq)
    z = (v * x1).astype(jnp.float32)
    zf = jnp.fft.rfft(z, n=2 * L, axis=1)
    ff = jnp.fft.rfft(filt, n=2 * L, axis=0)
    y = jnp.fft.irfft(zf * ff[None], n=2 * L, axis=1)[:, :L] + z * d_bias.astype(jnp.float32)
    return (x0 * y.astype(h.dtype)) @ w_out + b_out

def conv_ffn(h, w_up, conv_w, conv_b, w_down):
    a, g = jnp.split(h @ w_up, 2, axis=-1)
    return (a * jax.nn.gelu(dwconv_centred(g, conv_w, conv_b), approximate=False)) @ w_down

def second_inputs(seed: int = 0) -> dict:
    key = jax.random.key(seed)
    ks = iter(jax.random.split(key, 48))

    def nrm(shape, scale):
        return scale * jax.random.normal(next(ks), shape, jnp.float32)

    D = D_MODEL
    inp = {}
    inp['x'] = nrm((BATCH, SEQ, D), 1.0)
    inp['c'] = nrm((BATCH, D), 1.0)
    inp['ctx'] = nrm((BATCH, CTX_LEN, D), 1.0)
    inp['c_ctx'] = nrm((D,), 1.0)
    inp['l0_w_mod'] = nrm((D, N_MOD * D), D ** -0.5)
    inp['l0_b_mod'] = nrm((N_MOD * D,), 0.02)
    inp['l0_norm1'] = 1.0 + nrm((D,), 0.05)
    inp['l0_norm2'] = 1.0 + nrm((D,), 0.05)
    inp['l0_na_w_qkv'] = nrm((D, 3 * D), D ** -0.5)
    inp['l0_na_q_gain'] = 1.0 + nrm((NA_HEAD_DIM,), 0.05)
    inp['l0_na_k_gain'] = 1.0 + nrm((NA_HEAD_DIM,), 0.05)
    inp['l0_na_rpb'] = nrm((NA_HEADS, 2 * NA_WIN_H - 1, 2 * NA_WIN_W - 1), 0.1)
    inp['l0_na_w_o'] = nrm((D, D), D ** -0.5)
    inp['l0_ffn_w_up'] = nrm((D, 2 * D_FF), D ** -0.5)
    inp['l0_ffn_conv_w'] = nrm((FFN_CONV_WIDTH, D_FF), FFN_CONV_WIDTH ** -0.5)
    inp['l0_ffn_conv_b'] = nrm((D_FF,), 0.02)
    inp['l0_ffn_w_down'] = nrm((D_FF, D), D_FF ** -0.5)
    inp['l1_w_mod'] = nrm((D, N_MOD * D), D ** -0.5)
    inp['l1_b_mod'] = nrm((N_MOD * D,), 0.02)
    inp['l1_norm1'] = 1.0 + nrm((D,), 0.05)
    inp['l1_norm2'] = 1.0 + nrm((D,), 0.05)
    inp['l1_hy_w_in'] = nrm((D, 3 * D), D ** -0.5)
    inp['l1_hy_b_in'] = nrm((3 * D,), 0.02)
    inp['l1_hy_short_w'] = nrm((HY_SHORT_WIDTH, 3 * D), HY_SHORT_WIDTH ** -0.5)
    inp['l1_hy_short_b'] = nrm((3 * D,), 0.02)
    inp['l1_hy_f_w1'] = nrm((HY_EMB_DIM, HY_FILTER_WIDTH), HY_EMB_DIM ** -0.5)
    inp['l1_hy_f_b1'] = nrm((HY_FILTER_WIDTH,), 0.1)
    inp['l1_hy_f_w2'] = nrm((HY_FILTER_WIDTH, HY_FILTER_WIDTH), HY_FILTER_WIDTH ** -0.5)
    inp['l1_hy_f_b2'] = nrm((HY_FILTER_WIDTH,), 0.1)
    inp['l1_hy_f_w3'] = nrm((HY_FILTER_WIDTH, HY_FILTER_WIDTH), HY_FILTER_WIDTH ** -0.5)
    inp['l1_hy_f_b3'] = nrm((HY_FILTER_WIDTH,), 0.1)
    inp['l1_hy_f_wout'] = nrm((HY_FILTER_WIDTH, 2 * D), HY_FILTER_WIDTH ** -0.5)
    inp['l1_hy_f_freq'] = 1.0 + nrm((HY_FILTER_WIDTH,), 0.05)
    inp['l1_hy_d_bias'] = nrm((D,), 1.0)
    inp['l1_hy_w_out'] = nrm((D, D), D ** -0.5)
    inp['l1_hy_b_out'] = nrm((D,), 0.02)
    inp['l1_ffn_w_up'] = nrm((D, 2 * D_FF), D ** -0.5)
    inp['l1_ffn_conv_w'] = nrm((FFN_CONV_WIDTH, D_FF), FFN_CONV_WIDTH ** -0.5)
    inp['l1_ffn_conv_b'] = nrm((D_FF,), 0.02)
    inp['l1_ffn_w_down'] = nrm((D_FF, D), D_FF ** -0.5)
    return inp

def second_block(x, c, ctx, c_ctx,
              l0_w_mod, l0_b_mod, l0_norm1, l0_norm2, l0_na_w_qkv, l0_na_q_gain, l0_na_k_gain, l0_na_rpb,
              l0_na_w_o, l0_ffn_w_up, l0_ffn_conv_w, l0_ffn_conv_b, l0_ffn_w_down,
              l1_w_mod, l1_b_mod, l1_norm1, l1_norm2, l1_hy_w_in, l1_hy_b_in, l1_hy_short_w, l1_hy_short_b,
              l1_hy_f_w1, l1_hy_f_b1, l1_hy_f_w2, l1_hy_f_b2, l1_hy_f_w3, l1_hy_f_b3, l1_hy_f_wout, l1_hy_f_freq,
              l1_hy_d_bias, l1_hy_w_out, l1_hy_b_out, l1_ffn_w_up, l1_ffn_conv_w, l1_ffn_conv_b, l1_ffn_w_down):
    layers = [
        dict(w_mod=l0_w_mod, b_mod=l0_b_mod, norm1=l0_norm1, norm2=l0_norm2,
             mixer=(l0_na_w_qkv, l0_na_q_gain, l0_na_k_gain, l0_na_rpb, l0_na_w_o),
             ffn=(l0_ffn_w_up, l0_ffn_conv_w, l0_ffn_conv_b, l0_ffn_w_down)),
        dict(w_mod=l1_w_mod, b_mod=l1_b_mod, norm1=l1_norm1, norm2=l1_norm2,
             mixer=(l1_hy_w_in, l1_hy_b_in, l1_hy_short_w, l1_hy_short_b, l1_hy_f_w1, l1_hy_f_b1,
                    l1_hy_f_w2, l1_hy_f_b2, l1_hy_f_w3, l1_hy_f_b3, l1_hy_f_wout, l1_hy_f_freq,
                    l1_hy_d_bias, l1_hy_w_out, l1_hy_b_out),
             ffn=(l1_ffn_w_up, l1_ffn_conv_w, l1_ffn_conv_b, l1_ffn_w_down)),
    ]
    xc = ctx
    for i in range(DEPTH):
        p = layers[i]
        ctx_read_later = any(j % N_MIXERS == 0 for j in range(i + 1, DEPTH))
        sh1, sc1, g1, sh2, sc2, g2 = adaln(c[:, None, :], p['w_mod'], p['b_mod'])
        csh1, csc1, cg1, csh2, csc2, cg2 = adaln(c_ctx[None, None, :], p['w_mod'], p['b_mod'])
        h = modulate(rms_norm_2(x, p['norm1']), sh1, sc1)
        hc = modulate(rms_norm_2(xc, p['norm1']), csh1, csc1)
        if i % N_MIXERS == 0:
            w_qkv, q_gain, k_gain, rpb, w_o = p['mixer']
            w_q, w_k, w_v = jnp.split(w_qkv, 3, axis=1)
            q = rms_norm_2(split_heads(h @ w_q), q_gain)
            k = rms_norm_2(split_heads(h @ w_k), k_gain)
            v = split_heads(h @ w_v)
            kc = rms_norm_2(split_heads(hc @ w_k), k_gain)
            vc = split_heads(hc @ w_v)
            y = neighbourhood_attention(q, k, v, kc, vc, rpb) @ w_o
            if ctx_read_later:
                qc = rms_norm_2(split_heads(hc @ w_q), q_gain)
                yc = context_attention(qc, kc, vc) @ w_o
        else:
            y = hyena_mixer(h, *p['mixer'])
            if ctx_read_later:
                yc = hyena_mixer(hc, *p['mixer'])
        x = x + g1 * y
        x = x + g2 * conv_ffn(modulate(rms_norm_2(x, p['norm2']), sh2, sc2), *p['ffn'])
        if ctx_read_later:
            xc = xc + cg1 * yc
            xc = xc + cg2 * conv_ffn(modulate(rms_norm_2(xc, p['norm2']), csh2, csc2), *p['ffn'])
    return x


def setup_inputs(seed=0):
    out = dict(first_inputs(seed))
    for name, value in second_inputs(seed + 1).items():
        if name != "x":
            out[name + "_2"] = value
    return out


def reference(
    x, mem, norm_mix, w_in, conv_w, w_branch_a, w_branch_b, w_mix_out, norm_mem_q, norm_mem_kv,
    w_mem_q, w_mem_kv, w_mem_o, norm_ffn, w_ffn_in, w_ffn_out, norm_final, c_2, ctx_2, c_ctx_2,
    l0_w_mod_2, l0_b_mod_2, l0_norm1_2, l0_norm2_2, l0_na_w_qkv_2, l0_na_q_gain_2,
    l0_na_k_gain_2, l0_na_rpb_2, l0_na_w_o_2, l0_ffn_w_up_2, l0_ffn_conv_w_2, l0_ffn_conv_b_2,
    l0_ffn_w_down_2, l1_w_mod_2, l1_b_mod_2, l1_norm1_2, l1_norm2_2, l1_hy_w_in_2, l1_hy_b_in_2,
    l1_hy_short_w_2, l1_hy_short_b_2, l1_hy_f_w1_2, l1_hy_f_b1_2, l1_hy_f_w2_2, l1_hy_f_b2_2,
    l1_hy_f_w3_2, l1_hy_f_b3_2, l1_hy_f_wout_2, l1_hy_f_freq_2, l1_hy_d_bias_2, l1_hy_w_out_2,
    l1_hy_b_out_2, l1_ffn_w_up_2, l1_ffn_conv_w_2, l1_ffn_conv_b_2, l1_ffn_w_down_2,
):
    x = first_block(
        x, mem, norm_mix, w_in, conv_w, w_branch_a, w_branch_b, w_mix_out, norm_mem_q,
        norm_mem_kv, w_mem_q, w_mem_kv, w_mem_o, norm_ffn, w_ffn_in, w_ffn_out, norm_final,
    )
    return second_block(
        x, c_2, ctx_2, c_ctx_2, l0_w_mod_2, l0_b_mod_2, l0_norm1_2, l0_norm2_2, l0_na_w_qkv_2,
        l0_na_q_gain_2, l0_na_k_gain_2, l0_na_rpb_2, l0_na_w_o_2, l0_ffn_w_up_2,
        l0_ffn_conv_w_2, l0_ffn_conv_b_2, l0_ffn_w_down_2, l1_w_mod_2, l1_b_mod_2, l1_norm1_2,
        l1_norm2_2, l1_hy_w_in_2, l1_hy_b_in_2, l1_hy_short_w_2, l1_hy_short_b_2, l1_hy_f_w1_2,
        l1_hy_f_b1_2, l1_hy_f_w2_2, l1_hy_f_b2_2, l1_hy_f_w3_2, l1_hy_f_b3_2, l1_hy_f_wout_2,
        l1_hy_f_freq_2, l1_hy_d_bias_2, l1_hy_w_out_2, l1_hy_b_out_2, l1_ffn_w_up_2,
        l1_ffn_conv_w_2, l1_ffn_conv_b_2, l1_ffn_w_down_2,
    )


_drawn_inputs = setup_inputs


def setup_inputs(seed=0):
    import zlib

    import numpy as np

    out = dict(_drawn_inputs(seed))
    spreads = {}
    factors = {'norm_mem_q': 8.0,
     'norm_mem_kv': 7.546,
     'l0_norm1_2': 8.0,
     'l0_na_q_gain_2': 8.0,
     'l0_na_k_gain_2': 8.0,
     'l0_na_rpb_2': 8.0,
     'l0_ffn_conv_b_2': 29.532,
     'l0_norm2_2': 7.713}
    for name, (base, spread) in spreads.items():
        noise = np.random.default_rng([zlib.crc32(name.encode()), seed]).standard_normal(out[name].shape)
        drawn = base * np.exp(spread * noise) if base else spread * noise
        out[name] = __import__('jax').numpy.asarray(drawn.astype(out[name].dtype))
    for name, factor in factors.items():
        out[name] = (out[name] * factor).astype(out[name].dtype)
    return out
```

```python
import math
from contextlib import ExitStack

import numpy as np
import concourse.bass as bass
from concourse import mybir

F32 = mybir.dt.float32
F32R = mybir.dt.float32r
ACT = mybir.ActivationFunctionType
ALU = mybir.AluOpType
AX = mybir.AxisListType

P = 128
SEQ, MEM, CTX, D = 512, 256, 256, 1024
KT = D // P
TT = SEQ // P
SB_HEADS, SB_DIM = 8, 64
MEM_HEADS, MEM_DIM = 4, 256
FF = 2816
FT = FF // P
FH = FT // 2
GRID_W, GRID_H = 64, 8
NA_HEADS, NA_DIM, WIN_W = 16, 64, 16
EPS = 1e-6
NEG = -1.0e30

C_IDENT, C_TRI, C_ONES, C_MASK, C_ONE, C_EPS, C_HEADS, C_WIN = 0, 128, 256, 384, 512, 513, 514, 516
C_ALL = C_WIN + 96

LAYERS = [("qk", 4, 2048), ("v", 2, 2048), ("conv_in", 4, 2048), ("conv_gate", 2, 2048), ("gates", 8, 2048),
          ("branch", 4, 2048), ("mix", 4, 2048), ("mem_kv", 8, 2048), ("mem_q", 4, 2048), ("mem_o", 4, 2048),
          ("up0", FH, 2048), ("down0", KT, FH * P), ("up1", FH, 2048), ("down1", KT, FH * P),
          ("na_qkv", 12, 2048), ("na_o", 4, 2048),
          ("nup0", FH, 2048), ("ndown0", KT, FH * P), ("nup1", FH, 2048), ("ndown1", KT, FH * P)]
LAST_LAYER = "ndown1"


INPUTS = ["x", "mem", "norm_mix", "w_in", "conv_w", "w_branch_a", "w_branch_b", "w_mix_out", "norm_mem_q",
          "norm_mem_kv", "w_mem_q", "w_mem_kv", "w_mem_o", "norm_ffn", "w_ffn_in", "w_ffn_out", "norm_final",
          "c_2", "ctx_2", "c_ctx_2", "l0_w_mod_2", "l0_b_mod_2", "l0_norm1_2", "l0_norm2_2", "l0_na_w_qkv_2",
          "l0_na_q_gain_2", "l0_na_k_gain_2", "l0_na_rpb_2", "l0_na_w_o_2", "l0_ffn_w_up_2", "l0_ffn_conv_w_2",
          "l0_ffn_conv_b_2", "l0_ffn_w_down_2"]


def layer_table():
    table, at = {}, 0
    names = [x[0] for x in LAYERS]
    stop = names.index(LAST_LAYER) + 1
    for n, (name, units, size) in enumerate(LAYERS[:stop]):
        after = LAYERS[n + 1][2] if n + 1 < stop else 0
        table[name] = (at, units, size, after)
        at += units
    return table


def over(eng, n, base, body):
    if n <= 4:
        for i in range(n):
            body(i, (base + i) % 2, i == n - 1)
        return
    m = (n - 1) // 2 * 2
    with eng.Fori(0, m, 2) as i:
        body(i, base % 2, False)
        body(i + 1, (base + 1) % 2, False)
    for i in range(m, n):
        body(i, (base + i) % 2, i == n - 1)


def pairs(eng, n, body):
    with eng.Fori(0, n - 1, 1) as a:
        body(a, 0, False)
        body(a, 1, False)
    body(n - 1, 0, False)
    body(n - 1, 1, True)


def at(x, n=1):
    return bass.ds(x, n)


def constants():
    c = np.zeros((P, C_ALL), np.float32)
    r = np.arange(P)
    c[:, C_IDENT:C_IDENT + P] = np.eye(P)
    c[:, C_TRI:C_TRI + P] = np.where(r[:, None] >= r[None, :], -1.0, 0.0)
    c[:, C_ONES:C_ONES + P] = -1.0
    c[:, C_MASK:C_MASK + P] = np.where(r[:, None] >= r[None, :], NEG, 0.0)
    c[:, C_ONE] = 1.0
    c[:, C_EPS] = EPS
    c[0:64, C_HEADS] = 1.0
    c[64:128, C_HEADS + 1] = 1.0
    cl, jl = (r % 16)[:, None], np.arange(32)[None, :]
    for n, strip in enumerate((0, 1, 3)):
        col = 16 * strip + cl
        start = np.clip(col - WIN_W // 2, 0, GRID_W - WIN_W)
        key = min(max(16 * strip - 8, 0), 32) + jl
        c[:, C_WIN + 32 * n:C_WIN + 32 * n + 32] = np.where((key >= start) & (key < start + WIN_W), 0.0, NEG)
    return c


def program(nc, t, consts, out):
    tab = layer_table()
    n_units = sum(x[1] for x in tab.values())
    ctx = ExitStack()
    with ctx:
        base = 16512
        taken = [0]

        def place(name, off, shape, dt=F32):
            return nc.alloc_sbuf_tensor_at(name, shape, dt, offset=base + 4 * off)

        xT = place("xT", 0, [P, KT, SEQ])
        raw = [place(f"w_raw{s}", 4096 + 2048 * s, [P, 2048]) for s in range(2)]
        whi = [place(f"w_hi{s}", 8192 + 2048 * s, [P, 2048], F32R) for s in range(2)]
        wlo = [place(f"w_lo{s}", 12288 + 2048 * s, [P, 2048], F32R) for s in range(2)]
        h_hi = place("h_hi", 16384, [P, KT, SEQ], F32R)
        h_lo = place("h_lo", 20480, [P, KT, SEQ], F32R)
        cst = place("cst", 24576, [P, C_ALL])
        cstr = place("cstr", 25192, [P, 512], F32R)
        vecA = place("vecA", 25704, [P, 112])
        vecB = place("vecB", 25816, [P, 120])
        small = place("small", 25936, [P, 432])
        G = 26368

        ident = cst[:, C_IDENT:C_IDENT + P]
        one = cst[:, C_ONE:C_ONE + 1]
        eps = cst[:, C_EPS:C_EPS + 1]
        r_ident, r_tri, r_ones, r_mask = (cstr[:, P * n:P * n + P] for n in range(4))
        std = small[:, 0:4]
        rstd = small[:, 4:8]
        sumsq = small[:, 8:16]
        std0 = small[:, 16:24]
        rstd0 = small[:, 24:32]
        nmax = small[:, 32:40]
        den = small[:, 40:48]
        rden = small[:, 48:56]

        V_MIX, V_MQ, V_MKV, V_FFN, V_FIN, V_N1, V_N2, V_CONV, V_C, V_CC, V_QG, V_KG, V_CB = \
            0, 8, 16, 24, 32, 40, 48, 56, 68, 76, 84, 85, 86
        NA_ROWS = 108
        V_BMOD, V_CW = 0, 48
        NB_ROWS = 114
        vcol = lambda n: vecA[:, n:n + 1]

        tb = [place("tb0", G + 9728, [P, 512]), place("tb1", G + 24064, [P, 512])]
        tb3 = [tb[0], place("tb3", G + 11776, [P, 512])]
        sq = place("sq", G + 10240, [P, 2, SEQ])
        sqacc = place("sqacc", G + 11264, [P, SEQ])

        xn = place("x_rows", G + 16384, [P, TT, D])
        rowsA = place("rowsA", G + 20480, [P, P])
        rowsB = place("rowsB", G + 20608, [P, P])
        junk = place("junk", 16384, [P, D])
        qk_hi = place("qk_hi", G + 0, [P, 8, SEQ], F32R)
        qk_lo = place("qk_lo", G + 4096, [P, 8, SEQ], F32R)
        v_hi = place("v_hi", G + 8192, [P, TT, 512], F32R)
        v_lo = place("v_lo", G + 10240, [P, TT, 512], F32R)
        yb_hi = place("yb_hi", G + 12288, [P, 4, SEQ], F32R)
        yb_lo = place("yb_lo", G + 14336, [P, 4, SEQ], F32R)
        vraw = place("vraw", G + 16384, [P, 4, SEQ])
        usb = place("usb", G + 18432, [P, 2, SEQ])
        cu = place("cu", G + 19456, [P, 2, 516])
        cv = place("cv", G + 20488, [P, 4, SEQ])
        ybf = place("ybf", G + 22536, [P, 2, SEQ])
        sbT = [place(f"sbT{b}", G + 16384 + 5120 * b, [P, 1280]) for b in range(2)]
        sbS = [place(f"sbS{b}", G + 17664 + 5120 * b, [P, 1280]) for b in range(2)]
        sb_hi = [place(f"sb_hi{b}", G + 18944 + 5120 * b, [P, 1280], F32R) for b in range(2)]
        sb_lo = [place(f"sb_lo{b}", G + 20224 + 5120 * b, [P, 1280], F32R) for b in range(2)]
        mn = place("mn", G + 8192, [P, 4, D])
        hm_hi = place("hm_hi", G + 2048, [P, KT, MEM], F32R)
        hm_lo = place("hm_lo", G + 6144, [P, KT, MEM], F32R)
        ctxT = place("ctxT", G + 24576, [P, KT, CTX])
        sig = place("sig", G + 16384, [P, 2, KT, SEQ])
        mg = place("mg", G + 8192, [P, 2, SEQ])
        mt = place("mt", G + 9216, [P, 2, SEQ])
        vmraw = place("vmraw", G + 0, [P, KT, MEM])
        km_hi = place("km_hi", G + 12288, [P, KT, MEM], F32R)
        km_lo = place("km_lo", G + 14336, [P, KT, MEM], F32R)
        vm_hi = place("vm_hi", G + 16384, [P, 2, D], F32R)
        vm_lo = place("vm_lo", G + 18432, [P, 2, D], F32R)
        qm_hi = place("qm_hi", G + 0, [P, KT, SEQ], F32R)
        qm_lo = place("qm_lo", G + 4096, [P, KT, SEQ], F32R)
        em = place("em", G + 20480, [P, 2, TT, MEM])
        pt_hi = place("pt_hi", G + 22528, [P, 2, SEQ], F32R)
        pt_lo = place("pt_lo", G + 8192, [P, 2, SEQ], F32R)
        a_hi = place("a_hi", G + 0, [P, FH, SEQ], F32R)
        a_lo = place("a_lo", G + 16384, [P, FH, SEQ], F32R)
        sg = place("sg", G + 5632, [P, 2, SEQ])
        af = place("af", G + 6656, [P, 2, SEQ])

        mod_raw = [place(f"mod_raw{b}", G + 11776 + 2048 * b, [P, KT, 256]) for b in range(2)]
        mod_tmp = place("mod_tmp", G + 7680, [P, KT, 256])
        mod_acc = place("mod_acc", G + 22016, [P, 2048])
        MOD_GROUPS = [(0, 1024, True), (1024, 1024, True), (2048, 2048, False), (4096, 2048, False)]
        silu_c = small[:, 56:72]
        modv = small[:, 72:136]
        gain1, gain2, gain1c = (small[:, x:x + 8] for x in (136, 144, 152))
        qgain = small[:, 160:161]
        na_nmax_c, na_max, na_nmax = (small[:, x:x + 4] for x in (164, 168, 172))
        na_den = small[:, 176:184]
        na_dsum, na_rden = small[:, 184:188], small[:, 188:192]
        rpb_pad = place("rpb_pad", 25936 + 200, [120, 2, 48])
        hn_std = place("hn_std", 25936 + 296, [P, 24])
        hn_rstd = place("hn_rstd", 25936 + 320, [P, 24])
        q_hi = place("q_hi", G + 0, [P, KT, SEQ], F32R)
        q_raw = place("q_raw", G + 4096, [P, KT, SEQ])
        q_lo = place("q_lo", G + 4096, [P, KT, SEQ], F32R)
        k_hi = place("k_hi", G + 8192, [P, KT, SEQ], F32R)
        k_raw = place("k_raw", G + 12288, [P, KT, SEQ])
        k_lo = place("k_lo", G + 12288, [P, KT, SEQ], F32R)
        kc_hi = place("kc_hi", G + 16384, [P, KT, CTX], F32R)
        kc_raw = place("kc_raw", G + 18432, [P, KT, CTX])
        kc_lo = place("kc_lo", G + 18432, [P, KT, CTX], F32R)
        hc_hi = place("hc_hi", G + 20480, [P, KT, CTX], F32R)
        hc_lo = place("hc_lo", G + 22528, [P, KT, CTX], F32R)
        v_out = place("v_out", G + 24576, [P, 2, SEQ + CTX])
        hsq = place("hsq", G + 24576, [P, 2, SEQ])
        hsqc = place("hsqc", G + 25600, [P, 2, CTX])
        rexp = place("rexp", G + 26112, [P, 8, 64])
        vw = place("vw", G + 25344, [P, TT, 8, 32])
        tbk = place("tbk", G + 0, [P, 3, SEQ])
        tbq = place("tbq", G + 25600, [P, 1, SEQ])
        vt_h = [place(f"vt_h{b}", 16384 + 1280 * b, [P, 10, P], F32R) for b in range(2)]
        vt_l = [place(f"vt_l{b}", 18944 + 1280 * b, [P, 10, P], F32R) for b in range(2)]
        sc = place("sc", 21504, [P, 4, 512])
        np_hi = place("np_hi", 23552, [P, 2, 512], F32R)
        np_lo = place("np_lo", G + 24320, [P, 2, 512], F32R)
        vp = [place(f"vp{b}", G + 20480 + 768 * b, [P, SEQ + CTX]) for b in range(2)]
        bias = [place(f"bias{b}", G + 22016 + 768 * b, [P, 3, 8, 32]) for b in range(2)]
        gb = [place(f"gb{b}", G + 23552 + 384 * b, [P, 8, 48]) for b in range(2)]
        gs = place("gs", G + 5632, [P, 2, 516])
        gl = place("gl", G + 6664, [P, 2, SEQ])
        gc = place("gc", G + 7688, [P, 2, SEQ])
        gf = place("gf", G + 8712, [P, 2, SEQ])
        out_rows = place("out_rows", G + 16384, [P, TT, D])

        v_scr = nc.dram_tensor("v_scr", (KT, P, SEQ + CTX), F32).ap()
        PITCH = 15 * 48
        TABLE = NA_HEADS * PITCH
        COPY = TABLE + 32
        rpb_scr = nc.dram_tensor("rpb_scr", (16 * COPY + 16,), F32)
        bias_scr = nc.dram_tensor("bias_scr", (GRID_H, 16, NA_HEADS, GRID_H * 48), F32).ap()

        ps = ctx.enter_context(nc.psum_tensor("ps", [P, 8, 512], F32))

        def bank(n, cols=512):
            return ps[:, n, 0:cols]

        def sem(name):
            return ctx.enter_context(nc.semaphore(name))

        w_dma = [sem(f"w_dma{s}") for s in range(2)]
        w_hi, w_lo, pe_done, evac = sem("w_hi"), sem("w_lo"), sem("pe_done"), sem("evac")
        cst_in, vec_in = sem("cst_in"), sem("vec_in")
        x_in = [sem(f"x_in{n}") for n in range(TT)]
        mc_in = [sem(f"mc_in{n}") for n in range(4)]
        cstr_done, vec_T, vec_sb = sem("cstr_done"), sem("vec_T"), sem("vec_sb")
        ss_x, std_x, rstd_x = sem("ss_x"), sem("std_x"), sem("rstd_x")
        xT_ps, xT_dve, xT_act = sem("xT_ps"), sem("xT_dve"), sem("xT_act")
        stat_ps, std_done, rstd_done, r_ps = sem("stat_ps"), sem("std_done"), sem("rstd_done"), sem("r_ps")
        ht, hhi, hlo = sem("ht"), sem("hhi"), sem("hlo")
        x_sq, x_acc = sem("x_sq"), sem("x_acc")
        split_hi = sem("split_hi")
        usb_done, conv_step = sem("usb_done"), sem("conv_step")
        cu_zero = sem("cu_zero")
        ybf_done, yb_hi_done = sem("ybf_done"), sem("yb_hi_done")
        vt_ps, vt_hi, vt_lo = sem("vt_ps"), sem("vt_hi"), sem("vt_lo")
        z_ps, z_abs, z_exp, z_ln, sp_done, sp_hi, sp_lo = (sem(n) for n in (
            "z_ps", "z_abs", "z_exp", "z_ln", "sp_done", "sp_hi", "sp_lo"))
        tri_ps, wt_done, wt_hi, wt_lo, pv_ps, o_hi_done, o_lo_done = (sem(n) for n in (
            "tri_ps", "wt_done", "wt_hi", "wt_lo", "pv_ps", "o_hi_done", "o_lo_done"))
        mc_ss, mc_std, mc_rstd, mc_scaled, mc_T, mc_hi, mc_lo = (sem(n) for n in (
            "mc_ss", "mc_std", "mc_rstd", "mc_scaled", "mc_T", "mc_hi", "mc_lo"))
        sig_done = sem("sig_done")
        br_step, mg_done, mg_hi = sem("br_step"), sem("mg_done"), sem("mg_hi")
        ms_ps, ms_max, ms_exp, ms_rden, ms_norm, mp_ps, mp_hi, mp_lo, mo_ps, mo_hi, mo_lo = (sem(n) for n in (
            "ms_ps", "ms_max", "ms_exp", "ms_rden", "ms_norm", "mp_ps", "mp_hi", "mp_lo", "mo_ps", "mo_hi", "mo_lo"))
        silu_done, af_done, a_hi_done, a_lo_done = (sem(n) for n in ("silu_done", "af_done", "a_hi_done", "a_lo_done"))
        silu_c_done, mod_step, mod_ps, mod_sb, mod_vec = (sem(n) for n in (
            "silu_c_done", "mod_step", "mod_ps", "mod_sb", "mod_vec"))
        mod_in = [sem(f"mod_in{b}") for b in range(2)]
        rpb_zero, rpb_in, rpb_copy, rpb_out = sem("rpb_zero"), sem("rpb_in"), sem("rpb_copy"), sem("rpb_out")
        xfin, hc_t, hc_h, hc_l = sem("xfin"), sem("hc_t"), sem("hc_h"), sem("hc_l")
        v_spill = sem("v_spill")
        hn_sq, hn_ps, hn_sd, hn_rd, hn_x, hn_r, hn_t, hn_hi, hn_lo = (sem(n) for n in (
            "hn_sq", "hn_ps", "hn_sd", "hn_rd", "hn_x", "hn_r", "hn_t", "hn_hi", "hn_lo"))
        vw_done = sem("vw_done")
        vp_in = [sem(f"vp_in{b}") for b in range(2)]
        gb_in = [sem(f"gb_in{b}") for b in range(2)]
        bias_done = sem("bias_done")
        nv_ps, nv_hi, nv_lo = sem("nv_ps"), sem("nv_hi"), sem("nv_lo")
        ns_ps, ns_red, ns_max, ns_exp, ns_dsum, ns_rden, ns_norm = (sem(n) for n in (
            "ns_ps", "ns_red", "ns_max", "ns_exp", "ns_dsum", "ns_rden", "ns_norm"))
        np_ps, np_h, np_l, no_ps, no_hi, no_lo = (sem(n) for n in ("np_ps", "np_h", "np_l", "no_ps", "no_hi", "no_lo"))
        gs_zero, gs_done, gc_step, gl_done, gf_done, ga_hi = (sem(n) for n in (
            "gs_zero", "gs_done", "gc_step", "gl_done", "gf_done", "ga_hi"))
        out_T, out_sb, out_dma = sem("out_T"), sem("out_sb"), sem("out_dma")

        def hstat(with_context):
            return bank(6)[:, 0:24 if with_context else 16]

        def head_jobs(i):
            if 1 <= i <= 4:
                return [dict(j=i - 1, raw=k_raw, hi=k_hi, lo=k_lo, tmp=tbk, raw_c=kc_raw, hi_c=kc_hi, lo_c=kc_lo,
                             unit=i - 1, round=3 * (i - 1))]
            if 5 <= i <= 8:
                return [dict(j=i - 5, raw=q_raw, hi=q_hi, lo=q_lo, tmp=tbq, raw_c=None, hi_c=None, lo_c=None,
                             unit=i - 1, round=12 + 2 * (i - 5))]
            return []

        span = [0, 8, 24, 32]

        def grid(x):
            return x.rearrange("p (r c) -> p r c", c=GRID_W)

        def strips(x):
            return x.rearrange("p (t r c) -> p t r c", t=TT, c=16)

        def strips_of_rows(x):
            return x.rearrange("p (r t c) -> p t r c", t=TT, c=16)

        block = ctx.enter_context(nc.Block())

        @block.sync
        def _(sp):
            x_rows = t["x"].rearrange("b (n p) d -> (b n) p d", p=P)
            for n in range(TT):
                sp.dma_start(xn[:, n, :], x_rows[n]).then_inc(x_in[n], 16)

            def load(u, s, parts):
                if not isinstance(u, int) or u >= 2:
                    sp.wait_ge(w_lo, u - 1)
                for dst, src in parts:
                    sp.dma_start(dst, src).then_inc(w_dma[s], 16)

            def weights(name):
                return t[name].rearrange("l (k p) n -> p (l k) n", p=P)

            def pair_layer(name, w, col0=0):
                b, n, _, _ = tab[name]

                def body(i, s, last):
                    dst = raw[s][:, :].rearrange("p (k n) -> p k n", n=256)
                    load(b + i, s, [(dst[:, 4 * g:4 * g + 4, :], w[:, 4 * g:4 * g + 4, at(i * 256 + col0, 256)])
                                    for g in range(2)])
                over(sp, n, b, body)

            def two_layer(name, w, col_a, col_b):
                b, n, _, _ = tab[name]

                def body(i, s, last):
                    dst = raw[s][:, :].rearrange("p (k n) -> p k n", n=256)
                    load(b + i, s, [(dst[:, :, 128 * g:128 * g + 128], w[:, :, at(i * 128 + c, 128)])
                                    for g, c in enumerate((col_a, col_b))])
                over(sp, n, b, body)

            def down_layer(name, w, k0):
                b, n, _, _ = tab[name]

                def body(i, s, last):
                    dst = raw[s][:, 0:FH * P].rearrange("p (k n) -> p k n", n=P)
                    load(b + i, s, [(dst[:, lo:hi, :], w[:, k0 + lo:k0 + hi, at(i * 128, 128)])
                                    for lo, hi in ((0, 6), (6, FH))])
                over(sp, n, b, body)

            w_in = weights("w_in")
            pair_layer("qk", w_in, 0)
            pair_layer("v", w_in, 1024)
            two_layer("conv_in", w_in, 1536, 2560)
            pair_layer("conv_gate", w_in, 2048)
            two_layer("gates", w_in, 3072, 4096)
            b, n, _, _ = tab["branch"]
            w_a, w_b = weights("w_branch_a"), weights("w_branch_b")
            for i in range(n):
                s = (b + i) % 2
                dst = raw[s][:, :].rearrange("p (k n) -> p k n", n=256)
                load(b + i, s, [(dst[:, 0:4, :], w_a[:, :, 256 * i:256 * i + 256]),
                                (dst[:, 4:8, :], w_b[:, :, 256 * i:256 * i + 256])])
            pair_layer("mix", weights("w_mix_out"))
            pair_layer("mem_kv", weights("w_mem_kv"))
            pair_layer("mem_q", weights("w_mem_q"))
            pair_layer("mem_o", weights("w_mem_o"))
            two_layer("up0", weights("w_ffn_in"), 0, FF)
            down_layer("down0", weights("w_ffn_out"), 0)
            two_layer("up1", weights("w_ffn_in"), FH * P, FF + FH * P)
            down_layer("down1", weights("w_ffn_out"), FH)
            w_qkv = t["l0_na_w_qkv_2"].rearrange("(k p) n -> p k n", p=P)
            b, n, _, _ = tab["na_qkv"]
            for i in range(n):
                s = (b + i) % 2
                col = (1024, 0, 2048)[i // 4] + 256 * (i % 4)
                dst = raw[s][:, :].rearrange("p (k n) -> p k n", n=256)
                load(b + i, s, [(dst[:, 4 * g:4 * g + 4, :], w_qkv[:, 4 * g:4 * g + 4, col:col + 256]) for g in range(2)])
            pair_layer("na_o", t["l0_na_w_o_2"].rearrange("(k p) n -> p k n", p=P))
            w_up = t["l0_ffn_w_up_2"].rearrange("(k p) n -> p k n", p=P)
            w_down = t["l0_ffn_w_down_2"].rearrange("(k p) n -> p k n", p=P)
            two_layer("nup0", w_up, 0, FF)
            down_layer("ndown0", w_down, 0)
            two_layer("nup1", w_up, FH * P, FF + FH * P)
            down_layer("ndown1", w_down, FH)
            for n in range(TT):
                sp.wait_ge(out_sb, 2 * n + 2)
                sp.dma_start(out[0, n * P:n * P + P, :], out_rows[:, n, :]).then_inc(out_dma, 16)
            sp.wait_ge(out_dma, 16 * TT)

        @block.scalar
        def _(act):
            act.dma_start(cst[:, :], consts).then_inc(cst_in, 16)
            vec = [(rowsA, V_MIX, "norm_mix", 8), (rowsA, V_MQ, "norm_mem_q", 8), (rowsA, V_MKV, "norm_mem_kv", 8),
                   (rowsA, V_FFN, "norm_ffn", 8), (rowsA, V_FIN, "norm_final", 8), (rowsA, V_N1, "l0_norm1_2", 8),
                   (rowsA, V_N2, "l0_norm2_2", 8), (rowsA, V_CONV, "conv_w", 12), (rowsA, V_C, "c_2", 8),
                   (rowsA, V_CC, "c_ctx_2", 8), (rowsA, V_CB, "l0_ffn_conv_b_2", 22),
                   (rowsB, V_BMOD, "l0_b_mod_2", 48), (rowsB, V_CW, "l0_ffn_conv_w_2", 66)]
            for rows, r0, name, n in vec:
                src = t[name]
                letters = "abc"[:len(src.shape)]
                flat = src if len(src.shape) == 1 else src.rearrange(f"{' '.join(letters)} -> ({' '.join(letters)})")
                act.dma_start(rows[r0:r0 + n, :], flat.rearrange("(r p) -> r p", p=P)).then_inc(vec_in, 16)
            for r0, name in ((V_QG, "l0_na_q_gain_2"), (V_KG, "l0_na_k_gain_2")):
                for g in range(2):
                    act.dma_start(rowsA[r0:r0 + 1, 64 * g:64 * g + 64],
                                  t[name].rearrange("(r p) -> r p", r=1)).then_inc(vec_in, 16)
            n_vec = len(vec) + 4

            def split_w(u, s, size):
                act.wait_ge(w_dma[s], 16 * u + (32 if s == 0 else 16))
                if not isinstance(u, int) or u >= 2:
                    act.wait_ge(pe_done, u - 1)
                act.activation(whi[s][:, 0:size], raw[s][:, 0:size], ACT.Copy).then_inc(w_hi, 1)

            def next_split(name, i, s, last):
                b, _, size, after = tab[name]
                if not last or after:
                    split_w(b + i + 1, 1 - s, after if last else size)

            def norm_std(n):
                act.wait_ge(stat_ps, n + 1)
                act.activation(std, bank(7)[:, 0:4], ACT.Sqrt, bias=eps, scale=1.0 / D).then_inc(std_done, 1)

            def norm_high(n):
                norm_std(n)
                high_parts(n + 1)

            def high_parts(n):
                for k in range(KT):
                    act.wait_ge(ht, KT * n + k + 1)
                    act.activation(h_hi[:, k, :], tb[k % 2][:, :], ACT.Copy).then_inc(hhi, 1)

            act.wait_ge(cst_in, 16)
            act.activation(cstr[:, :], cst[:, 0:512], ACT.Copy).then_inc(cstr_done, 1)
            for n in range(TT):
                act.wait_ge(x_in[n], 16)
                if n:
                    act.wait_ge(ss_x, n)
                act.activation(junk[:, :], xn[:, n, :], ACT.Square, accum_out=sumsq[:, n:n + 1]).then_inc(ss_x, 1)
            act.wait_ge(ss_x, TT)
            act.activation(std0[:, 0:4], sumsq[:, 0:4], ACT.Sqrt, bias=eps, scale=1.0 / D).then_inc(std_x, 1)
            for k in range(1, KT, 2):
                act.wait_ge(xT_ps, KT * (TT - 1) + k + 1)
                act.activation(xT[:, k, :], bank(k), ACT.Copy).then_inc(xT_act, 1)
            split_w(0, 0, 2048)
            high_parts(0)

            b, n, _, _ = tab["qk"]
            for i in range(n):
                s = (b + i) % 2
                next_split("qk", i, s, i == n - 1)
                act.wait_ge(pe_done, b + i + 1)
                for m in range(2):
                    act.activation(qk_hi[:, 2 * i + m, :], bank(2 * s + m), ACT.Copy,
                                   scale=SB_DIM ** -0.5 if i < 2 else 1.0).then_inc(split_hi, 1)
            b, n, _, _ = tab["v"]
            for i in range(n):
                next_split("v", i, (b + i) % 2, i == n - 1)
            b, n, _, _ = tab["conv_in"]
            for i in range(n):
                s = (b + i) % 2
                next_split("conv_in", i, s, i == n - 1)
                act.wait_ge(pe_done, b + i + 1)
                act.activation(usb[:, i % 2, :], bank(2 * s), ACT.Copy).then_inc(usb_done, 1)
            b, n, _, _ = tab["conv_gate"]
            for i in range(n):
                next_split("conv_gate", i, (b + i) % 2, i == n - 1)
                for m in range(2):
                    act.wait_ge(ybf_done, 2 * i + m + 1)
                    act.activation(yb_hi[:, 2 * i + m, :], ybf[:, m, :], ACT.Copy).then_inc(yb_hi_done, 1)
            for n in range(TT):
                act.wait_ge(vt_ps, n + 1)
                act.activation(v_hi[:, n, :], bank(n), ACT.Copy).then_inc(vt_hi, 1)

            def sb_first(a, half, last):
                g = 2 * a + half + 1
                z = ps[:, 3 * half:3 * half + 3, :].rearrange("p b n -> p (b n)")[:, 0:1280]
                act.wait_ge(z_ps, g)
                act.activation(sbT[half][:, :], z, ACT.Abs).then_inc(z_abs, 1)
                act.wait_ge(z_abs, g)
                act.activation(sbT[half][:, :], sbT[half][:, :], ACT.Exp, scale=-1.0).then_inc(z_exp, 1)
                act.wait_ge(z_exp, g)
                act.activation(sbT[half][:, :], sbT[half][:, :], ACT.Ln, bias=1.0).then_inc(z_ln, 1)
                act.wait_ge(tri_ps, g)
                act.activation(sbT[half][:, :], z, ACT.Exp).then_inc(wt_done, 1)

            def sb_out(a, half, last):
                act.wait_ge(pv_ps, 2 * a + half + 1)
                rows = slice(64 * half, 64 * half + 64)
                act.activation(qk_hi[rows, at(a), :], ps[rows, 6 + half:7 + half, :], ACT.Copy).then_inc(o_hi_done, 1)

            def sb(a, half, last):
                sb_first(a, half, last)
                sb_out(a, half, last)
            act.preload_act_table_set("natural_log_exp_and_others")
            pairs(act, SB_HEADS // 2, sb)

            act.wait_ge(pv_ps, SB_HEADS)
            for n in range(4):
                rows = t["mem" if n < 2 else "ctx_2"].rearrange("b (n p) d -> (b n) p d", p=P)
                act.dma_start(mn[:, n, :], rows[n % 2]).then_inc(mc_in[n], 16)
            for n in range(4):
                act.wait_ge(mc_in[n], 16)
                if n:
                    act.wait_ge(mc_ss, n)
                act.activation(sbS[0][:, 0:D], mn[:, n, :], ACT.Square,
                               accum_out=sumsq[:, 4 + n:5 + n]).then_inc(mc_ss, 1)
            act.wait_ge(mc_ss, 4)
            act.activation(std0[:, 4:8], sumsq[:, 4:8], ACT.Sqrt, bias=eps, scale=1.0 / D).then_inc(mc_std, 1)
            for k in range(KT):
                act.wait_ge(mc_T, k + 1)
                act.activation(hm_hi[:, k, :], bank(k % 4, MEM), ACT.Copy, scale=vcol(V_MKV + k)).then_inc(mc_hi, 1)

            b, n, _, _ = tab["gates"]

            def gates(i, s, last):
                next_split("gates", i, s, last)
                act.wait_ge(evac, b + i + 1)
                act.activation(sig[:, :, at(i), :], sig[:, :, at(i), :], ACT.Sigmoid).then_inc(sig_done, 1)
            over(act, n, b, gates)

            b, n, _, _ = tab["branch"]
            for i in range(n):
                next_split("branch", i, (b + i) % 2, i == n - 1)
                for m in range(2):
                    act.wait_ge(mg_done, 2 * i + m + 1)
                    act.activation(h_hi[:, 2 * i + m, :], mg[:, m, :], ACT.Copy).then_inc(mg_hi, 1)

            def squares(name, per):
                act.preload_act_table(ACT.Sqrt)
                b, n, _, _ = tab[name]

                def body(i, s, last):
                    next_split(name, i, s, last)
                    act.wait_ge(evac, b + i + 1)
                    for m in range(per):
                        act.activation(sq[:, at(m if per == 2 else s, 1), :], xT[:, at(i * per + m), :],
                                       ACT.Square).then_inc(x_sq, 1)
                over(act, n, b, body)

            squares("mix", 2)
            b, n, _, _ = tab["mem_kv"]
            for i in range(n):
                s = (b + i) % 2
                if i == 1:
                    norm_std(0)
                if i == 4:
                    high_parts(1)
                next_split("mem_kv", i, s, i == n - 1)
                if i < 4:
                    act.wait_ge(pe_done, b + i + 1)
                    for m in range(2):
                        act.activation(km_hi[:, 2 * i + m, :], bank(2 * s + m, MEM), ACT.Copy).then_inc(split_hi, 1)
            for n in range(4):
                act.wait_ge(vt_ps, TT + n + 1)
                act.activation(vm_hi[:, n // 2, 512 * (n % 2):512 * (n % 2) + 512], bank(n), ACT.Copy).then_inc(vt_hi, 1)
            b, n, _, _ = tab["mem_q"]
            for i in range(n):
                s = (b + i) % 2
                next_split("mem_q", i, s, i == n - 1)
                act.wait_ge(pe_done, b + i + 1)
                for m in range(2):
                    act.activation(qm_hi[:, 2 * i + m, :], bank(2 * s + m), ACT.Copy,
                                   scale=MEM_DIM ** -0.5).then_inc(split_hi, 1)
            act.activation(silu_c, vecA[:, V_C:V_C + 16], ACT.Silu).then_inc(silu_c_done, 1)
            act.preload_act_table(ACT.Exp)

            def mem_out(g):
                for m in range(2):
                    act.wait_ge(mo_ps, 2 * g + m + 1)
                    act.activation(h_hi[:, 2 * g + m, :], bank(6 + m), ACT.Copy).then_inc(mo_hi, 1)
            for g in range(MEM_HEADS):
                act.wait_ge(ms_max, g + 1)
                for n in range(TT):
                    act.activation(em[:, g % 2, n, :], ps[:, 2 * (g % 2) + n // 2, 256 * (n % 2):256 * (n % 2) + 256],
                                   ACT.Exp, bias=nmax[:, 4 * (g % 2) + n:4 * (g % 2) + n + 1],
                                   accum_out=den[:, 4 * (g % 2) + n:4 * (g % 2) + n + 1]).then_inc(ms_exp, 1)
                if g:
                    mem_out(g - 1)
                act.wait_ge(mp_ps, g + 1)
                act.activation(pt_hi[:, :, :], ps[:, 4:6, :], ACT.Copy).then_inc(mp_hi, 1)
            mem_out(MEM_HEADS - 1)
            squares("mem_o", 2)
            norm_high(1)

            def up(name, count):
                b, n, _, _ = tab[name]

                def body(i, s, last):
                    next_split(name, i, s, last)
                    act.wait_ge(pe_done, b + i + 1)
                    act.activation(sg[:, at(s), :], ps[:, 2 * s:2 * s + 1, :], ACT.Silu).then_inc(silu_done, 1)
                    act.wait_ge(af_done, count + i + 1)
                    act.activation(a_hi[:, at(i), :], af[:, at(s), :], ACT.Copy).then_inc(a_hi_done, 1)
                over(act, n, b, body)
            up("up0", 0)
            b, n, _, _ = tab["down0"]
            over(act, n, b, lambda i, s, last: next_split("down0", i, s, last))
            up("up1", FH)
            squares("down1", 1)
            norm_std(2)
            for k in range(KT):
                act.wait_ge(xfin, k + 1)
                if k >= 2:
                    act.wait_ge(x_acc, (KT + 1) * 3 + k)
                act.activation(sq[:, k % 2, :], xT[:, k, :], ACT.Square).then_inc(x_sq, 1)

            def high_parts_shifted(n, shift, tb):
                for k in range(KT):
                    act.wait_ge(ht, KT * n + k + 1)
                    act.activation(h_hi[:, k, :], tb[k % 2][:, :], ACT.Identity,
                                   bias=modv[:, shift + k:shift + k + 1]).then_inc(hhi, 1)
            act.wait_ge(hc_t, KT)
            act.activation(hc_hi[:, :, :], ctxT[:, :, :], ACT.Copy).then_inc(hc_h, 1)
            norm_std(3)
            high_parts_shifted(3, 0, tb3)

            def head_squares(src, j, src_c=None):
                act.activation(hsq[:, :, :], src[:, 2 * j:2 * j + 2, :], ACT.Square).then_inc(hn_sq, 1)
                if src_c is not None:
                    act.activation(hsqc[:, :, :], src_c[:, 2 * j:2 * j + 2, :], ACT.Square).then_inc(hn_sq, 1)

            def head_norm(j, hi, tmp, hi_c, n_unit, n_round):
                act.wait_ge(hn_ps, n_unit + 1)
                act.activation(hn_std[:, 0:24 if hi_c is not None else 16], hstat(hi_c is not None),
                               ACT.Sqrt, bias=eps, scale=1.0 / NA_DIM).then_inc(hn_sd, 1)
                for m in range(3 if hi_c is not None else 2):
                    act.wait_ge(hn_t, n_round + m + 1)
                    if m < 2:
                        dst, src = hi[:, 2 * j + m, :], tmp[:, m if hi_c is not None else 0, :]
                        if hi_c is None:
                            dst, src = strips(dst), strips_of_rows(src)
                        act.activation(dst, src, ACT.Copy).then_inc(hn_hi, 1)
                    else:
                        act.activation(hi_c[:, 2 * j:2 * j + 2, :], tmp[:, m, :].rearrange("p (a n) -> p a n", a=2),
                                       ACT.Copy).then_inc(hn_hi, 1)
            b, n, _, _ = tab["na_qkv"]
            for i in range(n):
                s = (b + i) % 2
                next_split("na_qkv", i, s, i == n - 1)
                for job in head_jobs(i):
                    head_squares(job["raw"], job["j"], job["raw_c"])
                    head_norm(job["j"], job["hi"], job["tmp"], job["hi_c"], job["unit"], job["round"])
                if i < 8:
                    act.wait_ge(evac, b + i + 1)

            def na_exp(g, tau):
                act.wait_ge(ns_max, g + 1)
                act.activation(sc[:, tau, 0:256], sc[:, tau, 0:256], ACT.Exp, bias=na_nmax[:, tau:tau + 1],
                               accum_out=na_den[:, 2 * tau:2 * tau + 1])
                act.activation(sc[:, tau, 256:512], ps[:, tau, 256:512], ACT.Exp, bias=na_nmax[:, tau:tau + 1],
                               accum_out=na_den[:, 2 * tau + 1:2 * tau + 2]).then_inc(ns_exp, 1)

            def na_v(buf, r, count):
                act.wait_ge(nv_ps, count)
                cols = 512 if r < 2 else 256
                act.activation(vt_h[buf][:, 4 * r:4 * r + cols // P, :].rearrange("p c n -> p (c n)"), bank(7, cols),
                               ACT.Copy).then_inc(nv_hi, 1)

            def na_out(a, half, count):
                act.wait_ge(no_ps, count)
                rows = slice(64 * half, 64 * half + 64)
                act.activation(q_hi[rows, at(a), :].rearrange("p o (r t c) -> p (o t) r c", t=4, c=16),
                               bank(6)[0:64, :].rearrange("p (t r c) -> p t r c", t=4, r=8), ACT.Copy).then_inc(no_hi, 1)

            def na_pair(a, buf, first=False, last=False):
                for st in range(8):
                    g = 8 * a + st
                    if not (last and st + 2 >= 8):
                        na_exp(g + 2, (st + 2) % 4)
                    act.wait_ge(np_ps, g + 1)
                    act.activation(np_hi[:, st % 2, :], bank(4 + st % 2), ACT.Copy).then_inc(np_h, 1)
                    if st % 4 == 0 and not (first and st == 0):
                        na_out(a if st else a - 1, 0 if st else 1, 2 * a + (1 if st else 0))
                    if st in (1, 3, 5) and not last:
                        na_v(1 - buf, st // 2, 3 * (a + 1) + st // 2 + 1)
            act.preload_act_table(ACT.Exp)
            na_exp(0, 0)
            na_exp(1, 1)
            for r in range(3):
                na_v(0, r, r + 1)
            na_pair(0, 0, first=True)
            with act.Fori(1, 7, 2) as a:
                na_pair(a, 1)
                na_pair(a + 1, 0)
            na_pair(7, 1, last=True)
            na_out(7, 1, NA_HEADS)

            squares("na_o", 2)
            norm_std(4)
            high_parts_shifted(4, 24, tb)

            def up_conv(name, count):
                b, n, _, _ = tab[name]

                def body(i, s, last):
                    next_split(name, i, s, last)
                    act.wait_ge(pe_done, b + i + 1)
                    act.activation(gs[:, at(s), 1:1 + SEQ], ps[:, 2 * s + 1:2 * s + 2, :], ACT.Copy).then_inc(gs_done, 1)
                    act.wait_ge(gc_step, 3 * i + (3 * count + 3))
                    act.activation(gl[:, at(s), :], gc[:, at(s), :], ACT.Gelu, bias=vecA[:, at(i + (V_CB + count))]).then_inc(gl_done, 1)
                    act.wait_ge(gf_done, i + (count + 1))
                    act.activation(a_hi[:, at(i), :], gf[:, at(s), :], ACT.Copy).then_inc(ga_hi, 1)
                over(act, n, b, body)
            up_conv("nup0", 0)
            b, n, _, _ = tab["ndown0"]
            over(act, n, b, lambda i, s, last: next_split("ndown0", i, s, last))
            up_conv("nup1", FH)
            b, n, _, _ = tab["ndown1"]
            over(act, n, b, lambda i, s, last: next_split("ndown1", i, s, last))

        @block.vector
        def _(dve):
            v = nc.vector

            def split_w(u, s, size):
                dve.wait_ge(w_hi, u + 1)
                v.tensor_tensor(wlo[s][:, 0:size], raw[s][:, 0:size], whi[s][:, 0:size].bitcast(F32),
                                ALU.subtract).then_inc(w_lo, 1)

            def next_split(name, i, s, last):
                b, _, size, after = tab[name]
                if not last or after:
                    split_w(b + i + 1, 1 - s, after if last else size)

            def low(out, full, high):
                return v.tensor_tensor(out, full, high.bitcast(F32), ALU.subtract)

            def norm_apply(n, gain):
                def lo(k):
                    dve.wait_ge(hhi, KT * n + k + 1)
                    low(h_lo[:, k, :], tb[k % 2][:, :], h_hi[:, k, :]).then_inc(hlo, 1)
                for k in range(KT):
                    if k >= 2:
                        dve.wait_ge(hlo, KT * n + k - 1)
                    v.scalar_tensor_tensor(tb[k % 2][:, :], xT[:, k, :], vcol(gain + k), bank(6),
                                           ALU.mult, ALU.mult).then_inc(ht, 1)
                    if k:
                        lo(k - 1)
                lo(KT - 1)

            def norm_rstd(n):
                dve.wait_ge(std_done, n + 1)
                v.reciprocal(rstd, std).then_inc(rstd_done, 1)

            def norm_spread(n):
                dve.wait_ge(r_ps, n + 2)

            dve.wait_ge(vec_T, 1)
            v.tensor_copy(vecA[:, 0:NA_ROWS], bank(0)[:, 0:NA_ROWS]).then_inc(vec_sb, 1)
            dve.wait_ge(vec_T, 2)
            v.tensor_copy(vecB[:, 0:NB_ROWS], bank(1)[:, 0:NB_ROWS]).then_inc(vec_sb, 1)
            dve.wait_ge(std_x, 1)
            v.reciprocal(rstd0[:, 0:4], std0[:, 0:4]).then_inc(rstd_x, 1)
            for k in range(0, KT, 2):
                dve.wait_ge(xT_ps, KT * (TT - 1) + k + 1)
                v.tensor_copy(xT[:, k, :], bank(k)).then_inc(xT_dve, 1)
            dve.wait_ge(vec_sb, 2)
            dve.wait_ge(xT_dve, 4)
            dve.wait_ge(xT_act, 4)
            v.memset(cu[:, :, 0:2], 0.0).then_inc(cu_zero, 1)
            dve.wait_ge(r_ps, 1)
            split_w(0, 0, 2048)
            norm_apply(0, V_MIX)

            b, n, _, _ = tab["qk"]
            for i in range(n):
                s = (b + i) % 2
                next_split("qk", i, s, i == n - 1)
                for m in range(2):
                    j = 2 * i + m
                    dve.wait_ge(split_hi, j + 1)
                    last = v.scalar_tensor_tensor(qk_lo[:, j, :], bank(2 * s + m), SB_DIM ** -0.5 if i < 2 else 1.0,
                                                  qk_hi[:, j, :].bitcast(F32), ALU.mult, ALU.subtract)
                last.then_inc(evac, 1)
            b, n, _, _ = tab["v"]
            for i in range(n):
                s = (b + i) % 2
                next_split("v", i, s, i == n - 1)
                dve.wait_ge(pe_done, b + i + 1)
                v.tensor_copy(vraw[:, 2 * i:2 * i + 2, :], ps[:, 2 * s:2 * s + 2, :]).then_inc(evac, 1)

            b, n, _, _ = tab["conv_in"]
            dve.wait_ge(cu_zero, 1)
            for i in range(n):
                s = (b + i) % 2
                next_split("conv_in", i, s, i == n - 1)
                c = cu[:, i % 2, :]
                dve.wait_ge(usb_done, i + 1)
                if i >= 2:
                    dve.wait_ge(conv_step, 3 * (i - 1))
                v.tensor_tensor(c[:, 2:2 + SEQ], bank(2 * s + 1), usb[:, i % 2, :], ALU.mult).then_inc(evac, 1)
                dve.wait_ge(evac, b + i + 1)
                v.tensor_scalar(cv[:, i, :], c[:, 2:2 + SEQ], vcol(V_CONV + 8 + i), None, ALU.mult).then_inc(conv_step, 1)
                for tap in (1, 0):
                    dve.wait_ge(conv_step, 3 * i + 2 - tap)
                    v.scalar_tensor_tensor(cv[:, i, :], c[:, tap:tap + SEQ], vcol(V_CONV + 4 * tap + i), cv[:, i, :],
                                           ALU.mult, ALU.add).then_inc(conv_step, 1)
            dve.wait_ge(conv_step, 12)
            b, n, _, _ = tab["conv_gate"]
            for i in range(n):
                s = (b + i) % 2
                next_split("conv_gate", i, s, i == n - 1)
                dve.wait_ge(pe_done, b + i + 1)
                if i:
                    dve.wait_ge(evac, b + i)
                for m in range(2):
                    last = v.tensor_tensor(ybf[:, m, :], bank(2 * s + m), cv[:, 2 * i + m, :], ALU.mult)
                    last.then_inc(ybf_done, 1)
                for m in range(2):
                    dve.wait_ge(yb_hi_done, 2 * i + m + 1)
                    last = low(yb_lo[:, 2 * i + m, :], ybf[:, m, :], yb_hi[:, 2 * i + m, :])
                last.then_inc(evac, 1)
            for n in range(TT):
                dve.wait_ge(vt_hi, n + 1)
                low(v_lo[:, n, :], bank(n), v_hi[:, n, :]).then_inc(vt_lo, 1)

            def sb(a, half, last):
                g = 2 * a + half + 1
                z = ps[:, 3 * half:3 * half + 3, :].rearrange("p b n -> p (b n)")[:, 0:1280]
                dve.wait_ge(z_ln, g)
                v.scalar_tensor_tensor(sbS[half][:, :], z, 0.0, sbT[half][:, :], ALU.max, ALU.add).then_inc(sp_done, 1)
                dve.wait_ge(sp_done, g)
                v.tensor_copy(sb_hi[half][:, :], sbS[half][:, :]).then_inc(sp_hi, 1)
                dve.wait_ge(sp_hi, g)
                low(sb_lo[half][:, :], sbS[half][:, :], sb_hi[half][:, :]).then_inc(sp_lo, 1)
                dve.wait_ge(wt_done, g)
                v.tensor_copy(sb_hi[half][:, :], sbT[half][:, :]).then_inc(wt_hi, 1)
                dve.wait_ge(wt_hi, g)
                low(sb_lo[half][:, :], sbT[half][:, :], sb_hi[half][:, :]).then_inc(wt_lo, 1)
                dve.wait_ge(o_hi_done, g)
                rows = slice(64 * half, 64 * half + 64)
                low(qk_lo[rows, at(a), :], ps[rows, 6 + half:7 + half, :], qk_hi[rows, at(a), :]).then_inc(o_lo_done, 1)
            pairs(dve, SB_HEADS // 2, sb)

            dve.wait_ge(mc_std, 1)
            v.reciprocal(rstd0[:, 4:8], std0[:, 4:8]).then_inc(mc_rstd, 1)
            dve.wait_ge(mc_rstd, 1)
            for n in range(4):
                v.tensor_scalar(mn[:, n, :], mn[:, n, :], rstd0[:, 4 + n:5 + n], None, ALU.mult).then_inc(mc_scaled, 1)
            for k in range(KT):
                dve.wait_ge(mc_hi, k + 1)
                v.scalar_tensor_tensor(hm_lo[:, k, :], bank(k % 4, MEM), vcol(V_MKV + k), hm_hi[:, k, :].bitcast(F32),
                                       ALU.mult, ALU.subtract)
                v.tensor_copy(ctxT[:, k, :], ps[:, k % 4, 256:512]).then_inc(mc_lo, 1)

            b, n, _, _ = tab["gates"]

            def gates(i, s, last):
                next_split("gates", i, s, last)
                dve.wait_ge(pe_done, b + i + 1)
                v.tensor_copy(sig[:, :, at(i), :], ps[:, 2 * s:2 * s + 2, :].rearrange("p b (o n) -> p b o n", o=1)).then_inc(evac, 1)
            over(dve, n, b, gates)

            b, n, _, _ = tab["branch"]
            dve.wait_ge(sig_done, KT)
            for i in range(n):
                s = (b + i) % 2
                next_split("branch", i, s, i == n - 1)
                dve.wait_ge(pe_done, b + i + 1)
                if i:
                    dve.wait_ge(evac, b + i)
                for m in range(2):
                    j = 2 * i + m
                    v.tensor_tensor(mg[:, m, :], bank(2 * s + m), sig[:, 0, j, :], ALU.mult)
                    last = v.tensor_tensor(mt[:, m, :], bank(4 + 2 * s + m), sig[:, 1, j, :], ALU.mult)
                    last.then_inc(br_step, 1)
                for m in range(2):
                    j = 2 * i + m
                    dve.wait_ge(br_step, j + 1)
                    v.tensor_tensor(mg[:, m, :], mg[:, m, :], mt[:, m, :], ALU.add).then_inc(mg_done, 1)
                for m in range(2):
                    j = 2 * i + m
                    dve.wait_ge(mg_hi, j + 1)
                    last = low(h_lo[:, j, :], mg[:, m, :], h_hi[:, j, :])
                last.then_inc(evac, 1)

            def update(name, per, norm=None, gate=None):
                b, n, _, _ = tab[name]

                def body(i, s, last):
                    next_split(name, i, s, last)
                    dve.wait_ge(pe_done, b + i + 1)
                    for m in range(per):
                        x = xT[:, at(i * per + m), :]
                        y = ps[:, 2 * s + m:2 * s + m + 1, :]
                        if gate is None:
                            r = v.tensor_tensor(x, x, y, ALU.add)
                        else:
                            r = v.scalar_tensor_tensor(x, y, modv[:, at(i * per + (gate + m))], x, ALU.mult, ALU.add)
                    r.then_inc(evac, 1)
                    for m in range(0 if norm is None else per):
                        dve.wait_ge(x_sq, i * per + (KT * norm + m + 1))
                        dve.wait_ge(x_acc, i * per + ((KT + 1) * norm + m + 1))
                        v.tensor_tensor(sqacc[:, :], sqacc[:, :], sq[:, m if per == 2 else s, :], ALU.add).then_inc(x_acc, 1)
                if norm is not None:
                    v.memset(sqacc[:, :], 0.0).then_inc(x_acc, 1)
                over(dve, n, b, body)
            update("mix", 2, 0)

            b, n, _, _ = tab["mem_kv"]
            for i in range(n):
                s = (b + i) % 2
                if i == 2:
                    norm_rstd(0)
                if i == 4:
                    norm_spread(0)
                    norm_apply(1, V_MQ)
                next_split("mem_kv", i, s, i == n - 1)
                if i < 4:
                    for m in range(2):
                        j = 2 * i + m
                        dve.wait_ge(split_hi, 8 + j + 1)
                        last = low(km_lo[:, j, :], bank(2 * s + m, MEM), km_hi[:, j, :])
                    last.then_inc(evac, 1)
                else:
                    dve.wait_ge(pe_done, b + i + 1)
                    v.tensor_copy(vmraw[:, 2 * i - 8:2 * i - 6, :], ps[:, 2 * s:2 * s + 2, 0:MEM]).then_inc(evac, 1)
            for n in range(4):
                dve.wait_ge(vt_hi, TT + n + 1)
                low(vm_lo[:, n // 2, 512 * (n % 2):512 * (n % 2) + 512], bank(n),
                    vm_hi[:, n // 2, 512 * (n % 2):512 * (n % 2) + 512]).then_inc(vt_lo, 1)
            b, n, _, _ = tab["mem_q"]
            for i in range(n):
                s = (b + i) % 2
                next_split("mem_q", i, s, i == n - 1)
                for m in range(2):
                    j = 2 * i + m
                    dve.wait_ge(split_hi, 16 + j + 1)
                    last = v.scalar_tensor_tensor(qm_lo[:, j, :], bank(2 * s + m), MEM_DIM ** -0.5,
                                                  qm_hi[:, j, :].bitcast(F32), ALU.mult, ALU.subtract)
                last.then_inc(evac, 1)
            def mem_max(g):
                dve.wait_ge(ms_ps, g + 1)
                if g >= 2:
                    dve.wait_ge(ms_exp, TT * (g - 1))
                v.tensor_reduce(nmax[:, 4 * (g % 2):4 * (g % 2) + 4],
                                ps[:, 2 * (g % 2):2 * (g % 2) + 2, :].rearrange("p b (o n) -> p (b o) n", o=2),
                                AX.X, ALU.max, negate=True).then_inc(ms_max, 1)

            def mem_out(g):
                for m in range(2):
                    dve.wait_ge(mo_hi, 2 * g + m + 1)
                    low(h_lo[:, 2 * g + m, :], bank(6 + m), h_hi[:, 2 * g + m, :]).then_inc(mo_lo, 1)
            mem_max(0)
            for g in range(MEM_HEADS):
                dve.wait_ge(ms_exp, TT * (g + 1))
                cols = slice(4 * (g % 2), 4 * (g % 2) + 4)
                v.reciprocal(rden[:, cols], den[:, cols]).then_inc(ms_rden, 1)
                dve.wait_ge(ms_rden, g + 1)
                for n in range(TT):
                    v.tensor_scalar(em[:, g % 2, n, :], em[:, g % 2, n, :],
                                    rden[:, 4 * (g % 2) + n:4 * (g % 2) + n + 1], None, ALU.mult).then_inc(ms_norm, 1)
                if g + 1 < MEM_HEADS:
                    mem_max(g + 1)
                if g:
                    mem_out(g - 1)
                dve.wait_ge(mp_hi, g + 1)
                low(pt_lo[:, :, :], ps[:, 4:6, :], pt_hi[:, :, :]).then_inc(mp_lo, 1)
            mem_out(MEM_HEADS - 1)
            update("mem_o", 2, 1)
            norm_rstd(1)
            norm_spread(1)
            norm_apply(2, V_FFN)

            def up(name, count):
                b, n, _, _ = tab[name]

                def body(i, s, last):
                    next_split(name, i, s, last)
                    dve.wait_ge(silu_done, count + i + 1)
                    v.tensor_tensor(af[:, at(s), :], ps[:, 2 * s + 1:2 * s + 2, :], sg[:, at(s), :], ALU.mult).then_inc(af_done, 1)
                    dve.wait_ge(a_hi_done, count + i + 1)
                    low(a_lo[:, at(i), :], af[:, at(s), :], a_hi[:, at(i), :]).then_inc(evac, 1)
                over(dve, n, b, body)
            up("up0", 0)
            update("down0", 1)
            up("up1", FH)
            update("down1", 1, 2)
            norm_rstd(2)
            v.memset(sqacc[:, :], 0.0).then_inc(x_acc, 1)
            norm_spread(2)

            def take_squares(k):
                dve.wait_ge(x_sq, KT * 3 + k + 1)
                dve.wait_ge(x_acc, (KT + 1) * 3 + k + 1)
                v.tensor_tensor(sqacc[:, :], sqacc[:, :], sq[:, k % 2, :], ALU.add).then_inc(x_acc, 1)
            for k in range(KT):
                v.scalar_tensor_tensor(xT[:, k, :], xT[:, k, :], vcol(V_FIN + k), bank(6), ALU.mult, ALU.mult).then_inc(xfin, 1)
                if k:
                    take_squares(k - 1)
            take_squares(KT - 1)
            dve.wait_ge(mod_ps, 4)
            v.tensor_tensor(modv[:, 0:48], bank(5)[:, 0:48], vecB[:, V_BMOD:V_BMOD + 48], ALU.add).then_inc(mod_sb, 1)
            v.tensor_tensor(modv[:, 48:64], bank(5)[:, 48:64], vecB[:, V_BMOD:V_BMOD + 16], ALU.add).then_inc(mod_sb, 1)
            v.tensor_scalar(qgain, vcol(V_QG), NA_DIM ** -0.5, None, ALU.mult).then_inc(mod_sb, 1)
            dve.wait_ge(mod_sb, 3)
            for o, scale, gain in ((gain1, 8, V_N1), (gain2, 32, V_N2), (gain1c, 56, V_N1)):
                v.scalar_tensor_tensor(o, modv[:, scale:scale + 8], 1.0, vecA[:, gain:gain + 8], ALU.add, ALU.mult).then_inc(mod_vec, 1)
            dve.wait_ge(mod_vec, 3)
            for k in range(KT):
                v.tensor_scalar(ctxT[:, k, :], ctxT[:, k, :], gain1c[:, k:k + 1], modv[:, 48 + k:49 + k],
                                ALU.mult, ALU.add).then_inc(hc_t, 1)
            norm_rstd(3)
            dve.wait_ge(hc_h, 1)
            low(hc_lo[:, :, :], ctxT[:, :, :], hc_hi[:, :, :]).then_inc(hc_l, 1)
            norm_spread(3)

            def norm_apply_shifted(n, gain, shift, tb):
                def lo(k):
                    dve.wait_ge(hhi, KT * n + k + 1)
                    v.scalar_tensor_tensor(h_lo[:, k, :], tb[k % 2][:, :], modv[:, shift + k:shift + k + 1],
                                           h_hi[:, k, :].bitcast(F32), ALU.add, ALU.subtract).then_inc(hlo, 1)
                for k in range(KT):
                    if k >= 2:
                        dve.wait_ge(hlo, KT * n + k - 1)
                    v.scalar_tensor_tensor(tb[k % 2][:, :], xT[:, k, :], gain[:, k:k + 1], bank(6),
                                           ALU.mult, ALU.mult).then_inc(ht, 1)
                    if k:
                        lo(k - 1)
                lo(KT - 1)
            norm_apply_shifted(3, gain1, 0, tb3)

            def head_norm(job):
                cols = 24 if job["hi_c"] is not None else 16
                dve.wait_ge(hn_sd, job["unit"] + 1)
                v.reciprocal(hn_rstd[:, 0:cols], hn_std[:, 0:cols]).then_inc(hn_rd, 1)
                gain = qgain if job["hi_c"] is None else vcol(V_KG)
                j = job["j"]
                dve.wait_ge(hn_rd, job["unit"] + 1)
                for m in range(3 if job["hi_c"] is not None else 2):
                    v.tensor_copy(rexp[:, :, :], hn_rstd[:, 8 * m:8 * m + 8].rearrange("p (h o) -> p h o", o=1)
                                  .to_broadcast([P, 8, 64])).then_inc(hn_x, 1)
                    dve.wait_ge(hn_r, job["round"] + m + 1)
                    if job["round"] + m:
                        dve.wait_ge(hn_lo, job["round"] + m)
                    slot = m if job["hi_c"] is not None else 0
                    if m < 2:
                        v.scalar_tensor_tensor(job["tmp"][:, slot, :], job["raw"][:, 2 * j + m, :], gain, bank(7),
                                               ALU.mult, ALU.mult).then_inc(hn_t, 1)
                        dve.wait_ge(hn_hi, job["round"] + m + 1)
                        dst, src, high = job["lo"][:, 2 * j + m, :], job["tmp"][:, slot, :], job["hi"][:, 2 * j + m, :]
                        if job["hi_c"] is None:
                            dst, src, high = strips(dst), strips_of_rows(src), strips(high)
                        low(dst, src, high).then_inc(hn_lo, 1)
                    else:
                        tmp = job["tmp"][:, m, :].rearrange("p (a n) -> p a n", a=2)
                        v.scalar_tensor_tensor(tmp, job["raw_c"][:, 2 * j:2 * j + 2, :], gain,
                                               bank(7).rearrange("p (a n) -> p a n", a=2), ALU.mult, ALU.mult).then_inc(hn_t, 1)
                        dve.wait_ge(hn_hi, job["round"] + m + 1)
                        low(job["lo_c"][:, 2 * j:2 * j + 2, :], tmp, job["hi_c"][:, 2 * j:2 * j + 2, :]).then_inc(hn_lo, 1)
            b, n, _, _ = tab["na_qkv"]
            for i in range(n):
                s = (b + i) % 2
                next_split("na_qkv", i, s, i == n - 1)
                for job in head_jobs(i):
                    head_norm(job)
                dve.wait_ge(pe_done, b + i + 1)
                x_banks = ps[:, 2 * s:2 * s + 2, :]
                c_bank = bank(4 + s).rearrange("p (a n) -> p a n", a=2)
                j = 2 * (i % 4)
                if i >= 8:
                    if i == 8:
                        dve.wait_ge(hn_lo, 20)
                    else:
                        dve.wait_ge(v_spill, 16 * (i - 8))
                    v.tensor_copy(v_out[:, :, 0:SEQ], x_banks)
                    v.tensor_copy(v_out[:, :, SEQ:SEQ + CTX], c_bank).then_inc(evac, 1)
                elif i < 4:
                    v.tensor_copy(k_raw[:, j:j + 2, :], x_banks)
                    v.tensor_copy(kc_raw[:, j:j + 2, :], c_bank).then_inc(evac, 1)
                else:
                    v.tensor_copy(q_raw[:, j:j + 2, :], x_banks).then_inc(evac, 1)

            def na_den_step(g, tau):
                dve.wait_ge(ns_exp, g + 1)
                v.tensor_tensor(na_dsum[:, tau:tau + 1], na_den[:, 2 * tau:2 * tau + 1], na_den[:, 2 * tau + 1:2 * tau + 2],
                                ALU.add).then_inc(ns_dsum, 1)
                dve.wait_ge(ns_dsum, g + 1)
                v.reciprocal(na_rden[:, tau:tau + 1], na_dsum[:, tau:tau + 1]).then_inc(ns_rden, 1)

            def na_v(buf, r, count):
                dve.wait_ge(nv_hi, count)
                cols = 512 if r < 2 else 256
                low(vt_l[buf][:, 4 * r:4 * r + cols // P, :].rearrange("p c n -> p (c n)"), bank(7, cols),
                    vt_h[buf][:, 4 * r:4 * r + cols // P, :].rearrange("p c n -> p (c n)")).then_inc(nv_lo, 1)

            def na_out(a, half, count):
                dve.wait_ge(no_hi, count)
                rows = slice(64 * half, 64 * half + 64)
                v.tensor_tensor(q_lo[rows, at(a), :].rearrange("p o (r t c) -> p (o t) r c", t=4, c=16),
                                bank(6)[0:64, :].rearrange("p (t r c) -> p t r c", t=4, r=8),
                                q_hi[rows, at(a), :].bitcast(F32).rearrange("p o (r t c) -> p (o t) r c", t=4, c=16),
                                ALU.subtract).then_inc(no_lo, 1)

            def na_pair(a, buf, first=False, last=False):
                for st in range(8):
                    g = 8 * a + st
                    if not (last and st + 1 >= 8):
                        na_den_step(g + 1, (st + 1) % 4)
                    if not (last and st + 3 >= 8):
                        head = (st + 3) // 4
                        na_max_step_in(a, st + 3, head % 2)
                    dve.wait_ge(np_h, g + 1)
                    low(np_lo[:, st % 2, :], bank(4 + st % 2), np_hi[:, st % 2, :]).then_inc(np_l, 1)
                    if st % 4 == 0 and not (first and st == 0):
                        na_out(a if st else a - 1, 0 if st else 1, 2 * a + (1 if st else 0))
                    if st in (1, 3, 5) and not last:
                        na_v(1 - buf, st // 2, 3 * (a + 1) + st // 2 + 1)

            def na_max_step_in(a, st, b):
                g, tau = 8 * a + st, st % 4
                dve.wait_ge(ns_ps, g + 1)
                if not isinstance(g, int) or g >= 4:
                    dve.wait_ge(np_ps, g - 3)
                if tau == 0:
                    dve.wait_ge(bias_done, 2 * a + st // 4 + 1)
                v.tensor_reduce(na_nmax_c[:, tau:tau + 1], ps[:, tau, 256:512], AX.X, ALU.max, negate=True)
                v.tensor_tensor_reduce(out=sc[:, tau, 0:256], in0=ps[:, tau, 0:256],
                                       in1=bias[b][:, (0, 1, 1, 2)[tau], :, :].rearrange("p i j -> p (i j)"),
                                       scale=1.0, scalar=-3.0e38, op0=ALU.add, op1=ALU.max,
                                       accum_out=na_max[:, tau:tau + 1]).then_inc(ns_red, 1)
                dve.wait_ge(ns_red, g + 1)
                v.scalar_tensor_tensor(na_nmax[:, tau:tau + 1], na_max[:, tau:tau + 1], -1.0, na_nmax_c[:, tau:tau + 1],
                                       ALU.mult, ALU.min).then_inc(ns_max, 1)
            for st in range(3):
                na_max_step_in(0, st, 0)
            na_den_step(0, 0)
            dve.wait_ge(v_spill, 64)
            dve.wait_ge(vp_in[0], 16)
            for tau in range(TT):
                last = v.tensor_copy(vw[:, tau, :, :], grid(vp[0][:, 0:SEQ])[:, :, span[tau]:span[tau] + 32])
            last.then_inc(vw_done, 1)
            for r in range(3):
                na_v(0, r, r + 1)
            na_pair(0, 0, first=True)
            with dve.Fori(1, 7, 2) as a:
                na_pair(a, 1)
                na_pair(a + 1, 0)
            na_pair(7, 1, last=True)
            na_out(7, 1, NA_HEADS)

            update("na_o", 2, 4, gate=16)
            v.memset(gs[:, :, 0:1], 0.0).then_inc(gs_zero, 1)
            v.memset(gs[:, :, SEQ + 1:SEQ + 2], 0.0).then_inc(gs_zero, 1)
            norm_rstd(4)
            norm_spread(4)
            norm_apply_shifted(4, gain2, 24, tb)
            dve.wait_ge(gs_zero, 2)

            def up_conv(name, count):
                b, n, _, _ = tab[name]

                def body(i, s, last):
                    next_split(name, i, s, last)
                    g = gs[:, at(s), :]
                    c = gc[:, at(s), :]
                    dve.wait_ge(gs_done, i + (count + 1))
                    v.tensor_scalar(c, g[:, :, 0:SEQ], vecB[:, at(i + (V_CW + count))], None, ALU.mult).then_inc(gc_step, 1)
                    for tap in (1, 2):
                        dve.wait_ge(gc_step, 3 * i + (3 * count + tap))
                        v.scalar_tensor_tensor(c, g[:, :, tap:tap + SEQ], vecB[:, at(i + (V_CW + count + FT * tap))], c,
                                               ALU.mult, ALU.add).then_inc(gc_step, 1)
                    dve.wait_ge(gl_done, i + (count + 1))
                    v.tensor_tensor(gf[:, at(s), :], ps[:, 2 * s:2 * s + 1, :], gl[:, at(s), :], ALU.mult).then_inc(gf_done, 1)
                    dve.wait_ge(ga_hi, i + (count + 1))
                    low(a_lo[:, at(i), :], gf[:, at(s), :], a_hi[:, at(i), :]).then_inc(evac, 1)
                over(dve, n, b, body)
            up_conv("nup0", 0)
            update("ndown0", 1, gate=40)
            up_conv("nup1", FH)
            update("ndown1", 1, gate=40)
            for n in range(2 * TT):
                dve.wait_ge(out_T, n + 1)
                v.tensor_copy(out_rows[:, n // 2, 512 * (n % 2):512 * (n % 2) + 512], bank(n)).then_inc(out_sb, 1)

        @block.tensor
        def _(pe):
            mm = nc.tensor.matmul

            def product(o, w_h, w_l, x_h, x_l, first, last, **kw):
                mm(o, w_h, x_h, start=first, stop=False, **kw)
                mm(o, w_h, x_l, start=False, stop=False, **kw)
                return mm(o, w_l, x_h, start=False, stop=last, **kw)

            def unit(u):
                pe.wait_ge(w_lo, u + 1)
                if not isinstance(u, int) or u >= 2:
                    pe.wait_ge(evac, u - 1)

            def pair_unit(u, s, x_h, x_l, cols=SEQ, arrive=None):
                unit(u)
                for k in range(KT):
                    if arrive:
                        arrive(k)
                    for m in range(2):
                        w = slice(256 * k + 128 * m, 256 * k + 128 * m + 128)
                        last = product(bank(2 * s + m, cols), whi[s][:, w], wlo[s][:, w], x_h[:, k, :], x_l[:, k, :],
                                       k == 0, k == KT - 1)
                last.then_inc(pe_done, 1)

            def pair_layer(name, x_h, x_l, cols=SEQ, arrive=None, after_first=None):
                b, n, _, _ = tab[name]
                if arrive:
                    pair_unit(b, b % 2, x_h, x_l, cols, arrive)
                    if after_first:
                        after_first()
                    if n <= 4:
                        for i in range(1, n):
                            pair_unit(b + i, (b + i) % 2, x_h, x_l, cols)
                    else:
                        over(pe, n - 1, b + 1, lambda i, s, last: pair_unit(b + 1 + i, s, x_h, x_l, cols))
                else:
                    over(pe, n, b, lambda i, s, last: pair_unit(b + i, s, x_h, x_l, cols))

            def down_layer(name, source):
                b, n, _, _ = tab[name]

                def body(i, s, last, follow=False):
                    unit(b + i)
                    for k in range(FH):
                        if follow:
                            pe.wait_ge(evac, tab[source][0] + k + 1)
                        w = slice(128 * k, 128 * k + 128)
                        r = product(bank(2 * s), whi[s][:, w], wlo[s][:, w], a_hi[:, k, :], a_lo[:, k, :],
                                    k == 0, k == FH - 1)
                    r.then_inc(pe_done, 1)
                body(0, b % 2, False, follow=True)
                over(pe, n - 1, b + 1, lambda i, s, last: body(i + 1, s, last))

            def norm_stats(n, acc):
                pe.wait_ge(x_acc, acc)
                for q in range(TT):
                    last = mm(bank(7)[:, q:q + 1], sqacc[:, q * P:q * P + P], one, start=True, stop=True)
                last.then_inc(stat_ps, 1)

            def norm_spread(n):
                pe.wait_ge(rstd_done, n + 1)
                for q in range(TT):
                    last = nc.tensor.transpose(bank(6)[:, q * P:q * P + P], rstd[:, q:q + 1].to_broadcast([P, P]), ident)
                last.then_inc(r_ps, 1)

            def mod_group(group):
                first, cols, both = MOD_GROUPS[group]
                pe.wait_ge(mod_step, 32 * (group + 1))
                for j in range(cols // P):
                    o = first // P + j
                    last = mm(bank(5)[:, o:o + 1], mod_acc[:, j * P:j * P + P], one, start=True, stop=True)
                    if both:
                        last = mm(bank(5)[:, 48 + o:49 + o], mod_acc[:, 1024 + j * P:1024 + j * P + P], one, start=True, stop=True)
                last.then_inc(mod_ps, 1)

            pe.wait_ge(cst_in, 16)
            pe.wait_ge(vec_in, 16 * 17)
            nc.tensor.transpose(bank(0)[:, 0:NA_ROWS], rowsA[0:NA_ROWS, :], ident[0:NA_ROWS, 0:NA_ROWS]).then_inc(vec_T, 1)
            nc.tensor.transpose(bank(1)[:, 0:NB_ROWS], rowsB[0:NB_ROWS, :], ident[0:NB_ROWS, 0:NB_ROWS]).then_inc(vec_T, 1)
            pe.wait_ge(vec_sb, 2)
            for n in range(TT):
                pe.wait_ge(x_in[n], 16)
                for k in range(KT):
                    nc.tensor.transpose(bank(k)[:, n * P:n * P + P], xn[:, n, k * P:k * P + P], ident).then_inc(xT_ps, 1)
            pe.wait_ge(rstd_x, 1)
            pe.wait_ge(xT_dve, 4)
            for q in range(TT):
                last = nc.tensor.transpose(bank(6)[:, q * P:q * P + P], rstd0[:, q:q + 1].to_broadcast([P, P]), ident)
            last.then_inc(r_ps, 1)
            pe.wait_ge(xT_act, 4)

            pair_layer("qk", h_hi, h_lo, arrive=lambda k: pe.wait_ge(hlo, k + 1))
            pair_layer("v", h_hi, h_lo)
            pair_layer("conv_in", h_hi, h_lo)
            pair_layer("conv_gate", h_hi, h_lo)

            b, n, _, _ = tab["conv_gate"]
            pe.wait_ge(evac, b + n)
            for n in range(TT):
                for j in range(4):
                    last = nc.tensor.transpose(bank(n)[:, j * P:j * P + P], vraw[:, j, n * P:n * P + P], ident)
                last.then_inc(vt_ps, 1)
            pe.wait_ge(vt_lo, TT)
            pe.wait_ge(cstr_done, 1)

            zat = [0, 512, 1024, 896]
            zlen = [512, 384, 256, 128]

            def score(a, half):
                z = ps[:, 3 * half:3 * half + 3, :].rearrange("p b n -> p (b n)")
                rows = slice(64 * half, 64 * half + 64)
                for n in (0, 1, 3, 2):
                    o = z[:, zat[n]:zat[n] + zlen[n]]
                    q_h, q_l = (x[rows, at(a), n * P:SEQ] for x in (qk_hi, qk_lo))
                    k_h, k_l = (x[rows, at(a + 4), n * P:n * P + P] for x in (qk_hi, qk_lo))
                    mm(o, k_h, q_h, start=n != 3, stop=False, skip_group_check=True)
                    mm(o, k_h, q_l, start=False, stop=False, skip_group_check=True)
                    mm(o, k_l, q_h, start=False, stop=False, skip_group_check=True)
                for n in (0, 1, 3, 2):
                    last = mm(z[:, zat[n]:zat[n] + P], r_ident, r_mask, start=False, stop=False, skip_group_check=True)
                last.then_inc(z_ps, 1)

            def later(half, g):
                z = ps[:, 3 * half:3 * half + 3, :].rearrange("p b n -> p (b n)")
                pe.wait_ge(sp_lo, g)
                for n in (0, 1, 3, 2):
                    for s in (sb_hi[half], sb_lo[half]):
                        for j in range(n, TT):
                            w = r_tri if j == n else r_ones
                            last = mm(z[:, zat[n] + (j - n) * P:zat[n] + zlen[n]], w, s[:, zat[j]:zat[j] + zlen[j]],
                                      start=False, stop=j == TT - 1, skip_group_check=True)
                last.then_inc(tri_ps, 1)

            def values(a, half, g):
                pe.wait_ge(wt_lo, g)
                for n in range(TT):
                    w = [x[:, n, at(a * P, P)] for x in (v_hi, v_lo)]
                    x = [s[half][:, zat[n]:zat[n] + zlen[n]] for s in (sb_hi, sb_lo)]
                    last = product(bank(6 + half)[:, n * P:SEQ], w[0], w[1], x[0], x[1], n == 0, n == TT - 1)
                last.then_inc(pv_ps, 1)

            score(0, 0)

            def head(a, half, first=False, last=False):
                g = 2 * a + half + 1
                if not last:
                    score(a + half, 1 - half)
                later(half, g)
                if not first:
                    pe.wait_ge(o_lo_done, g - 2)
                values(a, half, g)

            head(0, 0, first=True)
            head(0, 1, first=True)
            for a in range(1, SB_HEADS // 2 - 1):
                head(a, 0)
                head(a, 1)
            head(SB_HEADS // 2 - 1, 0)
            head(SB_HEADS // 2 - 1, 1, last=True)

            pe.wait_ge(mc_scaled, 4)
            for k in range(KT):
                if k >= 4:
                    pe.wait_ge(mc_lo, k - 3)
                for n in range(4):
                    last = nc.tensor.transpose(bank(k % 4)[:, n * P:n * P + P], mn[:, n, k * P:k * P + P], ident)
                last.then_inc(mc_T, 1)
            pe.wait_ge(mc_lo, KT)
            pair_layer("gates", h_hi, h_lo)

            b, n, _, _ = tab["branch"]
            pe.wait_ge(o_lo_done, SB_HEADS)
            for i in range(n):
                s = (b + i) % 2
                unit(b + i)
                for m in range(2):
                    for br, (x_h, x_l) in enumerate(((qk_hi, qk_lo), (yb_hi, yb_lo))):
                        for k in range(4):
                            w = slice(256 * (4 * br + k) + 128 * m, 256 * (4 * br + k) + 128 * m + 128)
                            last = product(bank(4 * br + 2 * s + m), whi[s][:, w], wlo[s][:, w], x_h[:, k, :], x_l[:, k, :],
                                           k == 0, k == 3)
                last.then_inc(pe_done, 1)
            pair_layer("mix", h_hi, h_lo, arrive=lambda k: pe.wait_ge(evac, tab["branch"][0] + k // 2 + 1))

            b, n, _, _ = tab["mem_kv"]
            for i in range(n):
                pair_unit(b + i, (b + i) % 2, hm_hi, hm_lo, MEM)
                if i == 0:
                    norm_stats(0, 9)
                if i == 2:
                    norm_spread(0)
            pe.wait_ge(evac, b + n)
            for n in range(4):
                for j in range(4):
                    f = 4 * (n % 2) + j
                    last = nc.tensor.transpose(bank(n)[:, j * P:j * P + P], vmraw[:, f, P * (n // 2):P * (n // 2) + P], ident)
                last.then_inc(vt_ps, 1)
            pe.wait_ge(vt_lo, TT + 4)
            pair_layer("mem_q", h_hi, h_lo, arrive=lambda k: pe.wait_ge(hlo, KT + k + 1))
            b, n, _, _ = tab["mem_q"]
            pe.wait_ge(evac, b + n)

            def mem_scores(g):
                if g >= 2:
                    pe.wait_ge(ms_exp, TT * (g - 1))
                for n in range(TT):
                    for k in range(2):
                        f = 2 * g + k
                        q = [x[:, f, n * P:n * P + P] for x in (qm_hi, qm_lo)]
                        c = [x[:, f, :] for x in (km_hi, km_lo)]
                        last = product(ps[:, 2 * (g % 2) + n // 2, 256 * (n % 2):256 * (n % 2) + 256], q[0], q[1], c[0], c[1],
                                       k == 0, k == 1)
                last.then_inc(ms_ps, 1)

            mem_scores(0)
            for g in range(MEM_HEADS):
                if g + 1 < MEM_HEADS:
                    mem_scores(g + 1)
                pe.wait_ge(ms_norm, TT * (g + 1))
                if g:
                    pe.wait_ge(mp_lo, g)
                for c in range(2):
                    for n in range(TT):
                        last = nc.tensor.transpose(bank(4 + c)[:, n * P:n * P + P], em[:, g % 2, n, c * P:c * P + P], ident)
                last.then_inc(mp_ps, 1)
                pe.wait_ge(mp_lo, g + 1)
                if g:
                    pe.wait_ge(mo_lo, 2 * g)
                for m in range(2):
                    for c in range(2):
                        w = [x[:, c, g * 256 + m * P:g * 256 + m * P + P] for x in (vm_hi, vm_lo)]
                        last = product(bank(6 + m), w[0], w[1], pt_hi[:, c, :], pt_lo[:, c, :], c == 0, c == 1)
                    last.then_inc(mo_ps, 1)
            pair_layer("mem_o", h_hi, h_lo, arrive=lambda k: pe.wait_ge(mo_lo, k + 1))
            norm_stats(1, 18)
            norm_spread(1)
            pair_layer("up0", h_hi, h_lo, arrive=lambda k: pe.wait_ge(hlo, 2 * KT + k + 1), after_first=lambda: mod_group(0))
            mod_group(1)
            down_layer("down0", "up0")
            pair_layer("up1", h_hi, h_lo)
            mod_group(2)
            down_layer("down1", "up1")
            norm_stats(2, 27)
            norm_spread(2)
            mod_group(3)
            norm_stats(3, 36)
            norm_spread(3)

            def head_stats(job):
                ctx_too = job["hi_c"] is not None
                pe.wait_ge(hn_sq, hn_sq_count(job))
                pairs_of = cst[:, C_HEADS:C_HEADS + 2]
                for m in range(2):
                    for q in range(TT):
                        last = mm(bank(6)[:, 8 * m + 2 * q:8 * m + 2 * q + 2], hsq[:, m, q * P:q * P + P], pairs_of,
                                  start=True, stop=True)
                for m in range(2 if ctx_too else 0):
                    for q in range(2):
                        last = mm(bank(6)[:, 16 + 4 * m + 2 * q:18 + 4 * m + 2 * q], hsqc[:, m, q * P:q * P + P], pairs_of,
                                  start=True, stop=True)
                last.then_inc(hn_ps, 1)

            def hn_sq_count(job):
                return 2 * (job["unit"] + 1) if job["unit"] < 4 else 8 + job["unit"] - 3

            def head_spread(job, m):
                r = job["round"] + m
                pe.wait_ge(hn_x, r + 1)
                if r:
                    pe.wait_ge(hn_lo, r)
                for q in range(TT):
                    last = nc.tensor.transpose(bank(7)[:, q * P:q * P + P],
                                               rexp[:, 2 * q:2 * q + 2, :].rearrange("p h n -> p (h n)"), ident)
                last.then_inc(hn_r, 1)

            b, n, _, _ = tab["na_qkv"]
            for i in range(n):
                s = (b + i) % 2
                unit(b + i)
                job = (head_jobs(i) or [None])[0]
                between = [] if job is None else [lambda: head_stats(job)] + [
                    (lambda m=m: head_spread(job, m)) for m in range(3 if job["hi_c"] is not None else 2)]
                for k in range(KT):
                    if i == 0:
                        pe.wait_ge(hlo, 3 * KT + k + 1)
                    for m in range(2):
                        w = slice(256 * k + 128 * m, 256 * k + 128 * m + 128)
                        last = product(bank(2 * s + m), whi[s][:, w], wlo[s][:, w], h_hi[:, k, :], h_lo[:, k, :],
                                       k == 0, k == KT - 1)
                    if k % 2 and between:
                        between.pop(0)()
                if i == 0:
                    pe.wait_ge(hc_l, 1)
                for m in range(0 if 4 <= i < 8 else 2):
                    for k in range(KT):
                        w = slice(256 * k + 128 * m, 256 * k + 128 * m + 128)
                        last = product(bank(4 + s)[:, 256 * m:256 * m + 256], whi[s][:, w], wlo[s][:, w],
                                       hc_hi[:, k, :], hc_lo[:, k, :], k == 0, k == KT - 1)
                assert not between
                last.then_inc(pe_done, 1)
            pe.wait_ge(hn_lo, 20)
            pe.wait_ge(evac, b + n)

            def na_scores(g):
                head, tau = divmod(g, 4)
                a, rows = head // 2, slice(64 * (head % 2), 64 * (head % 2) + 64)
                if g >= 4:
                    pe.wait_ge(ns_exp, g - 3)
                q = [x[rows, a, P * tau:P * tau + P] for x in (q_hi, q_lo)]
                k = [grid(x[rows, a, :])[:, :, span[tau]:span[tau] + 32] for x in (k_hi, k_lo)]
                c = [x[rows, a, :] for x in (kc_hi, kc_lo)]
                product(bank(tau, 256), q[0], q[1], k[0], k[1], True, True)
                product(ps[:, tau, 256:512], q[0], q[1], c[0], c[1], True, True).then_inc(ns_ps, 1)

            def na_transpose(g):
                pe.wait_ge(ns_norm, g + 1)
                if g >= 2:
                    pe.wait_ge(np_l, g - 1)
                for c in range(4):
                    last = nc.tensor.transpose(bank(4 + g % 2)[:, c * P:c * P + P], sc[:, g % 4, c * P:c * P + P], ident)
                last.then_inc(np_ps, 1)

            def na_values(g):
                head, tau = divmod(g, 4)
                a, cols = head // 2, slice(64 * (head % 2), 64 * (head % 2) + 64)
                pe.wait_ge(np_l, g + 1)
                if tau == 0:
                    pe.wait_ge(nv_lo, 3 * a + 3)
                    if head:
                        pe.wait_ge(no_lo, head)
                for c in range(4):
                    chunk = 2 * tau + c if c < 2 else 6 + c
                    last = product(bank(6)[0:64, tau * P:tau * P + P], vt_h[a % 2][:, chunk, cols], vt_l[a % 2][:, chunk, cols],
                                   np_hi[:, g % 2, c * P:c * P + P], np_lo[:, g % 2, c * P:c * P + P], c == 0, c == 3)
                if tau == 3:
                    last.then_inc(no_ps, 1)

            def na_v(a, r):
                if r == 0:
                    pe.wait_ge(vw_done, a + 1)
                if a or r:
                    pe.wait_ge(nv_lo, 3 * a + r)
                for x in range(4 if r < 2 else 2):
                    if r < 2:
                        tau, c = 2 * r + x // 2, x % 2
                        src = vw[:, tau, 4 * c:4 * c + 4, :].rearrange("p r c -> p (r c)")
                    else:
                        src = vp[a % 2][:, SEQ + x * P:SEQ + x * P + P]
                    last = nc.tensor.transpose(bank(7)[:, x * P:x * P + P], src, ident)
                last.then_inc(nv_ps, 1)

            for g in range(4):
                na_scores(g)
            for r in range(3):
                na_v(0, r)
            for g in range(4 * NA_HEADS):
                na_transpose(g)
                if g + 4 < 4 * NA_HEADS:
                    na_scores(g + 4)
                if g:
                    na_values(g - 1)
                a, st = divmod(g, 8)
                if st in (1, 3, 5) and a + 1 < NA_HEADS // 2:
                    na_v(a + 1, st // 2)
            na_values(4 * NA_HEADS - 1)

            pair_layer("na_o", q_hi, q_lo, arrive=lambda k: pe.wait_ge(no_lo, 2 * k + 2))
            norm_stats(4, 45)
            norm_spread(4)
            pair_layer("nup0", h_hi, h_lo, arrive=lambda k: pe.wait_ge(hlo, 4 * KT + k + 1))
            down_layer("ndown0", "nup0")
            pair_layer("nup1", h_hi, h_lo)
            down_layer("ndown1", "nup1")
            pe.wait_ge(evac, n_units)
            for n in range(TT):
                for k in range(KT):
                    last = nc.tensor.transpose(bank(2 * n + k // 4)[:, (k % 4) * P:(k % 4) * P + P],
                                               xT[:, k, n * P:n * P + P], ident)
                    if k % 4 == 3:
                        last.then_inc(out_T, 1)

        @block.gpsimd
        def _(pool):
            pool.memset(rpb_pad[:, :, :], 0.0).then_inc(rpb_zero, 1)
            pool.wait_ge(rpb_zero, 1)
            pool.dma_start(rpb_pad[:, :, 17:48], t["l0_na_rpb_2"].rearrange("h a c -> (h a) c")
                           .rearrange("(p o) c -> p o c", o=2)).then_inc(rpb_in, 16)
            pool.dma_start(bass.AP(rpb_scr, TABLE, [[COPY + 1, 16], [1, 16]]), rpb_pad[0:16, 0, 0:16]).then_inc(rpb_copy, 16)
            pool.wait_ge(rpb_in, 16)
            scr = rpb_scr.ap()
            with pool.Fori(0, 16, 1) as c:
                pool.dma_start(scr[at(c * (COPY + 1), TABLE)].rearrange("(p n) -> p n", p=120),
                               rpb_pad[:, :, :].rearrange("p o c -> p (o c)")).then_inc(rpb_copy, 16)
            pool.wait_ge(rpb_copy, 16 * 17)
            for row in range(GRID_H):
                pool.dma_start(bias_scr[row], bass.AP(rpb_scr, 16 + (7 - row) * 48, [[COPY, 16], [PITCH, NA_HEADS], [1, GRID_H * 48]])
                               ).then_inc(rpb_out, 16)

            w_mod = t["l0_w_mod_2"].rearrange("(k p) n -> p k n", p=P)
            pool.wait_ge(silu_c_done, 1)
            pool.wait_ge(mo_lo, 2 * MEM_HEADS)

            def mod_load(b, col):
                pool.dma_start(mod_raw[b][:, :, :], w_mod[:, :, at(col, 256)]).then_inc(mod_in[b], 16)

            def mod_sum(step, b, vec, col):
                pool.tensor_tensor(mod_tmp[:, :, :], mod_raw[b][:, :, :],
                                   silu_c[:, vec:vec + 8].rearrange("p (k o) -> p k o", o=1).to_broadcast([P, KT, 256]),
                                   ALU.mult).then_inc(mod_step, 1)
                pool.wait_ge(mod_step, step + 1)
                pool.tensor_tensor(mod_tmp[:, 0:4, :], mod_tmp[:, 0:4, :], mod_tmp[:, 4:8, :], ALU.add).then_inc(mod_step, 1)
                pool.wait_ge(mod_step, step + 2)
                pool.tensor_tensor(mod_tmp[:, 0:2, :], mod_tmp[:, 0:2, :], mod_tmp[:, 2:4, :], ALU.add).then_inc(mod_step, 1)
                pool.wait_ge(mod_step, step + 3)
                pool.tensor_tensor(mod_acc[:, at(col, 256)].rearrange("p (o n) -> p o n", o=1), mod_tmp[:, 0:1, :],
                                   mod_tmp[:, 1:2, :], ALU.add).then_inc(mod_step, 1)
                pool.wait_ge(mod_step, step + 4)

            def mod_chunk(c, step, b, both, col, load):
                pool.wait_ge(mod_in[b], c * 8 + (16 if b == 0 else 8))
                mod_sum(step, b, 0, col)
                if both:
                    mod_sum(step + 4, b, 8, col + 1024)
                if load is not None:
                    mod_load(b, load)

            mod_load(0, 0)
            mod_load(1, 256)
            for group, (first, cols, both) in enumerate(MOD_GROUPS):
                if group:
                    pool.wait_ge(mod_ps, group)
                n, per = cols // 256, 8 if both else 4
                with pool.Fori(0, n // 2 - 1, 1) as i:
                    for b in range(2):
                        mod_chunk(i * 2 + (first // 256 + b), i * (2 * per) + (32 * group + per * b), b, both,
                                  i * 512 + 256 * b, i * 512 + (first + 512 + 256 * b))
                for b in range(2):
                    c = n - 2 + b
                    mod_chunk(first // 256 + c, 32 * group + per * c, b, both, 256 * c,
                              first + cols + 256 * b if group < 3 else None)

            b, n, _, _ = tab["na_qkv"]
            for i in range(4):
                pool.wait_ge(evac, b + 8 + i + 1)
                pool.dma_start(v_scr[2 * i:2 * i + 2].rearrange("t p n -> p t n"), v_out[:, :, :]).then_inc(v_spill, 16)
            pool.wait_ge(v_spill, 16)
            pool.wait_ge(rpb_out, 16 * GRID_H)

            def load_bias(head):
                pool.dma_start(gb[head % 2][:, :, :].rearrange("p i x -> p (i x)"),
                               bias_scr.rearrange("r c h n -> (r c) h n")[:, head, :]).then_inc(gb_in[head % 2], 16)

            def build_bias(head):
                pool.wait_ge(gb_in[head % 2], 16 * (head // 2 + 1))
                for kind, x0 in enumerate((16, 8, 0)):
                    w = cst[:, C_WIN + 32 * kind:C_WIN + 32 * kind + 32].rearrange("p (o j) -> p o j", o=1).to_broadcast([P, 8, 32])
                    last = pool.tensor_tensor(bias[head % 2][:, kind, :, :], gb[head % 2][:, :, x0:x0 + 32], w, ALU.add)
                last.then_inc(bias_done, 1)

            load_bias(0)
            load_bias(1)
            for a in range(2):
                pool.dma_start(vp[a][:, :], v_scr[a]).then_inc(vp_in[a], 16)
            for head in range(2):
                build_bias(head)
            pool.wait_ge(bias_done, 2)
            load_bias(2)
            load_bias(3)

            def window_values(a):
                pool.wait_ge(vp_in[a % 2], 16 * (a // 2 + 1))
                for tau in range(TT):
                    last = pool.tensor_copy(vw[:, tau, :, :], grid(vp[a % 2][:, 0:SEQ])[:, :, span[tau]:span[tau] + 32])
                last.then_inc(vw_done, 1)

            def normalise(g):
                pool.wait_ge(ns_rden, g + 1)
                pool.tensor_tensor(sc[:, g % 4, :], sc[:, g % 4, :], na_rden[:, g % 4:g % 4 + 1].to_broadcast([P, 512]),
                                   ALU.mult).then_inc(ns_norm, 1)

            normalise(0)
            for g in range(4 * NA_HEADS):
                if g + 1 < 4 * NA_HEADS:
                    normalise(g + 1)
                head, tau = divmod(g, 4)
                if tau == 1 and head + 2 < NA_HEADS:
                    pool.wait_ge(ns_max, 4 * head + 4)
                    build_bias(head + 2)
                    if head + 4 < NA_HEADS:
                        pool.wait_ge(bias_done, head + 3)
                        load_bias(head + 4)
                a = g // 8
                if g % 8 == 0 and a + 1 < NA_HEADS // 2:
                    pool.wait_ge(nv_ps, 3 * (a + 1))
                    window_values(a + 1)
                    if g == 0:
                        pool.wait_ge(v_spill, 64)
                    if a + 2 < NA_HEADS // 2:
                        pool.dma_start(vp[a % 2][:, :], v_scr[a + 2]).then_inc(vp_in[a % 2], 16)



_OUT_SHAPE = (1, SEQ, D)


def kernel(**inputs):
    import concourse.bacc as bacc
    from concourse.bass_utils import run_bass_kernel_spmd

    nc = bacc.Bacc("TRN2", target_bir_lowering=False, num_devices=1)
    arrays, t = {}, {}
    for name in INPUTS:
        a = np.ascontiguousarray(inputs[name])
        arrays[f"in_{name}"] = a
        t[name] = nc.dram_tensor(f"in_{name}", a.shape, mybir.dt.from_np(a.dtype), kind="ExternalInput").ap()
    arrays["in_consts"] = constants()
    consts = nc.dram_tensor("in_consts", (P, C_ALL), F32, kind="ExternalInput").ap()
    out = nc.dram_tensor("out", _OUT_SHAPE, F32, kind="ExternalOutput").ap()
    program(nc, t, consts, out)
    r = run_bass_kernel_spmd(nc, [arrays], core_ids=[0])
    return r.results[0]["out"]
```

```python
from contextlib import ExitStack

import numpy as np
import concourse.bass as bass
from concourse import mybir

F32 = mybir.dt.float32
F32R = mybir.dt.float32r
ACT = mybir.ActivationFunctionType
ALU = mybir.AluOpType
AX = mybir.AxisListType

P = 128
SEQ, MEM, CTX, D = 512, 256, 256, 1024
KT = D // P
TT = SEQ // P
SB_HEADS, SB_DIM = 8, 64
MEM_HEADS, MEM_DIM = 4, 256
FF = 2816
FT = FF // P
FH = FT // 2
GRID_W, GRID_H = 64, 8
NA_HEADS, NA_DIM, WIN_W = 16, 64, 16
EPS = 1e-6
NEG = -1.0e30

C_IDENT, C_TRI, C_ONES, C_MASK, C_ONE, C_EPS, C_HEADS, C_WIN = 0, 128, 256, 384, 512, 513, 514, 516
C_ALL = C_WIN + 96

LAYERS = [("qk", 4, 2048), ("v", 2, 2048), ("conv_in", 4, 2048), ("conv_gate", 2, 2048), ("gates", 8, 2048),
          ("branch", 4, 2048), ("mix", 4, 2048), ("mem_kv", 8, 2048), ("mem_q", 4, 2048), ("mem_o", 4, 2048),
          ("up0", FH, 2048), ("down0", KT, FH * P), ("up1", FH, 2048), ("down1", KT, FH * P),
          ("na_qkv", 12, 2048), ("na_o", 4, 2048),
          ("nup0", FH, 2048), ("ndown0", KT, FH * P), ("nup1", FH, 2048), ("ndown1", KT, FH * P)]


INPUTS = ["x", "mem", "norm_mix", "w_in", "conv_w", "w_branch_a", "w_branch_b", "w_mix_out", "norm_mem_q",
          "norm_mem_kv", "w_mem_q", "w_mem_kv", "w_mem_o", "norm_ffn", "w_ffn_in", "w_ffn_out", "norm_final",
          "c_2", "ctx_2", "c_ctx_2", "l0_w_mod_2", "l0_b_mod_2", "l0_norm1_2", "l0_norm2_2", "l0_na_w_qkv_2",
          "l0_na_q_gain_2", "l0_na_k_gain_2", "l0_na_rpb_2", "l0_na_w_o_2", "l0_ffn_w_up_2", "l0_ffn_conv_w_2",
          "l0_ffn_conv_b_2", "l0_ffn_w_down_2"]


def layer_table():
    table, at = {}, 0
    for n, (name, units, size) in enumerate(LAYERS):
        after = LAYERS[n + 1][2] if n + 1 < len(LAYERS) else 0
        table[name] = (at, units, size, after)
        at += units
    return table


def over(eng, n, base, body):
    if n <= 4:
        for i in range(n):
            body(i, (base + i) % 2, i == n - 1)
        return
    m = (n - 1) // 2 * 2
    with eng.Fori(0, m, 2) as i:
        body(i, base % 2, False)
        body(i + 1, (base + 1) % 2, False)
    for i in range(m, n):
        body(i, (base + i) % 2, i == n - 1)


def first_apart(eng, n, base, body, split_done):
    if not split_done:
        over(eng, n, base, body)
        return
    body(0, base % 2, False, split=False)
    over(eng, n - 1, base + 1, lambda i, s, last: body(i + 1, s, last))


def sb_heads(eng, body):
    with eng.Fori(0, SB_HEADS // 2 - 1, 1) as a:
        body(a * 2, a, 0, 2)
        body(a * 2 + 1, a, 1, 2)
    body(SB_HEADS - 2, SB_HEADS // 2 - 1, 0, 1)
    body(SB_HEADS - 1, SB_HEADS // 2 - 1, 1, 0)


def at(x, n=1):
    return bass.ds(x, n)


def constants():
    c = np.zeros((P, C_ALL), np.float32)
    r = np.arange(P)
    c[:, C_IDENT:C_IDENT + P] = np.eye(P)
    c[:, C_TRI:C_TRI + P] = np.where(r[:, None] >= r[None, :], -1.0, 0.0)
    c[:, C_ONES:C_ONES + P] = -1.0
    c[:, C_MASK:C_MASK + P] = np.where(r[:, None] >= r[None, :], NEG, 0.0)
    c[:, C_ONE] = 1.0
    c[:, C_EPS] = EPS
    c[0:64, C_HEADS] = 1.0
    c[64:128, C_HEADS + 1] = 1.0
    cl, jl = (r % 16)[:, None], np.arange(32)[None, :]
    for n, strip in enumerate((0, 1, 3)):
        col = 16 * strip + cl
        start = np.clip(col - WIN_W // 2, 0, GRID_W - WIN_W)
        key = min(max(16 * strip - 8, 0), 32) + jl
        c[:, C_WIN + 32 * n:C_WIN + 32 * n + 32] = np.where((key >= start) & (key < start + WIN_W), 0.0, NEG)
    return c


def program(nc, t, consts, out):
    tab = layer_table()
    n_units = sum(x[1] for x in tab.values())
    ctx = ExitStack()
    with ctx:
        base = 16512

        def place(name, off, shape, dt=F32):
            return nc.alloc_sbuf_tensor_at(name, shape, dt, offset=base + 4 * off)

        xT = place("xT", 0, [P, KT, SEQ])
        raw = [place(f"w_raw{s}", 4096 + 2048 * s, [P, 2048]) for s in range(2)]
        whi = [place(f"w_hi{s}", 8192 + 2048 * s, [P, 2048], F32R) for s in range(2)]
        wlo = [place(f"w_lo{s}", 12288 + 2048 * s, [P, 2048], F32R) for s in range(2)]
        h_hi = place("h_hi", 16384, [P, KT, SEQ], F32R)
        h_lo = place("h_lo", 20480, [P, KT, SEQ], F32R)
        cst = place("cst", 24576, [P, C_ALL])
        cstr = place("cstr", 25192, [P, 512], F32R)
        vecA = place("vecA", 25704, [P, 112])
        vecB = place("vecB", 25816, [P, 120])
        small = place("small", 25936, [P, 432])
        G = 26368

        ident = cst[:, C_IDENT:C_IDENT + P]
        one = cst[:, C_ONE:C_ONE + 1]
        eps = cst[:, C_EPS:C_EPS + 1]
        r_ident, r_tri, r_ones, r_mask = (cstr[:, P * n:P * n + P] for n in range(4))
        std = small[:, 0:4]
        rstd = small[:, 4:8]
        sumsq = small[:, 8:16]
        std0 = small[:, 16:24]
        rstd0 = small[:, 24:32]
        nmax = small[:, 32:40]
        den = small[:, 40:48]
        rden = small[:, 48:56]

        V_MIX, V_MQ, V_MKV, V_FFN, V_FIN, V_N1, V_N2, V_CONV, V_C, V_CC, V_QG, V_KG, V_CB = \
            0, 8, 16, 24, 32, 40, 48, 56, 68, 76, 84, 85, 86
        NA_ROWS = 108
        V_BMOD, V_CW = 0, 48
        NB_ROWS = 114
        vcol = lambda n: vecA[:, n:n + 1]

        tb = [place("tb0", G + 9728, [P, 512]), place("tb1", G + 24064, [P, 512])]
        tb3 = [tb[0], place("tb3", G + 11776, [P, 512])]
        sq = place("sq", G + 10240, [P, 2, SEQ])
        sqacc = place("sqacc", G + 11264, [P, SEQ])

        xn = place("x_rows", G + 16384, [P, TT, D])
        rowsA = place("rowsA", G + 20480, [P, P])
        rowsB = place("rowsB", G + 20608, [P, P])
        junk = place("junk", 16384, [P, D])
        qk_hi = place("qk_hi", G + 0, [P, 8, SEQ], F32R)
        qk_lo = place("qk_lo", G + 4096, [P, 8, SEQ], F32R)
        v_hi = place("v_hi", G + 8192, [P, TT, 512], F32R)
        v_lo = place("v_lo", G + 10240, [P, TT, 512], F32R)
        yb_hi = place("yb_hi", G + 12288, [P, 4, SEQ], F32R)
        yb_lo = place("yb_lo", G + 14336, [P, 4, SEQ], F32R)
        vraw = place("vraw", G + 16384, [P, 4, SEQ])
        usb = place("usb", G + 18432, [P, 2, SEQ])
        cu = place("cu", G + 19456, [P, 2, 516])
        cv = place("cv", G + 20488, [P, 4, SEQ])
        ybf = place("ybf", G + 22536, [P, 2, SEQ])
        sbT = [place(f"sbT{b}", G + 16384 + 5120 * b, [P, 1280]) for b in range(2)]
        sbS = [place(f"sbS{b}", G + 17664 + 5120 * b, [P, 1280]) for b in range(2)]
        sb_hi = [place(f"sb_hi{b}", G + 18944 + 5120 * b, [P, 1280], F32R) for b in range(2)]
        sb_lo = [place(f"sb_lo{b}", G + 20224 + 5120 * b, [P, 1280], F32R) for b in range(2)]
        mn = place("mn", G + 8192, [P, 4, D])
        hm_hi = place("hm_hi", G + 2048, [P, KT, MEM], F32R)
        hm_lo = place("hm_lo", G + 6144, [P, KT, MEM], F32R)
        ctxT = place("ctxT", G + 24576, [P, KT, CTX])
        mc_junk = place("mc_junk", G + 24576, [P, D])
        sig = place("sig", G + 16384, [P, 2, KT, SEQ])
        mg = place("mg", G + 8192, [P, 2, SEQ])
        mt = place("mt", G + 9216, [P, 2, SEQ])
        vmraw = place("vmraw", G + 0, [P, KT, MEM])
        km_hi = place("km_hi", G + 12288, [P, KT, MEM], F32R)
        km_lo = place("km_lo", G + 14336, [P, KT, MEM], F32R)
        vm_hi = place("vm_hi", G + 16384, [P, 2, D], F32R)
        vm_lo = place("vm_lo", G + 18432, [P, 2, D], F32R)
        qm_hi = place("qm_hi", G + 0, [P, KT, SEQ], F32R)
        qm_lo = place("qm_lo", G + 4096, [P, KT, SEQ], F32R)
        em = place("em", G + 20480, [P, 2, TT, MEM])
        pt_hi = place("pt_hi", G + 22528, [P, 2, SEQ], F32R)
        pt_lo = place("pt_lo", G + 8192, [P, 2, SEQ], F32R)
        a_hi = place("a_hi", G + 0, [P, FH, SEQ], F32R)
        a_lo = place("a_lo", G + 16384, [P, FH, SEQ], F32R)
        sg = place("sg", G + 5632, [P, 2, SEQ])
        af = place("af", G + 6656, [P, 2, SEQ])

        mod_raw = [place(f"mod_raw{b}", G + 11776 + 2048 * b, [P, KT, 256]) for b in range(2)]
        mod_tmp = place("mod_tmp", G + 7680, [P, KT, 256])
        mod_acc = [place("mod_acc0", G + 22016, [P, 2048]), place("mod_acc1", G + 9728, [P, 2048])]
        MOD_GROUPS = [(0, 1024, True), (1024, 1024, True), (2048, 2048, False), (4096, 2048, False)]
        silu_c = small[:, 56:72]
        modv = small[:, 72:136]
        gain1, gain2, gain1c = (small[:, x:x + 8] for x in (136, 144, 152))
        qgain = small[:, 160:161]
        na_nmax_c, na_max, na_nmax = (small[:, x:x + 4] for x in (164, 168, 172))
        na_den, na_rden = small[:, 176:180], small[:, 180:184]
        rpb_pad = place("rpb_pad", 25936 + 200, [120, 2, 48])
        hn_std = place("hn_std", 25936 + 296, [P, 24])
        hn_rstd = place("hn_rstd", 25936 + 320, [P, 24])
        q_hi = place("q_hi", G + 0, [P, KT, SEQ], F32R)
        q_raw = place("q_raw", G + 4096, [P, KT, SEQ])
        q_lo = place("q_lo", G + 4096, [P, KT, SEQ], F32R)
        k_hi = place("k_hi", G + 8192, [P, KT, SEQ], F32R)
        k_raw = place("k_raw", G + 12288, [P, KT, SEQ])
        k_lo = place("k_lo", G + 12288, [P, KT, SEQ], F32R)
        kc_hi = place("kc_hi", G + 16384, [P, KT, CTX], F32R)
        kc_raw = place("kc_raw", G + 18432, [P, KT, CTX])
        kc_lo = place("kc_lo", G + 18432, [P, KT, CTX], F32R)
        hc_hi = place("hc_hi", G + 20480, [P, KT, CTX], F32R)
        hc_lo = place("hc_lo", G + 22528, [P, KT, CTX], F32R)
        v_out = place("v_out", G + 24576, [P, 2, SEQ + CTX])
        hsq = place("hsq", G + 24576, [P, 2, SEQ])
        hsqc = place("hsqc", G + 25600, [P, 2, CTX])
        rexp = [place("rexp0", G + 26112, [P, 8, 64]), place("rexp1", G + 25600, [P, 8, 64])]
        vw = place("vw", G + 25344, [P, TT, 8, 32])
        vw_first = place("vw_first", 18944 + 1280, [P, TT, 8, 32])
        vt_h = [place(f"vt_h{b}", 16384 + 1280 * b, [P, 10, P], F32R) for b in range(2)]
        vt_l = [place(f"vt_l{b}", 18944 + 1280 * b, [P, 10, P], F32R) for b in range(2)]
        sc = place("sc", 21504, [P, 4, 512])
        np_hi = place("np_hi", 23552, [P, 2, 512], F32R)
        np_lo = place("np_lo", G + 24320, [P, 2, 512], F32R)
        vp = [place(f"vp{b}", G + 20480 + 768 * b, [P, SEQ + CTX]) for b in range(2)]
        bias = [place(f"bias{b}", G + 22016 + 768 * b, [P, 3, 8, 32]) for b in range(2)]
        gb = [place(f"gb{b}", G + 23552 + 384 * b, [P, 8, 48]) for b in range(2)]
        gs = place("gs", G + 5632, [P, 2, 516])
        gl = place("gl", G + 6664, [P, 2, SEQ])
        gc = place("gc", G + 7688, [P, 2, SEQ])
        gf = place("gf", G + 8712, [P, 2, SEQ])
        out_rows = place("out_rows", G + 16384, [P, TT, D])

        v_scr = nc.dram_tensor("v_scr", (KT, P, SEQ + CTX), F32).ap()
        PITCH = 15 * 48
        TABLE = NA_HEADS * PITCH
        COPY = TABLE + 32
        rpb_scr = nc.dram_tensor("rpb_scr", (16 * COPY + 16,), F32)
        bias_scr = nc.dram_tensor("bias_scr", (GRID_H, 16, NA_HEADS, GRID_H * 48), F32).ap()

        ps = ctx.enter_context(nc.psum_tensor("ps", [P, 8, 512], F32))

        def bank(n, cols=512):
            return ps[:, n, 0:cols]

        def sem(name):
            return ctx.enter_context(nc.semaphore(name))

        w_dma = [sem(f"w_dma{s}") for s in range(2)]
        w_hi, w_lo, pe_done, evac = sem("w_hi"), sem("w_lo"), sem("pe_done"), sem("evac")
        cst_in, vec_in = sem("cst_in"), sem("vec_in")
        x_in = [sem(f"x_in{n}") for n in range(TT)]
        mc_in = [sem(f"mc_in{n}") for n in range(4)]
        cstr_done, vec_T, vec_sb = sem("cstr_done"), sem("vec_T"), sem("vec_sb")
        ss_x, std_x, rstd_x = sem("ss_x"), sem("std_x"), sem("rstd_x")
        xT_ps, xT_dve, xT_act = sem("xT_ps"), sem("xT_dve"), sem("xT_act")
        stat_ps, std_done, rstd_done, r_ps = sem("stat_ps"), sem("std_done"), sem("rstd_done"), sem("r_ps")
        ht, hhi, hlo = sem("ht"), sem("hhi"), sem("hlo")
        x_sq, x_acc = sem("x_sq"), sem("x_acc")
        split_hi = sem("split_hi")
        usb_done, conv_step = sem("usb_done"), sem("conv_step")
        cu_zero = sem("cu_zero")
        ybf_done, yb_hi_done = sem("ybf_done"), sem("yb_hi_done")
        vt_ps, vt_hi, vt_lo = sem("vt_ps"), sem("vt_hi"), sem("vt_lo")
        z_ps, z_abs, z_exp, z_ln, sp_done, sp_hi, sp_lo = (sem(n) for n in (
            "z_ps", "z_abs", "z_exp", "z_ln", "sp_done", "sp_hi", "sp_lo"))
        tri_ps, wt_done, wt_hi, wt_lo, pv_ps, o_hi_done, o_lo_done = (sem(n) for n in (
            "tri_ps", "wt_done", "wt_hi", "wt_lo", "pv_ps", "o_hi_done", "o_lo_done"))
        mc_ss, mc_std, mc_rstd, mc_scaled, mc_T, mc_hi, mc_lo = (sem(n) for n in (
            "mc_ss", "mc_std", "mc_rstd", "mc_scaled", "mc_T", "mc_hi", "mc_lo"))
        sig_done = sem("sig_done")
        br_step, mg_done, mg_hi = sem("br_step"), sem("mg_done"), sem("mg_hi")
        ms_ps, ms_max, ms_exp, ms_rden, ms_norm, mp_ps, mp_hi, mp_lo, mo_ps, mo_hi, mo_lo = (sem(n) for n in (
            "ms_ps", "ms_max", "ms_exp", "ms_rden", "ms_norm", "mp_ps", "mp_hi", "mp_lo", "mo_ps", "mo_hi", "mo_lo"))
        silu_done, af_done, a_hi_done, a_lo_done = (sem(n) for n in ("silu_done", "af_done", "a_hi_done", "a_lo_done"))
        silu_c_done, mod_step, mod_ps, mod_sb, mod_vec = (sem(n) for n in (
            "silu_c_done", "mod_step", "mod_ps", "mod_sb", "mod_vec"))
        mod_in = [sem(f"mod_in{b}") for b in range(2)]
        rpb_zero, rpb_in, rpb_copy, rpb_out = sem("rpb_zero"), sem("rpb_in"), sem("rpb_copy"), sem("rpb_out")
        xfin, hc_t, hc_h, hc_l = sem("xfin"), sem("hc_t"), sem("hc_h"), sem("hc_l")
        v_spill = sem("v_spill")
        hn_sq, hn_ps, hn_sd, hn_rd, hn_x, hn_r, hn_t, hn_hi, hn_lo = (sem(n) for n in (
            "hn_sq", "hn_ps", "hn_sd", "hn_rd", "hn_x", "hn_r", "hn_t", "hn_hi", "hn_lo"))
        vw_done = sem("vw_done")
        vp_in = [sem(f"vp_in{b}") for b in range(2)]
        gb_in = [sem(f"gb_in{b}") for b in range(2)]
        bias_done = sem("bias_done")
        nv_ps, nv_hi, nv_lo = sem("nv_ps"), sem("nv_hi"), sem("nv_lo")
        ns_ps, ns_red, ns_max, ns_exp, ns_rden, ns_norm = (sem(n) for n in (
            "ns_ps", "ns_red", "ns_max", "ns_exp", "ns_rden", "ns_norm"))
        np_ps, np_h, np_l, no_ps, no_hi, no_lo = (sem(n) for n in ("np_ps", "np_h", "np_l", "no_ps", "no_hi", "no_lo"))
        gs_zero, gs_done, gc_step, gl_done, gf_done, ga_hi = (sem(n) for n in (
            "gs_zero", "gs_done", "gc_step", "gl_done", "gf_done", "ga_hi"))
        out_T, out_sb, out_dma = sem("out_T"), sem("out_sb"), sem("out_dma")

        def hstat(with_context):
            return bank(6)[:, 0:24 if with_context else 16]

        def head_jobs(i):
            if 1 <= i <= 4:
                return [dict(j=i - 1, raw=k_raw, hi=k_hi, lo=k_lo, tmp=None, raw_c=kc_raw, hi_c=kc_hi, lo_c=kc_lo,
                             unit=i - 1, round=3 * (i - 1))]
            if 5 <= i <= 8:
                return [dict(j=i - 5, raw=q_raw, hi=q_hi, lo=q_lo, tmp=hsq, raw_c=None, hi_c=None, lo_c=None,
                             unit=i - 1, round=12 + 2 * (i - 5))]
            return []

        NA_V_STEPS = (3, 5, 6)
        span = [0, 8, 24, 32]

        def grid(x):
            return x.rearrange("p (r c) -> p r c", c=GRID_W)

        def strips(x):
            return x.rearrange("p (t r c) -> p t r c", t=TT, c=16)

        def strips_of_rows(x):
            return x.rearrange("p (r t c) -> p t r c", t=TT, c=16)

        def head_tiles(job, m):
            j = job["j"]
            if m == 2:
                return tuple(job[x][:, 2 * j:2 * j + 2, :] for x in ("raw_c", "hi_c", "lo_c"))
            full, high, low = (job[x][:, 2 * j + m, :] for x in ("raw", "hi", "lo"))
            if job["tmp"] is None:
                return full, high, low
            return strips_of_rows(job["tmp"][:, m, :]), strips(high), strips(low)

        def head_bank(i, m):
            return 7 if m != 1 else 4 + (tab["na_qkv"][0] + i + 1) % 2

        VECTORS = [(rowsA, V_MIX, "norm_mix", 8), (rowsA, V_MQ, "norm_mem_q", 8), (rowsA, V_MKV, "norm_mem_kv", 8),
                   (rowsA, V_FFN, "norm_ffn", 8), (rowsA, V_FIN, "norm_final", 8), (rowsA, V_N1, "l0_norm1_2", 8),
                   (rowsA, V_N2, "l0_norm2_2", 8), (rowsA, V_CONV, "conv_w", 12), (rowsA, V_C, "c_2", 8),
                   (rowsA, V_CC, "c_ctx_2", 8), (rowsA, V_CB, "l0_ffn_conv_b_2", 22),
                   (rowsB, V_BMOD, "l0_b_mod_2", 48), (rowsB, V_CW, "l0_ffn_conv_w_2", 66)]

        def vector_loads(eng):
            for rows, r0, name, n in VECTORS:
                src = t[name]
                letters = "abc"[:len(src.shape)]
                flat = src if len(src.shape) == 1 else src.rearrange(f"{' '.join(letters)} -> ({' '.join(letters)})")
                eng.dma_start(rows[r0:r0 + n, :], flat.rearrange("(r p) -> r p", p=P)).then_inc(vec_in, 16)
            for r0, name in ((V_QG, "l0_na_q_gain_2"), (V_KG, "l0_na_k_gain_2")):
                for g in range(2):
                    eng.dma_start(rowsA[r0:r0 + 1, 64 * g:64 * g + 64],
                                  t[name].rearrange("(r p) -> r p", r=1)).then_inc(vec_in, 16)

        block = ctx.enter_context(nc.Block())

        @block.sync
        def _(sp):
            x_rows = t["x"].rearrange("b (n p) d -> (b n) p d", p=P)
            for n in range(TT):
                sp.dma_start(xn[:, n, :], x_rows[n]).then_inc(x_in[n], 16)
            def load(u, s, parts):
                if not isinstance(u, int) or u >= 2:
                    sp.wait_ge(w_lo, u - 1)
                for dst, src in parts:
                    sp.dma_start(dst, src).then_inc(w_dma[s], 16)

            def weights(name):
                return t[name].rearrange("l (k p) n -> p (l k) n", p=P)

            def pair_layer(name, w, col0=0, after_first=None):
                b, n, _, _ = tab[name]

                def body(i, s, last):
                    dst = raw[s][:, :].rearrange("p (k n) -> p k n", n=256)
                    load(b + i, s, [(dst[:, 4 * g:4 * g + 4, :], w[:, 4 * g:4 * g + 4, at(i * 256 + col0, 256)])
                                    for g in range(2)])
                    if after_first and i == 0:
                        after_first()
                over(sp, n, b, body)

            def two_layer(name, w, col_a, col_b):
                b, n, _, _ = tab[name]

                def body(i, s, last):
                    dst = raw[s][:, :].rearrange("p (k n) -> p k n", n=256)
                    load(b + i, s, [(dst[:, :, 128 * g:128 * g + 128], w[:, :, at(i * 128 + c, 128)])
                                    for g, c in enumerate((col_a, col_b))])
                over(sp, n, b, body)

            def down_layer(name, w, k0):
                b, n, _, _ = tab[name]

                def body(i, s, last):
                    dst = raw[s][:, 0:FH * P].rearrange("p (k n) -> p k n", n=P)
                    load(b + i, s, [(dst[:, lo:hi, :], w[:, k0 + lo:k0 + hi, at(i * 128, 128)])
                                    for lo, hi in ((0, 6), (6, FH))])
                over(sp, n, b, body)

            w_in = weights("w_in")
            pair_layer("qk", w_in, 0, after_first=lambda: vector_loads(sp))
            pair_layer("v", w_in, 1024)
            two_layer("conv_in", w_in, 1536, 2560)
            pair_layer("conv_gate", w_in, 2048)
            two_layer("gates", w_in, 3072, 4096)
            b, n, _, _ = tab["branch"]
            w_a, w_b = weights("w_branch_a"), weights("w_branch_b")
            for i in range(n):
                s = (b + i) % 2
                dst = raw[s][:, :].rearrange("p (k n) -> p k n", n=256)
                load(b + i, s, [(dst[:, 0:4, :], w_a[:, :, 256 * i:256 * i + 256]),
                                (dst[:, 4:8, :], w_b[:, :, 256 * i:256 * i + 256])])
            pair_layer("mix", weights("w_mix_out"))
            pair_layer("mem_kv", weights("w_mem_kv"))
            pair_layer("mem_q", weights("w_mem_q"))
            pair_layer("mem_o", weights("w_mem_o"))
            two_layer("up0", weights("w_ffn_in"), 0, FF)
            down_layer("down0", weights("w_ffn_out"), 0)
            two_layer("up1", weights("w_ffn_in"), FH * P, FF + FH * P)
            down_layer("down1", weights("w_ffn_out"), FH)
            w_qkv = t["l0_na_w_qkv_2"].rearrange("(k p) n -> p k n", p=P)
            b, n, _, _ = tab["na_qkv"]
            for i in range(n):
                s = (b + i) % 2
                col = (1024, 0, 2048)[i // 4] + 256 * (i % 4)
                dst = raw[s][:, :].rearrange("p (k n) -> p k n", n=256)
                load(b + i, s, [(dst[:, 4 * g:4 * g + 4, :], w_qkv[:, 4 * g:4 * g + 4, col:col + 256]) for g in range(2)])
            w_o = t["l0_na_w_o_2"].rearrange("(k p) n -> p k n", p=P)

            def na_o_unit(i):
                u = tab["na_o"][0] + i
                dst = raw[u % 2][:, :].rearrange("p (k n) -> p k n", n=256)
                load(u, u % 2, [(dst[:, 4 * g:4 * g + 4, :], w_o[:, 4 * g:4 * g + 4, 256 * i:256 * i + 256]) for g in range(2)])

            def load_bias(head, slot):
                sp.dma_start(gb[slot][:, :, :].rearrange("p i x -> p (i x)"),
                             bias_scr.rearrange("r c h n -> (r c) h n")[:, at(head), :]
                             .rearrange("p h n -> p (h n)")).then_inc(gb_in[slot], 16)

            def load_values(a, slot):
                sp.dma_start(vp[slot][:, :], v_scr[at(a)].rearrange("o p n -> p (o n)")).then_inc(vp_in[slot], 16)

            for i in range(3):
                na_o_unit(i)
            sp.wait_ge(evac, sum(tab["na_qkv"][:2]))
            sp.wait_ge(rpb_out, 16 * GRID_H)
            load_bias(0, 0)
            load_bias(1, 1)
            sp.wait_ge(v_spill, 16)
            load_values(0, 0)
            load_values(1, 1)
            sp.wait_ge(v_spill, 64)
            for head in (2, 3):
                sp.wait_ge(bias_done, head - 1)
                load_bias(head, head % 2)

            def pair_loads(a, slot):
                sp.wait_ge(nv_ps, a * 3 + 3)
                load_values(a + 2, slot)
                for half in range(2):
                    sp.wait_ge(bias_done, a * 2 + (3 + half))
                    load_bias(a * 2 + (4 + half), half)
            with sp.Fori(0, 3, 1) as i:
                pair_loads(i * 2, 0)
                pair_loads(i * 2 + 1, 1)
            na_o_unit(3)
            w_up = t["l0_ffn_w_up_2"].rearrange("(k p) n -> p k n", p=P)
            w_down = t["l0_ffn_w_down_2"].rearrange("(k p) n -> p k n", p=P)
            two_layer("nup0", w_up, 0, FF)
            down_layer("ndown0", w_down, 0)
            two_layer("nup1", w_up, FH * P, FF + FH * P)
            down_layer("ndown1", w_down, FH)
            for n in range(TT):
                sp.wait_ge(out_sb, 2 * n + 2)
                sp.dma_start(out[0, n * P:n * P + P, :], out_rows[:, n, :]).then_inc(out_dma, 16)
            sp.wait_ge(out_dma, 16 * TT)

        @block.scalar
        def _(act):
            act.dma_start(cst[:, :], consts).then_inc(cst_in, 16)

            def split_w(u, s, size):
                act.wait_ge(w_dma[s], 16 * u + (32 if s == 0 else 16))
                if not isinstance(u, int) or u >= 2:
                    act.wait_ge(pe_done, u - 1)
                act.activation(whi[s][:, 0:size], raw[s][:, 0:size], ACT.Copy).then_inc(w_hi, 1)

            def next_split(name, i, s, last):
                b, _, size, after = tab[name]
                if not last or after:
                    split_w(b + i + 1, 1 - s, after if last else size)

            def norm_std(n):
                act.wait_ge(stat_ps, n + 1)
                act.activation(std, bank(7)[:, 0:4], ACT.Sqrt, bias=eps, scale=1.0 / D).then_inc(std_done, 1)

            def norm_high(n):
                norm_std(n)
                high_parts(n + 1)

            def high_parts(n, ks=range(KT)):
                for k in ks:
                    act.wait_ge(ht, KT * n + k + 1)
                    act.activation(h_hi[:, k, :], tb[k % 2][:, :], ACT.Copy).then_inc(hhi, 1)

            act.preload_act_table(ACT.Sqrt)
            act.wait_ge(cst_in, 16)
            act.activation(cstr[:, :], cst[:, 0:512], ACT.Copy).then_inc(cstr_done, 1)
            for n in range(TT):
                act.wait_ge(x_in[n], 16)
                if n:
                    act.wait_ge(ss_x, n)
                act.activation(junk[:, :], xn[:, n, :], ACT.Square, accum_out=sumsq[:, n:n + 1]).then_inc(ss_x, 1)
            act.wait_ge(ss_x, TT)
            act.activation(std0[:, 0:4], sumsq[:, 0:4], ACT.Sqrt, bias=eps, scale=1.0 / D).then_inc(std_x, 1)
            for k in range(1, KT, 2):
                act.wait_ge(xT_ps, KT * (TT - 1) + k + 1)
                act.activation(xT[:, k, :], bank(k), ACT.Copy).then_inc(xT_act, 1)
            split_w(0, 0, 2048)
            high_parts(0)

            b, n, _, _ = tab["qk"]
            for i in range(n):
                s = (b + i) % 2
                next_split("qk", i, s, i == n - 1)
                act.wait_ge(pe_done, b + i + 1)
                for m in range(2):
                    act.activation(qk_hi[:, 2 * i + m, :], bank(2 * s + m), ACT.Copy,
                                   scale=SB_DIM ** -0.5 if i < 2 else 1.0).then_inc(split_hi, 1)
            b, n, _, _ = tab["v"]
            for i in range(n):
                next_split("v", i, (b + i) % 2, i == n - 1)
            b, n, _, _ = tab["conv_in"]
            for i in range(n):
                s = (b + i) % 2
                next_split("conv_in", i, s, i == n - 1)
                act.wait_ge(pe_done, b + i + 1)
                act.activation(usb[:, i % 2, :], bank(2 * s), ACT.Copy).then_inc(usb_done, 1)
            b, n, _, _ = tab["conv_gate"]
            for i in range(n):
                next_split("conv_gate", i, (b + i) % 2, i == n - 1)
                for m in range(2):
                    act.wait_ge(ybf_done, 2 * i + m + 1)
                    act.activation(yb_hi[:, 2 * i + m, :], ybf[:, m, :], ACT.Copy).then_inc(yb_hi_done, 1)
            for n in range(TT):
                act.wait_ge(vt_ps, n + 1)
                act.activation(v_hi[:, n, :], bank(n), ACT.Copy).then_inc(vt_hi, 1)

            def sb_scores(half):
                return ps[:, 3 * half:3 * half + 3, :].rearrange("p b n -> p (b n)")[:, 0:1280]

            def sb_front(g, half):
                act.wait_ge(z_ps, g + 1)
                if not isinstance(g, int) or g >= 2:
                    act.wait_ge(wt_lo, g - 1)
                act.activation(sbT[half][:, :], sb_scores(half), ACT.Abs).then_inc(z_abs, 1)
                act.wait_ge(z_abs, g + 1)
                act.activation(sbT[half][:, :], sbT[half][:, :], ACT.Exp, scale=-1.0).then_inc(z_exp, 1)
                act.wait_ge(z_exp, g + 1)
                act.activation(sbT[half][:, :], sbT[half][:, :], ACT.Ln, bias=1.0).then_inc(z_ln, 1)

            def sb_weights(g, half):
                act.wait_ge(tri_ps, g + 1)
                act.activation(sbT[half][:, :], sb_scores(half), ACT.Exp).then_inc(wt_done, 1)

            def sb_head(i, a, half, ahead):
                if ahead == 2:
                    sb_front(i + 2, half)
                act.wait_ge(pv_ps, i + 1)
                rows = slice(64 * half, 64 * half + 64)
                act.activation(qk_hi[rows, at(a), :], ps[rows, 6 + half:7 + half, :], ACT.Copy).then_inc(o_hi_done, 1)
                if ahead:
                    sb_weights(i + 1, 1 - half)
            act.preload_act_table_set("natural_log_exp_and_others")
            sb_front(0, 0)
            sb_front(1, 1)
            sb_weights(0, 0)
            sb_heads(act, sb_head)

            act.wait_ge(pv_ps, SB_HEADS)
            for n in range(4):
                rows = t["mem" if n < 2 else "ctx_2"].rearrange("b (n p) d -> (b n) p d", p=P)
                act.dma_start(mn[:, n, :], rows[n % 2]).then_inc(mc_in[n], 16)
            b, n, _, _ = tab["gates"]

            def gates(i, s, last):
                next_split("gates", i, s, last)
                act.wait_ge(evac, b + i + 1)
                act.activation(sig[:, :, at(i), :], sig[:, :, at(i), :], ACT.Sigmoid).then_inc(sig_done, 1)
            gates(0, b % 2, False)
            for n in range(4):
                act.wait_ge(mc_in[n], 16)
                if n:
                    act.wait_ge(mc_ss, n)
                act.activation(mc_junk[:, :], mn[:, n, :], ACT.Square,
                               accum_out=sumsq[:, 4 + n:5 + n]).then_inc(mc_ss, 1)
            act.wait_ge(mc_ss, 4)
            act.activation(std0[:, 4:8], sumsq[:, 4:8], ACT.Sqrt, bias=eps, scale=1.0 / D).then_inc(mc_std, 1)
            for i in (1, 2):
                gates(i, (b + i) % 2, False)
                for k in range(4 * i - 4, 4 * i):
                    act.wait_ge(mc_T, k + 1)
                    act.activation(hm_hi[:, k, :], bank(4 + k % 4, MEM), ACT.Copy, scale=vcol(V_MKV + k)).then_inc(mc_hi, 1)
            over(act, KT - 3, b + 3, lambda i, s, last: gates(i + 3, s, last))

            b, n, _, _ = tab["branch"]
            for i in range(n):
                next_split("branch", i, (b + i) % 2, i == n - 1)
                for m in range(2):
                    act.wait_ge(mg_done, 2 * i + m + 1)
                    act.activation(h_hi[:, 2 * i + m, :], mg[:, m, :], ACT.Copy).then_inc(mg_hi, 1)

            def squares(name, per):
                act.preload_act_table(ACT.Sqrt)
                b, n, _, _ = tab[name]

                def body(i, s, last):
                    next_split(name, i, s, last)
                    act.wait_ge(evac, b + i + 1)
                    for m in range(per):
                        act.activation(sq[:, at(m if per == 2 else s, 1), :], xT[:, at(i * per + m), :],
                                       ACT.Square).then_inc(x_sq, 1)
                over(act, n, b, body)

            squares("mix", 2)
            b, n, _, _ = tab["mem_kv"]
            for i in range(n):
                s = (b + i) % 2
                if i == 1:
                    norm_std(0)
                next_split("mem_kv", i, s, i == n - 1)
                if i >= 4:
                    high_parts(1, range(2 * i - 8, 2 * i - 6))
                if i < 4:
                    act.wait_ge(pe_done, b + i + 1)
                    for m in range(2):
                        act.activation(km_hi[:, 2 * i + m, :], bank(2 * s + m, MEM), ACT.Copy).then_inc(split_hi, 1)
            for n in range(4):
                act.wait_ge(vt_ps, TT + n + 1)
                act.activation(vm_hi[:, n // 2, 512 * (n % 2):512 * (n % 2) + 512], bank(n), ACT.Copy).then_inc(vt_hi, 1)
            b, n, _, _ = tab["mem_q"]
            for i in range(n):
                s = (b + i) % 2
                next_split("mem_q", i, s, i == n - 1)
                act.wait_ge(pe_done, b + i + 1)
                for m in range(2):
                    act.activation(qm_hi[:, 2 * i + m, :], bank(2 * s + m), ACT.Copy,
                                   scale=MEM_DIM ** -0.5).then_inc(split_hi, 1)
            act.activation(silu_c, vecA[:, V_C:V_C + 16], ACT.Silu).then_inc(silu_c_done, 1)
            act.preload_act_table(ACT.Exp)

            def mem_out(g):
                for m in range(2):
                    act.wait_ge(mo_ps, 2 * g + m + 1)
                    act.activation(h_hi[:, 2 * g + m, :], bank(6 + m), ACT.Copy).then_inc(mo_hi, 1)
            def mem_exp(g):
                act.wait_ge(ms_max, g + 1)
                for n in range(TT):
                    act.activation(em[:, g % 2, n, :], ps[:, 2 * (g % 2) + n // 2, 256 * (n % 2):256 * (n % 2) + 256],
                                   ACT.Exp, bias=nmax[:, 4 * (g % 2) + n:4 * (g % 2) + n + 1],
                                   accum_out=den[:, 4 * (g % 2) + n:4 * (g % 2) + n + 1]).then_inc(ms_exp, 1)
            mem_exp(0)
            for g in range(MEM_HEADS):
                if g + 1 < MEM_HEADS:
                    mem_exp(g + 1)
                if g:
                    mem_out(g - 1)
                act.wait_ge(mp_ps, g + 1)
                act.activation(pt_hi[:, :, :], ps[:, 4:6, :], ACT.Copy).then_inc(mp_hi, 1)
            mem_out(MEM_HEADS - 1)
            squares("mem_o", 2)
            next_split("up0", 0, tab["up0"][0] % 2, False)
            norm_high(1)

            def up(name, count):
                b, n, _, _ = tab[name]

                def body(i, s, last, split=True):
                    if split:
                        next_split(name, i, s, last)
                    act.wait_ge(pe_done, b + i + 1)
                    act.activation(sg[:, at(s), :], ps[:, 2 * s:2 * s + 1, :], ACT.Silu).then_inc(silu_done, 1)
                    act.wait_ge(af_done, count + i + 1)
                    act.activation(a_hi[:, at(i), :], af[:, at(s), :], ACT.Copy).then_inc(a_hi_done, 1)
                first_apart(act, n, b, body, not count)
            up("up0", 0)
            b, n, _, _ = tab["down0"]
            over(act, n, b, lambda i, s, last: next_split("down0", i, s, last))
            up("up1", FH)
            squares("down1", 1)
            norm_std(2)
            act.wait_ge(hc_t, KT)
            act.activation(hc_hi[:, :, :], ctxT[:, :, :], ACT.Copy).then_inc(hc_h, 1)
            next_split("na_qkv", 0, tab["na_qkv"][0] % 2, False)
            for k in range(KT):
                act.wait_ge(xfin, k + 1)
                if k >= 2:
                    act.wait_ge(x_acc, (KT + 1) * 3 + k)
                act.activation(sq[:, k % 2, :], xT[:, k, :], ACT.Square).then_inc(x_sq, 1)

            def high_parts_shifted(n, shift, tb):
                for k in range(KT):
                    act.wait_ge(ht, KT * n + k + 1)
                    act.activation(h_hi[:, k, :], tb[k % 2][:, :], ACT.Identity,
                                   bias=modv[:, shift + k:shift + k + 1]).then_inc(hhi, 1)
            norm_std(3)
            high_parts_shifted(3, 0, tb3)

            def head_squares(src, j, src_c=None):
                act.activation(hsq[:, :, :], src[:, 2 * j:2 * j + 2, :], ACT.Square).then_inc(hn_sq, 1)
                if src_c is not None:
                    act.activation(hsqc[:, :, :], src_c[:, 2 * j:2 * j + 2, :], ACT.Square).then_inc(hn_sq, 1)

            def head_norm(job):
                ctx_too = job["hi_c"] is not None
                act.wait_ge(hn_ps, job["unit"] + 1)
                act.activation(hn_std[:, 0:24 if ctx_too else 16], hstat(ctx_too),
                               ACT.Sqrt, bias=eps, scale=1.0 / NA_DIM).then_inc(hn_sd, 1)
                for m in range(3 if ctx_too else 2):
                    full, high, _ = head_tiles(job, m)
                    act.wait_ge(hn_t, job["round"] + m + 1)
                    act.activation(high, full, ACT.Copy).then_inc(hn_hi, 1)
            b, n, _, _ = tab["na_qkv"]
            for i in range(n):
                s = (b + i) % 2
                if i:
                    next_split("na_qkv", i, s, i == n - 1)
                for job in head_jobs(i):
                    if job["round"]:
                        act.wait_ge(hn_lo, job["round"])
                    head_squares(job["raw"], job["j"], job["raw_c"])
                    head_norm(job)
                if i < 8:
                    act.wait_ge(evac, b + i + 1)

            def na_exp(g, tau):
                act.wait_ge(ns_max, g + 1)
                if not isinstance(g, int) or g >= 4:
                    act.wait_ge(np_ps, g - 3)
                act.activation(sc[:, tau, :], bank(tau), ACT.Exp, bias=na_nmax[:, tau:tau + 1],
                               accum_out=na_den[:, tau:tau + 1]).then_inc(ns_exp, 1)

            def na_v(buf, r, count):
                act.wait_ge(nv_ps, count)
                cols = 512 if r < 2 else 256
                act.activation(vt_h[buf][:, 4 * r:4 * r + cols // P, :].rearrange("p c n -> p (c n)"), bank(7, cols),
                               ACT.Copy).then_inc(nv_hi, 1)

            def na_out(a, half, count):
                act.wait_ge(no_ps, count)
                rows = slice(64 * half, 64 * half + 64)
                act.activation(q_hi[rows, at(a), :].rearrange("p o (r t c) -> p (o t) r c", t=4, c=16),
                               bank(6)[0:64, :].rearrange("p (t r c) -> p t r c", t=4, r=8), ACT.Copy).then_inc(no_hi, 1)

            def na_pair(a, buf, first=False, last=False):
                for st in range(8):
                    g = 8 * a + st
                    if not (last and st + 2 >= 8):
                        na_exp(g + 2, (st + 2) % 4)
                    act.wait_ge(np_ps, g + 1)
                    act.activation(np_hi[:, st % 2, :], bank(4 + st % 2), ACT.Copy).then_inc(np_h, 1)
                    if st % 4 == 0 and not (first and st == 0):
                        na_out(a if st else a - 1, 0 if st else 1, 2 * a + (1 if st else 0))
                    if st in NA_V_STEPS and not last:
                        r = NA_V_STEPS.index(st)
                        na_v(1 - buf, r, 3 * (a + 1) + r + 1)
            act.preload_act_table(ACT.Exp)
            na_exp(0, 0)
            na_exp(1, 1)
            for r in range(3):
                na_v(0, r, r + 1)
            na_pair(0, 0, first=True)
            with act.Fori(1, 7, 2) as a:
                na_pair(a, 1)
                na_pair(a + 1, 0)
            na_pair(7, 1, last=True)
            na_out(7, 1, NA_HEADS)

            squares("na_o", 2)
            next_split("nup0", 0, tab["nup0"][0] % 2, False)
            norm_std(4)
            high_parts_shifted(4, 24, tb)

            def up_conv(name, count):
                b, n, _, _ = tab[name]

                def body(i, s, last, split=True):
                    if split:
                        next_split(name, i, s, last)
                    act.wait_ge(pe_done, b + i + 1)
                    act.activation(gs[:, at(s), 1:1 + SEQ], ps[:, 2 * s + 1:2 * s + 2, :], ACT.Copy).then_inc(gs_done, 1)
                    act.wait_ge(gc_step, 3 * i + (3 * count + 3))
                    act.activation(gl[:, at(s), :], gc[:, at(s), :], ACT.Gelu, bias=vecA[:, at(i + (V_CB + count))]).then_inc(gl_done, 1)
                    act.wait_ge(gf_done, i + (count + 1))
                    act.activation(a_hi[:, at(i), :], gf[:, at(s), :], ACT.Copy).then_inc(ga_hi, 1)
                first_apart(act, n, b, body, not count)
            up_conv("nup0", 0)
            b, n, _, _ = tab["ndown0"]
            over(act, n, b, lambda i, s, last: next_split("ndown0", i, s, last))
            up_conv("nup1", FH)
            b, n, _, _ = tab["ndown1"]
            over(act, n, b, lambda i, s, last: next_split("ndown1", i, s, last))

        @block.vector
        def _(dve):
            v = nc.vector

            def split_w(u, s, size):
                dve.wait_ge(w_hi, u + 1)
                v.tensor_tensor(wlo[s][:, 0:size], raw[s][:, 0:size], whi[s][:, 0:size].bitcast(F32),
                                ALU.subtract).then_inc(w_lo, 1)

            def next_split(name, i, s, last):
                b, _, size, after = tab[name]
                if not last or after:
                    split_w(b + i + 1, 1 - s, after if last else size)

            def low(out, full, high):
                return v.tensor_tensor(out, full, high.bitcast(F32), ALU.subtract)

            def norm_apply(n, gain, ks=range(KT)):
                def lo(k):
                    dve.wait_ge(hhi, KT * n + k + 1)
                    low(h_lo[:, k, :], tb[k % 2][:, :], h_hi[:, k, :]).then_inc(hlo, 1)
                for k in ks:
                    if k >= 2:
                        dve.wait_ge(hlo, KT * n + k - 1)
                    v.scalar_tensor_tensor(tb[k % 2][:, :], xT[:, k, :], vcol(gain + k), bank(6),
                                           ALU.mult, ALU.mult).then_inc(ht, 1)
                    if k > ks[0]:
                        lo(k - 1)
                lo(ks[-1])

            def norm_rstd(n):
                dve.wait_ge(std_done, n + 1)
                v.reciprocal(rstd, std).then_inc(rstd_done, 1)

            def norm_spread(n):
                dve.wait_ge(r_ps, n + 2)

            dve.wait_ge(std_x, 1)
            v.reciprocal(rstd0[:, 0:4], std0[:, 0:4]).then_inc(rstd_x, 1)
            for k in range(0, KT, 2):
                dve.wait_ge(xT_ps, KT * (TT - 1) + k + 1)
                v.tensor_copy(xT[:, k, :], bank(k)).then_inc(xT_dve, 1)
            split_w(0, 0, 2048)
            dve.wait_ge(vec_T, 1)
            v.tensor_copy(vecA[:, 0:NA_ROWS], bank(0)[:, 0:NA_ROWS]).then_inc(vec_sb, 1)
            dve.wait_ge(vec_T, 2)
            v.tensor_copy(vecB[:, 0:NB_ROWS], bank(1)[:, 0:NB_ROWS]).then_inc(vec_sb, 1)
            dve.wait_ge(vec_sb, 2)
            dve.wait_ge(xT_dve, 4)
            dve.wait_ge(xT_act, 4)
            v.memset(cu[:, :, 0:2], 0.0).then_inc(cu_zero, 1)
            dve.wait_ge(r_ps, 1)
            norm_apply(0, V_MIX)

            b, n, _, _ = tab["qk"]
            for i in range(n):
                s = (b + i) % 2
                next_split("qk", i, s, i == n - 1)
                for m in range(2):
                    j = 2 * i + m
                    dve.wait_ge(split_hi, j + 1)
                    last = v.scalar_tensor_tensor(qk_lo[:, j, :], bank(2 * s + m), SB_DIM ** -0.5 if i < 2 else 1.0,
                                                  qk_hi[:, j, :].bitcast(F32), ALU.mult, ALU.subtract)
                last.then_inc(evac, 1)
            b, n, _, _ = tab["v"]
            for i in range(n):
                s = (b + i) % 2
                next_split("v", i, s, i == n - 1)
                dve.wait_ge(pe_done, b + i + 1)
                v.tensor_copy(vraw[:, 2 * i:2 * i + 2, :], ps[:, 2 * s:2 * s + 2, :]).then_inc(evac, 1)

            b, n, _, _ = tab["conv_in"]
            dve.wait_ge(cu_zero, 1)
            for i in range(n):
                s = (b + i) % 2
                next_split("conv_in", i, s, i == n - 1)
                c = cu[:, i % 2, :]
                dve.wait_ge(usb_done, i + 1)
                if i >= 2:
                    dve.wait_ge(conv_step, 3 * (i - 1))
                v.tensor_tensor(c[:, 2:2 + SEQ], bank(2 * s + 1), usb[:, i % 2, :], ALU.mult).then_inc(evac, 1)
                dve.wait_ge(evac, b + i + 1)
                v.tensor_scalar(cv[:, i, :], c[:, 2:2 + SEQ], vcol(V_CONV + 8 + i), None, ALU.mult).then_inc(conv_step, 1)
                for tap in (1, 0):
                    dve.wait_ge(conv_step, 3 * i + 2 - tap)
                    v.scalar_tensor_tensor(cv[:, i, :], c[:, tap:tap + SEQ], vcol(V_CONV + 4 * tap + i), cv[:, i, :],
                                           ALU.mult, ALU.add).then_inc(conv_step, 1)
            dve.wait_ge(conv_step, 12)
            b, n, _, _ = tab["conv_gate"]
            for i in range(n):
                s = (b + i) % 2
                next_split("conv_gate", i, s, i == n - 1)
                dve.wait_ge(pe_done, b + i + 1)
                if i:
                    dve.wait_ge(evac, b + i)
                for m in range(2):
                    last = v.tensor_tensor(ybf[:, m, :], bank(2 * s + m), cv[:, 2 * i + m, :], ALU.mult)
                    last.then_inc(ybf_done, 1)
                for m in range(2):
                    dve.wait_ge(yb_hi_done, 2 * i + m + 1)
                    last = low(yb_lo[:, 2 * i + m, :], ybf[:, m, :], yb_hi[:, 2 * i + m, :])
                last.then_inc(evac, 1)
            for n in range(TT):
                dve.wait_ge(vt_hi, n + 1)
                low(v_lo[:, n, :], bank(n), v_hi[:, n, :]).then_inc(vt_lo, 1)

            def sb_softplus(g, half):
                z = ps[:, 3 * half:3 * half + 3, :].rearrange("p b n -> p (b n)")[:, 0:1280]
                dve.wait_ge(z_ln, g + 1)
                v.scalar_tensor_tensor(sbS[half][:, :], z, 0.0, sbT[half][:, :], ALU.max, ALU.add).then_inc(sp_done, 1)

            def sb_split(g, half):
                if not isinstance(g, int) or g >= 2:
                    dve.wait_ge(pv_ps, g - 1)
                dve.wait_ge(sp_done, g + 1)
                v.tensor_copy(sb_hi[half][:, :], sbS[half][:, :]).then_inc(sp_hi, 1)
                dve.wait_ge(sp_hi, g + 1)
                low(sb_lo[half][:, :], sbS[half][:, :], sb_hi[half][:, :]).then_inc(sp_lo, 1)

            def sb_weights(g, half):
                dve.wait_ge(wt_done, g + 1)
                v.tensor_copy(sb_hi[half][:, :], sbT[half][:, :]).then_inc(wt_hi, 1)
                dve.wait_ge(wt_hi, g + 1)
                low(sb_lo[half][:, :], sbT[half][:, :], sb_hi[half][:, :]).then_inc(wt_lo, 1)

            def sb_head(i, a, half, ahead):
                if ahead == 2:
                    sb_softplus(i + 2, half)
                dve.wait_ge(o_hi_done, i + 1)
                rows = slice(64 * half, 64 * half + 64)
                low(qk_lo[rows, at(a), :], ps[rows, 6 + half:7 + half, :], qk_hi[rows, at(a), :]).then_inc(o_lo_done, 1)
                if ahead == 2:
                    sb_split(i + 2, half)
                if ahead:
                    sb_weights(i + 1, 1 - half)
            for g in range(2):
                sb_softplus(g, g)
                sb_split(g, g)
            sb_weights(0, 0)
            sb_heads(dve, sb_head)

            b, n, _, _ = tab["gates"]

            def gates(i, s, last):
                next_split("gates", i, s, last)
                dve.wait_ge(pe_done, b + i + 1)
                v.tensor_copy(sig[:, :, at(i), :], ps[:, 2 * s:2 * s + 2, :].rearrange("p b (o n) -> p b o n", o=1)).then_inc(evac, 1)
            gates(0, b % 2, False)
            dve.wait_ge(mc_std, 1)
            v.reciprocal(rstd0[:, 4:8], std0[:, 4:8]).then_inc(mc_rstd, 1)
            dve.wait_ge(mc_rstd, 1)
            for n in range(4):
                v.tensor_scalar(mn[:, n, :], mn[:, n, :], rstd0[:, 4 + n:5 + n], None, ALU.mult).then_inc(mc_scaled, 1)
            for i in (1, 2):
                gates(i, (b + i) % 2, False)
                for k in range(4 * i - 4, 4 * i):
                    dve.wait_ge(mc_hi, k + 1)
                    v.scalar_tensor_tensor(hm_lo[:, k, :], bank(4 + k % 4, MEM), vcol(V_MKV + k), hm_hi[:, k, :].bitcast(F32),
                                           ALU.mult, ALU.subtract)
                    v.tensor_copy(ctxT[:, k, :], ps[:, 4 + k % 4, 256:512]).then_inc(mc_lo, 1)
            over(dve, KT - 3, b + 3, lambda i, s, last: gates(i + 3, s, last))

            b, n, _, _ = tab["branch"]
            dve.wait_ge(sig_done, KT)
            for i in range(n):
                s = (b + i) % 2
                next_split("branch", i, s, i == n - 1)
                dve.wait_ge(pe_done, b + i + 1)
                if i:
                    dve.wait_ge(evac, b + i)
                for m in range(2):
                    j = 2 * i + m
                    v.tensor_tensor(mg[:, m, :], bank(2 * s + m), sig[:, 0, j, :], ALU.mult)
                    last = v.tensor_tensor(mt[:, m, :], bank(4 + 2 * s + m), sig[:, 1, j, :], ALU.mult)
                    last.then_inc(br_step, 1)
                for m in range(2):
                    j = 2 * i + m
                    dve.wait_ge(br_step, j + 1)
                    v.tensor_tensor(mg[:, m, :], mg[:, m, :], mt[:, m, :], ALU.add).then_inc(mg_done, 1)
                for m in range(2):
                    j = 2 * i + m
                    dve.wait_ge(mg_hi, j + 1)
                    last = low(h_lo[:, j, :], mg[:, m, :], h_hi[:, j, :])
                last.then_inc(evac, 1)

            def update(name, per, norm=None, gate=None):
                b, n, _, _ = tab[name]

                def body(i, s, last):
                    next_split(name, i, s, last)
                    dve.wait_ge(pe_done, b + i + 1)
                    for m in range(per):
                        x = xT[:, at(i * per + m), :]
                        y = ps[:, 2 * s + m:2 * s + m + 1, :]
                        if gate is None:
                            r = v.tensor_tensor(x, x, y, ALU.add)
                        else:
                            r = v.scalar_tensor_tensor(x, y, modv[:, at(i * per + (gate + m))], x, ALU.mult, ALU.add)
                    r.then_inc(evac, 1)
                    for m in range(0 if norm is None else per):
                        dve.wait_ge(x_sq, i * per + (KT * norm + m + 1))
                        dve.wait_ge(x_acc, i * per + ((KT + 1) * norm + m + 1))
                        v.tensor_tensor(sqacc[:, :], sqacc[:, :], sq[:, m if per == 2 else s, :], ALU.add).then_inc(x_acc, 1)
                if norm is not None:
                    v.memset(sqacc[:, :], 0.0).then_inc(x_acc, 1)
                over(dve, n, b, body)
            update("mix", 2, 0)

            b, n, _, _ = tab["mem_kv"]
            for i in range(n):
                s = (b + i) % 2
                if i == 2:
                    norm_rstd(0)
                if i == 4:
                    norm_spread(0)
                next_split("mem_kv", i, s, i == n - 1)
                if i >= 4:
                    norm_apply(1, V_MQ, range(2 * i - 8, 2 * i - 6))
                if i < 4:
                    for m in range(2):
                        j = 2 * i + m
                        dve.wait_ge(split_hi, 8 + j + 1)
                        last = low(km_lo[:, j, :], bank(2 * s + m, MEM), km_hi[:, j, :])
                    last.then_inc(evac, 1)
                else:
                    dve.wait_ge(pe_done, b + i + 1)
                    v.tensor_copy(vmraw[:, 2 * i - 8:2 * i - 6, :], ps[:, 2 * s:2 * s + 2, 0:MEM]).then_inc(evac, 1)
            for n in range(4):
                dve.wait_ge(vt_hi, TT + n + 1)
                low(vm_lo[:, n // 2, 512 * (n % 2):512 * (n % 2) + 512], bank(n),
                    vm_hi[:, n // 2, 512 * (n % 2):512 * (n % 2) + 512]).then_inc(vt_lo, 1)
            b, n, _, _ = tab["mem_q"]
            for i in range(n):
                s = (b + i) % 2
                next_split("mem_q", i, s, i == n - 1)
                for m in range(2):
                    j = 2 * i + m
                    dve.wait_ge(split_hi, 16 + j + 1)
                    last = v.scalar_tensor_tensor(qm_lo[:, j, :], bank(2 * s + m), MEM_DIM ** -0.5,
                                                  qm_hi[:, j, :].bitcast(F32), ALU.mult, ALU.subtract)
                last.then_inc(evac, 1)
            def mem_max(g):
                dve.wait_ge(ms_ps, g + 1)
                if g >= 2:
                    dve.wait_ge(ms_exp, TT * (g - 1))
                v.tensor_reduce(nmax[:, 4 * (g % 2):4 * (g % 2) + 4],
                                ps[:, 2 * (g % 2):2 * (g % 2) + 2, :].rearrange("p b (o n) -> p (b o) n", o=2),
                                AX.X, ALU.max, negate=True).then_inc(ms_max, 1)

            def mem_out(g):
                for m in range(2):
                    dve.wait_ge(mo_hi, 2 * g + m + 1)
                    low(h_lo[:, 2 * g + m, :], bank(6 + m), h_hi[:, 2 * g + m, :]).then_inc(mo_lo, 1)
            def mem_norm(g):
                dve.wait_ge(ms_exp, TT * (g + 1))
                cols = slice(4 * (g % 2), 4 * (g % 2) + 4)
                v.reciprocal(rden[:, cols], den[:, cols]).then_inc(ms_rden, 1)
                dve.wait_ge(ms_rden, g + 1)
                for n in range(TT):
                    v.tensor_scalar(em[:, g % 2, n, :], em[:, g % 2, n, :],
                                    rden[:, 4 * (g % 2) + n:4 * (g % 2) + n + 1], None, ALU.mult).then_inc(ms_norm, 1)
            mem_max(0)
            mem_norm(0)
            for g in range(MEM_HEADS):
                if g + 1 < MEM_HEADS:
                    mem_max(g + 1)
                    mem_norm(g + 1)
                if g:
                    mem_out(g - 1)
                dve.wait_ge(mp_hi, g + 1)
                low(pt_lo[:, :, :], ps[:, 4:6, :], pt_hi[:, :, :]).then_inc(mp_lo, 1)
            mem_out(MEM_HEADS - 1)
            update("mem_o", 2, 1)
            next_split("up0", 0, tab["up0"][0] % 2, False)
            norm_rstd(1)
            norm_spread(1)
            norm_apply(2, V_FFN)

            def up(name, count):
                b, n, _, _ = tab[name]

                def body(i, s, last, split=True):
                    if split:
                        next_split(name, i, s, last)
                    dve.wait_ge(silu_done, count + i + 1)
                    v.tensor_tensor(af[:, at(s), :], ps[:, 2 * s + 1:2 * s + 2, :], sg[:, at(s), :], ALU.mult).then_inc(af_done, 1)
                    dve.wait_ge(a_hi_done, count + i + 1)
                    low(a_lo[:, at(i), :], af[:, at(s), :], a_hi[:, at(i), :]).then_inc(evac, 1)
                first_apart(dve, n, b, body, not count)
            up("up0", 0)
            update("down0", 1)
            up("up1", FH)
            dve.wait_ge(mod_ps, 4)
            v.tensor_tensor(modv[:, 0:48], bank(5)[:, 0:48], vecB[:, V_BMOD:V_BMOD + 48], ALU.add).then_inc(mod_sb, 1)
            v.tensor_tensor(modv[:, 48:64], bank(5)[:, 48:64], vecB[:, V_BMOD:V_BMOD + 16], ALU.add).then_inc(mod_sb, 1)
            v.tensor_scalar(qgain, vcol(V_QG), NA_DIM ** -0.5, None, ALU.mult).then_inc(mod_sb, 1)
            dve.wait_ge(mod_sb, 3)
            for o, scale, gain in ((gain1, 8, V_N1), (gain2, 32, V_N2), (gain1c, 56, V_N1)):
                v.scalar_tensor_tensor(o, modv[:, scale:scale + 8], 1.0, vecA[:, gain:gain + 8], ALU.add, ALU.mult).then_inc(mod_vec, 1)
            dve.wait_ge(mod_vec, 3)
            for k in range(KT):
                v.tensor_scalar(ctxT[:, k, :], ctxT[:, k, :], gain1c[:, k:k + 1], modv[:, 48 + k:49 + k],
                                ALU.mult, ALU.add).then_inc(hc_t, 1)
            update("down1", 1, 2)
            norm_rstd(2)
            dve.wait_ge(hc_h, 1)
            low(hc_lo[:, :, :], ctxT[:, :, :], hc_hi[:, :, :]).then_inc(hc_l, 1)
            v.memset(sqacc[:, :], 0.0).then_inc(x_acc, 1)
            norm_spread(2)

            def take_squares(k):
                dve.wait_ge(x_sq, KT * 3 + k + 1)
                dve.wait_ge(x_acc, (KT + 1) * 3 + k + 1)
                v.tensor_tensor(sqacc[:, :], sqacc[:, :], sq[:, k % 2, :], ALU.add).then_inc(x_acc, 1)
            for k in range(KT):
                v.scalar_tensor_tensor(xT[:, k, :], xT[:, k, :], vcol(V_FIN + k), bank(6), ALU.mult, ALU.mult).then_inc(xfin, 1)
                if k:
                    take_squares(k - 1)
            take_squares(KT - 1)
            norm_rstd(3)
            next_split("na_qkv", 0, tab["na_qkv"][0] % 2, False)
            norm_spread(3)

            def norm_apply_shifted(n, gain, shift, tb):
                def lo(k):
                    dve.wait_ge(hhi, KT * n + k + 1)
                    v.scalar_tensor_tensor(h_lo[:, k, :], tb[k % 2][:, :], modv[:, shift + k:shift + k + 1],
                                           h_hi[:, k, :].bitcast(F32), ALU.add, ALU.subtract).then_inc(hlo, 1)
                for k in range(KT):
                    if k >= 2:
                        dve.wait_ge(hlo, KT * n + k - 1)
                    v.scalar_tensor_tensor(tb[k % 2][:, :], xT[:, k, :], gain[:, k:k + 1], bank(6),
                                           ALU.mult, ALU.mult).then_inc(ht, 1)
                    if k:
                        lo(k - 1)
                lo(KT - 1)
            norm_apply_shifted(3, gain1, 0, tb3)

            def head_norm(i, job):
                cols = 24 if job["hi_c"] is not None else 16
                dve.wait_ge(hn_sd, job["unit"] + 1)
                v.reciprocal(hn_rstd[:, 0:cols], hn_std[:, 0:cols]).then_inc(hn_rd, 1)
                gain = qgain if job["hi_c"] is None else vcol(V_KG)
                j = job["j"]
                dve.wait_ge(hn_rd, job["unit"] + 1)
                j, r, n = job["j"], job["round"], 3 if job["hi_c"] is not None else 2

                def expand(m):
                    v.tensor_copy(rexp[m % 2][:, :, :], hn_rstd[:, 8 * m:8 * m + 8].rearrange("p (h o) -> p h o", o=1)
                                  .to_broadcast([P, 8, 64])).then_inc(hn_x, 1)

                def apply(m):
                    dve.wait_ge(hn_r, r + m + 1)
                    y = bank(head_bank(i, m))
                    if m == 2:
                        x = job["raw_c"][:, 2 * j:2 * j + 2, :]
                        y, out = y.rearrange("p (a n) -> p a n", a=2), x
                    else:
                        x = job["raw"][:, 2 * j + m, :]
                        out = x if job["tmp"] is None else job["tmp"][:, m, :]
                    v.scalar_tensor_tensor(out, x, gain, y, ALU.mult, ALU.mult).then_inc(hn_t, 1)

                def lower(m):
                    full, high, lo = head_tiles(job, m)
                    dve.wait_ge(hn_hi, r + m + 1)
                    low(lo, full, high).then_inc(hn_lo, 1)
                expand(0)
                expand(1)
                if n == 3:
                    dve.wait_ge(hn_r, r + 1)
                    expand(2)
                apply(0)
                apply(1)
                lower(0)
                if n == 3:
                    apply(2)
                lower(1)
                if n == 3:
                    lower(2)
            b, n, _, _ = tab["na_qkv"]
            for i in range(n):
                s = (b + i) % 2
                if i:
                    next_split("na_qkv", i, s, i == n - 1)
                for job in head_jobs(i):
                    head_norm(i, job)
                dve.wait_ge(pe_done, b + i + 1)
                x_banks = ps[:, 2 * s:2 * s + 2, :]
                c_bank = bank(4 + s).rearrange("p (a n) -> p a n", a=2)
                j = 2 * (i % 4)
                if i >= 8:
                    if i == 8:
                        dve.wait_ge(hn_lo, 20)
                    else:
                        dve.wait_ge(v_spill, 16 * (i - 8))
                    v.tensor_copy(v_out[:, :, 0:SEQ], x_banks)
                    v.tensor_copy(v_out[:, :, SEQ:SEQ + CTX], c_bank).then_inc(evac, 1)
                elif i < 4:
                    v.tensor_copy(k_raw[:, j:j + 2, :], x_banks)
                    v.tensor_copy(kc_raw[:, j:j + 2, :], c_bank).then_inc(evac, 1)
                else:
                    v.tensor_copy(q_raw[:, j:j + 2, :], x_banks).then_inc(evac, 1)

            def na_den_step(g, tau):
                dve.wait_ge(ns_exp, g + 1)
                v.reciprocal(na_rden[:, tau:tau + 1], na_den[:, tau:tau + 1]).then_inc(ns_rden, 1)

            def na_v(buf, r, count):
                dve.wait_ge(nv_hi, count)
                cols = 512 if r < 2 else 256
                low(vt_l[buf][:, 4 * r:4 * r + cols // P, :].rearrange("p c n -> p (c n)"), bank(7, cols),
                    vt_h[buf][:, 4 * r:4 * r + cols // P, :].rearrange("p c n -> p (c n)")).then_inc(nv_lo, 1)

            def na_out(a, half, count):
                dve.wait_ge(no_hi, count)
                rows = slice(64 * half, 64 * half + 64)
                v.tensor_tensor(q_lo[rows, at(a), :].rearrange("p o (r t c) -> p (o t) r c", t=4, c=16),
                                bank(6)[0:64, :].rearrange("p (t r c) -> p t r c", t=4, r=8),
                                q_hi[rows, at(a), :].bitcast(F32).rearrange("p o (r t c) -> p (o t) r c", t=4, c=16),
                                ALU.subtract).then_inc(no_lo, 1)

            def na_pair(a, buf, first=False, last=False):
                for st in range(8):
                    g = 8 * a + st
                    if not (last and st + 1 >= 8):
                        na_den_step(g + 1, (st + 1) % 4)
                    if not (last and st + 3 >= 8):
                        head = (st + 3) // 4
                        na_max_step_in(a, st + 3, head % 2)
                    dve.wait_ge(np_h, g + 1)
                    low(np_lo[:, st % 2, :], bank(4 + st % 2), np_hi[:, st % 2, :]).then_inc(np_l, 1)
                    if st % 4 == 0 and not (first and st == 0):
                        na_out(a if st else a - 1, 0 if st else 1, 2 * a + (1 if st else 0))
                    if st in NA_V_STEPS and not last:
                        r = NA_V_STEPS.index(st)
                        na_v(1 - buf, r, 3 * (a + 1) + r + 1)

            def na_max_step_in(a, st, b):
                g, tau = 8 * a + st, st % 4
                dve.wait_ge(ns_ps, g + 1)
                if tau == 0:
                    dve.wait_ge(bias_done, 2 * a + st // 4 + 1)
                v.tensor_reduce(na_nmax_c[:, tau:tau + 1], ps[:, tau, 256:512], AX.X, ALU.max, negate=True)
                v.tensor_tensor_reduce(out=ps[:, tau, 0:256], in0=ps[:, tau, 0:256],
                                       in1=bias[b][:, (0, 1, 1, 2)[tau], :, :].rearrange("p i j -> p (i j)"),
                                       scale=1.0, scalar=-3.0e38, op0=ALU.add, op1=ALU.max,
                                       accum_out=na_max[:, tau:tau + 1]).then_inc(ns_red, 1)
                dve.wait_ge(ns_red, g + 1)
                v.scalar_tensor_tensor(na_nmax[:, tau:tau + 1], na_max[:, tau:tau + 1], -1.0, na_nmax_c[:, tau:tau + 1],
                                       ALU.mult, ALU.min).then_inc(ns_max, 1)
            for st in range(3):
                na_max_step_in(0, st, 0)
            na_den_step(0, 0)
            dve.wait_ge(vp_in[0], 16)
            for tau in range(TT):
                v.tensor_copy(vw_first[:, tau, :, :], grid(vp[0][:, 0:SEQ])[:, :, span[tau]:span[tau] + 32]).then_inc(vw_done, 1)
            for r in range(3):
                na_v(0, r, r + 1)
            dve.wait_ge(v_spill, 64)
            na_pair(0, 0, first=True)
            with dve.Fori(1, 7, 2) as a:
                na_pair(a, 1)
                na_pair(a + 1, 0)
            na_pair(7, 1, last=True)
            na_out(7, 1, NA_HEADS)

            update("na_o", 2, 4, gate=16)
            next_split("nup0", 0, tab["nup0"][0] % 2, False)
            v.memset(gs[:, :, 0:1], 0.0).then_inc(gs_zero, 1)
            v.memset(gs[:, :, SEQ + 1:SEQ + 2], 0.0).then_inc(gs_zero, 1)
            norm_rstd(4)
            norm_spread(4)
            norm_apply_shifted(4, gain2, 24, tb)
            dve.wait_ge(gs_zero, 2)

            def up_conv(name, count):
                b, n, _, _ = tab[name]

                def body(i, s, last, split=True):
                    if split:
                        next_split(name, i, s, last)
                    g = gs[:, at(s), :]
                    c = gc[:, at(s), :]
                    dve.wait_ge(gs_done, i + (count + 1))
                    v.tensor_scalar(c, g[:, :, 0:SEQ], vecB[:, at(i + (V_CW + count))], None, ALU.mult).then_inc(gc_step, 1)
                    for tap in (1, 2):
                        dve.wait_ge(gc_step, 3 * i + (3 * count + tap))
                        v.scalar_tensor_tensor(c, g[:, :, tap:tap + SEQ], vecB[:, at(i + (V_CW + count + FT * tap))], c,
                                               ALU.mult, ALU.add).then_inc(gc_step, 1)
                    dve.wait_ge(gl_done, i + (count + 1))
                    v.tensor_tensor(gf[:, at(s), :], ps[:, 2 * s:2 * s + 1, :], gl[:, at(s), :], ALU.mult).then_inc(gf_done, 1)
                    dve.wait_ge(ga_hi, i + (count + 1))
                    low(a_lo[:, at(i), :], gf[:, at(s), :], a_hi[:, at(i), :]).then_inc(evac, 1)
                first_apart(dve, n, b, body, not count)
            up_conv("nup0", 0)
            update("ndown0", 1, gate=40)
            up_conv("nup1", FH)
            update("ndown1", 1, gate=40)
            for n in range(2 * TT):
                dve.wait_ge(out_T, n + 1)
                v.tensor_copy(out_rows[:, n // 2, 512 * (n % 2):512 * (n % 2) + 512], bank(n)).then_inc(out_sb, 1)

        @block.tensor
        def _(pe):
            mm = nc.tensor.matmul

            def product(o, w_h, w_l, x_h, x_l, first, last, **kw):
                mm(o, w_h, x_h, start=first, stop=False, **kw)
                mm(o, w_h, x_l, start=False, stop=False, **kw)
                return mm(o, w_l, x_h, start=False, stop=last, **kw)

            def unit(u):
                pe.wait_ge(w_lo, u + 1)
                if not isinstance(u, int) or u >= 2:
                    pe.wait_ge(evac, u - 1)

            def pair_unit(u, s, x_h, x_l, cols=SEQ, arrive=None):
                unit(u)
                for k in range(KT):
                    if arrive:
                        arrive(k)
                    for m in range(2):
                        w = slice(256 * k + 128 * m, 256 * k + 128 * m + 128)
                        last = product(bank(2 * s + m, cols), whi[s][:, w], wlo[s][:, w], x_h[:, k, :], x_l[:, k, :],
                                       k == 0, k == KT - 1)
                last.then_inc(pe_done, 1)

            def pair_layer(name, x_h, x_l, cols=SEQ, arrive=None, after_two=None):
                b, n, _, _ = tab[name]
                if arrive:
                    pair_unit(b, b % 2, x_h, x_l, cols, arrive)
                    if after_two:
                        pair_unit(b + 1, (b + 1) % 2, x_h, x_l, cols)
                        after_two()
                        over(pe, n - 2, b + 2, lambda i, s, last: pair_unit(b + 2 + i, s, x_h, x_l, cols))
                        return
                    if n <= 4:
                        for i in range(1, n):
                            pair_unit(b + i, (b + i) % 2, x_h, x_l, cols)
                    else:
                        over(pe, n - 1, b + 1, lambda i, s, last: pair_unit(b + 1 + i, s, x_h, x_l, cols))
                else:
                    over(pe, n, b, lambda i, s, last: pair_unit(b + i, s, x_h, x_l, cols))

            def down_layer(name, source):
                b, n, _, _ = tab[name]

                def body(i, s, last, follow=False):
                    unit(b + i)
                    for k in range(FH):
                        if follow:
                            pe.wait_ge(evac, tab[source][0] + k + 1)
                        w = slice(128 * k, 128 * k + 128)
                        r = product(bank(2 * s), whi[s][:, w], wlo[s][:, w], a_hi[:, k, :], a_lo[:, k, :],
                                    k == 0, k == FH - 1)
                    r.then_inc(pe_done, 1)
                body(0, b % 2, False, follow=True)
                over(pe, n - 1, b + 1, lambda i, s, last: body(i + 1, s, last))

            def norm_stats(n, acc):
                pe.wait_ge(x_acc, acc)
                for q in range(TT):
                    last = mm(bank(7)[:, q:q + 1], sqacc[:, q * P:q * P + P], one, start=True, stop=True)
                last.then_inc(stat_ps, 1)

            def norm_spread(n):
                pe.wait_ge(rstd_done, n + 1)
                for q in range(TT):
                    last = nc.tensor.transpose(bank(6)[:, q * P:q * P + P], rstd[:, q:q + 1].to_broadcast([P, P]), ident)
                last.then_inc(r_ps, 1)

            def mod_group(group):
                first, cols, both = MOD_GROUPS[group]
                pe.wait_ge(mod_step, 32 * (group + 1))
                for j in range(cols // P):
                    o = first // P + j
                    last = mm(bank(5)[:, o:o + 1], mod_acc[group % 2][:, j * P:j * P + P], one, start=True, stop=True)
                    if both:
                        last = mm(bank(5)[:, 48 + o:49 + o], mod_acc[group % 2][:, 1024 + j * P:1024 + j * P + P], one, start=True, stop=True)
                last.then_inc(mod_ps, 1)

            pe.wait_ge(cst_in, 16)
            for n in range(TT):
                pe.wait_ge(x_in[n], 16)
                for k in range(KT):
                    nc.tensor.transpose(bank(k)[:, n * P:n * P + P], xn[:, n, k * P:k * P + P], ident).then_inc(xT_ps, 1)
            pe.wait_ge(rstd_x, 1)
            pe.wait_ge(xT_dve, 4)
            for q in range(TT):
                last = nc.tensor.transpose(bank(6)[:, q * P:q * P + P], rstd0[:, q:q + 1].to_broadcast([P, P]), ident)
            last.then_inc(r_ps, 1)
            pe.wait_ge(xT_act, 4)
            pe.wait_ge(vec_in, 16 * 17)
            nc.tensor.transpose(bank(0)[:, 0:NA_ROWS], rowsA[0:NA_ROWS, :], ident[0:NA_ROWS, 0:NA_ROWS]).then_inc(vec_T, 1)
            nc.tensor.transpose(bank(1)[:, 0:NB_ROWS], rowsB[0:NB_ROWS, :], ident[0:NB_ROWS, 0:NB_ROWS]).then_inc(vec_T, 1)
            pe.wait_ge(vec_sb, 2)

            pair_layer("qk", h_hi, h_lo, arrive=lambda k: pe.wait_ge(hlo, k + 1))
            pair_layer("v", h_hi, h_lo)
            pair_layer("conv_in", h_hi, h_lo)
            pair_layer("conv_gate", h_hi, h_lo)

            b, n, _, _ = tab["conv_gate"]
            pe.wait_ge(evac, b + n)
            for n in range(TT):
                for j in range(4):
                    last = nc.tensor.transpose(bank(n)[:, j * P:j * P + P], vraw[:, j, n * P:n * P + P], ident)
                last.then_inc(vt_ps, 1)
            pe.wait_ge(vt_lo, TT)
            pe.wait_ge(cstr_done, 1)

            zat = [0, 512, 1024, 896]
            zlen = [512, 384, 256, 128]

            def score(a, half):
                z = ps[:, 3 * half:3 * half + 3, :].rearrange("p b n -> p (b n)")
                rows = slice(64 * half, 64 * half + 64)
                for n in (0, 1, 3, 2):
                    o = z[:, zat[n]:zat[n] + zlen[n]]
                    q_h, q_l = (x[rows, at(a), n * P:SEQ] for x in (qk_hi, qk_lo))
                    k_h, k_l = (x[rows, at(a + 4), n * P:n * P + P] for x in (qk_hi, qk_lo))
                    mm(o, k_h, q_h, start=n != 3, stop=False, skip_group_check=True)
                    mm(o, k_h, q_l, start=False, stop=False, skip_group_check=True)
                    mm(o, k_l, q_h, start=False, stop=False, skip_group_check=True)
                for n in (0, 1, 3, 2):
                    last = mm(z[:, zat[n]:zat[n] + P], r_ident, r_mask, start=False, stop=False, skip_group_check=True)
                last.then_inc(z_ps, 1)

            def later(half, g):
                z = ps[:, 3 * half:3 * half + 3, :].rearrange("p b n -> p (b n)")
                pe.wait_ge(sp_lo, g)
                for n in (0, 1, 3, 2):
                    for s in (sb_hi[half], sb_lo[half]):
                        for j in range(n, TT):
                            w = r_tri if j == n else r_ones
                            last = mm(z[:, zat[n] + (j - n) * P:zat[n] + zlen[n]], w, s[:, zat[j]:zat[j] + zlen[j]],
                                      start=False, stop=j == TT - 1, skip_group_check=True)
                last.then_inc(tri_ps, 1)

            def values(a, half, g):
                pe.wait_ge(wt_lo, g)
                for n in range(TT):
                    w = [x[:, n, at(a * P, P)] for x in (v_hi, v_lo)]
                    x = [s[half][:, zat[n]:zat[n] + zlen[n]] for s in (sb_hi, sb_lo)]
                    last = product(bank(6 + half)[:, n * P:SEQ], w[0], w[1], x[0], x[1], n == 0, n == TT - 1)
                last.then_inc(pv_ps, 1)

            score(0, 0)
            score(0, 1)
            later(0, 1)
            for i in range(SB_HEADS):
                a, half = divmod(i, 2)
                if i + 2 < SB_HEADS:
                    pe.wait_ge(wt_done, i + 1)
                    score(a + 1, half)
                if i >= 2:
                    pe.wait_ge(o_lo_done, i - 1)
                values(a, half, i + 1)
                if i + 1 < SB_HEADS:
                    later(1 - half, i + 2)

            b, n, _, _ = tab["gates"]
            for i in range(3):
                if i == 0:
                    pe.wait_ge(wt_done, SB_HEADS)
                pair_unit(b + i, (b + i) % 2, h_hi, h_lo)
                if i == 1:
                    pe.wait_ge(mc_scaled, 4)
                    pe.wait_ge(o_lo_done, SB_HEADS)
                for k in range(4 * i - 4, 4 * i) if i else ():
                    if k >= 4:
                        pe.wait_ge(mc_lo, k - 3)
                    for n in range(4):
                        last = nc.tensor.transpose(bank(4 + k % 4)[:, n * P:n * P + P], mn[:, n, k * P:k * P + P], ident)
                    last.then_inc(mc_T, 1)
            over(pe, KT - 3, b + 3, lambda i, s, last: pair_unit(b + 3 + i, s, h_hi, h_lo))

            b, n, _, _ = tab["branch"]
            pe.wait_ge(o_lo_done, SB_HEADS)
            for i in range(n):
                s = (b + i) % 2
                unit(b + i)
                for m in range(2):
                    for br, (x_h, x_l) in enumerate(((qk_hi, qk_lo), (yb_hi, yb_lo))):
                        for k in range(4):
                            w = slice(256 * (4 * br + k) + 128 * m, 256 * (4 * br + k) + 128 * m + 128)
                            last = product(bank(4 * br + 2 * s + m), whi[s][:, w], wlo[s][:, w], x_h[:, k, :], x_l[:, k, :],
                                           k == 0, k == 3)
                last.then_inc(pe_done, 1)
            pair_layer("mix", h_hi, h_lo, arrive=lambda k: pe.wait_ge(evac, tab["branch"][0] + k // 2 + 1))

            b, n, _, _ = tab["mem_kv"]
            for i in range(n):
                pair_unit(b + i, (b + i) % 2, hm_hi, hm_lo, MEM)
                if i == 0:
                    norm_stats(0, 9)
                if i == 2:
                    norm_spread(0)
            pe.wait_ge(evac, b + n)
            for n in range(4):
                for j in range(4):
                    f = 4 * (n % 2) + j
                    last = nc.tensor.transpose(bank(n)[:, j * P:j * P + P], vmraw[:, f, P * (n // 2):P * (n // 2) + P], ident)
                last.then_inc(vt_ps, 1)
            pe.wait_ge(vt_lo, TT + 4)
            pair_layer("mem_q", h_hi, h_lo, arrive=lambda k: pe.wait_ge(hlo, KT + k + 1))
            b, n, _, _ = tab["mem_q"]
            pe.wait_ge(evac, b + n)

            def mem_scores(g):
                if g >= 2:
                    pe.wait_ge(ms_exp, TT * (g - 1))
                for n in range(TT):
                    for k in range(2):
                        f = 2 * g + k
                        q = [x[:, f, n * P:n * P + P] for x in (qm_hi, qm_lo)]
                        c = [x[:, f, :] for x in (km_hi, km_lo)]
                        last = product(ps[:, 2 * (g % 2) + n // 2, 256 * (n % 2):256 * (n % 2) + 256], q[0], q[1], c[0], c[1],
                                       k == 0, k == 1)
                last.then_inc(ms_ps, 1)

            def mem_values(g):
                pe.wait_ge(mp_lo, g + 1)
                if g:
                    pe.wait_ge(mo_lo, 2 * g)
                for m in range(2):
                    for c in range(2):
                        w = [x[:, c, g * 256 + m * P:g * 256 + m * P + P] for x in (vm_hi, vm_lo)]
                        last = product(bank(6 + m), w[0], w[1], pt_hi[:, c, :], pt_lo[:, c, :], c == 0, c == 1)
                    last.then_inc(mo_ps, 1)

            mem_scores(0)
            mem_scores(1)
            for g in range(MEM_HEADS):
                pe.wait_ge(ms_norm, TT * (g + 1))
                if g:
                    pe.wait_ge(mp_lo, g)
                for c in range(2):
                    for n in range(TT):
                        last = nc.tensor.transpose(bank(4 + c)[:, n * P:n * P + P], em[:, g % 2, n, c * P:c * P + P], ident)
                last.then_inc(mp_ps, 1)
                if g:
                    mem_values(g - 1)
                if g + 2 < MEM_HEADS:
                    mem_scores(g + 2)
            mem_values(MEM_HEADS - 1)
            pair_layer("mem_o", h_hi, h_lo, arrive=lambda k: pe.wait_ge(mo_lo, k + 1))
            norm_stats(1, 18)
            norm_spread(1)
            pair_layer("up0", h_hi, h_lo, arrive=lambda k: pe.wait_ge(hlo, 2 * KT + k + 1), after_two=lambda: mod_group(0))
            mod_group(1)
            down_layer("down0", "up0")
            pair_layer("up1", h_hi, h_lo)
            mod_group(2)
            mod_group(3)
            down_layer("down1", "up1")
            norm_stats(2, 27)
            norm_spread(2)

            def context_part(u, s):
                unit(u)
                for m in range(2):
                    for k in range(KT):
                        w = slice(256 * k + 128 * m, 256 * k + 128 * m + 128)
                        last = product(bank(4 + s)[:, 256 * m:256 * m + 256], whi[s][:, w], wlo[s][:, w],
                                       hc_hi[:, k, :], hc_lo[:, k, :], k == 0, k == KT - 1)
                return last

            b = tab["na_qkv"][0]
            pe.wait_ge(hc_l, 1)
            context_part(b, b % 2)
            norm_stats(3, 36)
            norm_spread(3)
            context_part(b + 1, (b + 1) % 2)

            def head_stats(job):
                ctx_too = job["hi_c"] is not None
                pe.wait_ge(hn_sq, hn_sq_count(job))
                pairs_of = cst[:, C_HEADS:C_HEADS + 2]
                for m in range(2):
                    for q in range(TT):
                        last = mm(bank(6)[:, 8 * m + 2 * q:8 * m + 2 * q + 2], hsq[:, m, q * P:q * P + P], pairs_of,
                                  start=True, stop=True)
                for m in range(2 if ctx_too else 0):
                    for q in range(2):
                        last = mm(bank(6)[:, 16 + 4 * m + 2 * q:18 + 4 * m + 2 * q], hsqc[:, m, q * P:q * P + P], pairs_of,
                                  start=True, stop=True)
                last.then_inc(hn_ps, 1)

            def hn_sq_count(job):
                return 2 * (job["unit"] + 1) if job["unit"] < 4 else 8 + job["unit"] - 3

            def head_spread(i, job, m):
                r = job["round"] + m
                pe.wait_ge(hn_x, r + 1)
                if m == 2:
                    pe.wait_ge(hn_t, r - 1)
                if m == 1:
                    pe.wait_ge(evac, tab["na_qkv"][0] + i)
                for q in range(TT):
                    last = nc.tensor.transpose(bank(head_bank(i, m))[:, q * P:q * P + P],
                                               rexp[m % 2][:, 2 * q:2 * q + 2, :].rearrange("p h n -> p (h n)"), ident)
                last.then_inc(hn_r, 1)

            b, n, _, _ = tab["na_qkv"]
            for i in range(n):
                s = (b + i) % 2
                unit(b + i)
                job = (head_jobs(i) or [None])[0]
                for k in range(KT):
                    if i == 0:
                        pe.wait_ge(hlo, 3 * KT + k + 1)
                    for m in range(2):
                        w = slice(256 * k + 128 * m, 256 * k + 128 * m + 128)
                        last = product(bank(2 * s + m), whi[s][:, w], wlo[s][:, w], h_hi[:, k, :], h_lo[:, k, :],
                                       k == 0, k == KT - 1)
                    if job and k == 5:
                        head_stats(job)
                    if job and k == 7:
                        head_spread(i, job, 0)
                        head_spread(i, job, 1)
                if i in (2, 3):
                    pe.wait_ge(hn_t, 3 * (i - 2) + 2)
                    last = context_part(b + i, s)
                if job and job["hi_c"] is not None:
                    head_spread(i, job, 2)
                if i >= 8:
                    if i == 9:
                        pe.wait_ge(hn_t, 20)
                    last = context_part(b + i, s)
                last.then_inc(pe_done, 1)
            pe.wait_ge(hn_lo, 20)
            pe.wait_ge(evac, b + n)

            def na_scores(g):
                head, tau = divmod(g, 4)
                a, rows = head // 2, slice(64 * (head % 2), 64 * (head % 2) + 64)
                if g >= 4:
                    pe.wait_ge(ns_exp, g - 3)
                q = [x[rows, a, P * tau:P * tau + P] for x in (q_hi, q_lo)]
                k = [grid(x[rows, a, :])[:, :, span[tau]:span[tau] + 32] for x in (k_hi, k_lo)]
                c = [x[rows, a, :] for x in (kc_hi, kc_lo)]
                product(bank(tau, 256), q[0], q[1], k[0], k[1], True, True)
                product(ps[:, tau, 256:512], q[0], q[1], c[0], c[1], True, True).then_inc(ns_ps, 1)

            def na_transpose(g):
                pe.wait_ge(ns_norm, g + 1)
                if g >= 2:
                    pe.wait_ge(np_l, g - 1)
                for c in range(4):
                    last = nc.tensor.transpose(bank(4 + g % 2)[:, c * P:c * P + P], sc[:, g % 4, c * P:c * P + P], ident)
                last.then_inc(np_ps, 1)

            def na_values(g):
                head, tau = divmod(g, 4)
                a, cols = head // 2, slice(64 * (head % 2), 64 * (head % 2) + 64)
                pe.wait_ge(np_l, g + 1)
                if tau == 0:
                    pe.wait_ge(nv_lo, 3 * a + 3)
                    if head:
                        pe.wait_ge(no_lo, head)
                for c in range(4):
                    chunk = 2 * tau + c if c < 2 else 6 + c
                    last = product(bank(6)[0:64, tau * P:tau * P + P], vt_h[a % 2][:, chunk, cols], vt_l[a % 2][:, chunk, cols],
                                   np_hi[:, g % 2, c * P:c * P + P], np_lo[:, g % 2, c * P:c * P + P], c == 0, c == 3)
                if tau == 3:
                    last.then_inc(no_ps, 1)

            def na_v(a, r):
                if r < 2:
                    pe.wait_ge(vw_done, 4 * a + 2 * r + 2)
                if a or r:
                    pe.wait_ge(nv_lo, 3 * a + r)
                for x in range(4 if r < 2 else 2):
                    if r < 2:
                        tau, c = 2 * r + x // 2, x % 2
                        src = (vw if a else vw_first)[:, tau, 4 * c:4 * c + 4, :].rearrange("p r c -> p (r c)")
                    else:
                        src = vp[a % 2][:, SEQ + x * P:SEQ + x * P + P]
                    last = nc.tensor.transpose(bank(7)[:, x * P:x * P + P], src, ident)
                last.then_inc(nv_ps, 1)

            for g in range(4):
                na_scores(g)
            for r in range(3):
                na_v(0, r)
            for g in range(4 * NA_HEADS):
                na_transpose(g)
                if g + 4 < 4 * NA_HEADS:
                    na_scores(g + 4)
                if g:
                    na_values(g - 1)
                a, st = divmod(g, 8)
                if st in NA_V_STEPS and a + 1 < NA_HEADS // 2:
                    na_v(a + 1, NA_V_STEPS.index(st))
            na_values(4 * NA_HEADS - 1)

            pair_layer("na_o", q_hi, q_lo, arrive=lambda k: pe.wait_ge(no_lo, 2 * k + 2))
            norm_stats(4, 45)
            norm_spread(4)
            pair_layer("nup0", h_hi, h_lo, arrive=lambda k: pe.wait_ge(hlo, 4 * KT + k + 1))
            down_layer("ndown0", "nup0")
            pair_layer("nup1", h_hi, h_lo)
            down_layer("ndown1", "nup1")
            pe.wait_ge(evac, n_units)
            for n in range(TT):
                for k in range(KT):
                    last = nc.tensor.transpose(bank(2 * n + k // 4)[:, (k % 4) * P:(k % 4) * P + P],
                                               xT[:, k, n * P:n * P + P], ident)
                    if k % 4 == 3:
                        last.then_inc(out_T, 1)

        @block.gpsimd
        def _(pool):
            pool.memset(rpb_pad[:, :, :], 0.0).then_inc(rpb_zero, 1)
            pool.wait_ge(rpb_zero, 1)
            pool.dma_start(rpb_pad[:, :, 17:48], t["l0_na_rpb_2"].rearrange("h a c -> (h a) c")
                           .rearrange("(p o) c -> p o c", o=2)).then_inc(rpb_in, 16)
            pool.dma_start(bass.AP(rpb_scr, TABLE, [[COPY + 1, 16], [1, 16]]), rpb_pad[0:16, 0, 0:16]).then_inc(rpb_copy, 16)
            pool.wait_ge(rpb_in, 16)
            scr = rpb_scr.ap()
            with pool.Fori(0, 16, 1) as c:
                pool.dma_start(scr[at(c * (COPY + 1), TABLE)].rearrange("(p n) -> p n", p=120),
                               rpb_pad[:, :, :].rearrange("p o c -> p (o c)")).then_inc(rpb_copy, 16)
            pool.wait_ge(rpb_copy, 16 * 17)
            for row in range(GRID_H):
                pool.dma_start(bias_scr[row], bass.AP(rpb_scr, 16 + (7 - row) * 48, [[COPY, 16], [PITCH, NA_HEADS], [1, GRID_H * 48]])
                               ).then_inc(rpb_out, 16)

            w_mod = t["l0_w_mod_2"].rearrange("(k p) n -> p k n", p=P)
            pool.wait_ge(silu_c_done, 1)
            pool.wait_ge(mo_lo, 2 * MEM_HEADS)

            def mod_load(b, col):
                pool.dma_start(mod_raw[b][:, :, :], w_mod[:, :, at(col, 256)]).then_inc(mod_in[b], 16)

            def mod_sum(acc, step, b, vec, col):
                pool.tensor_tensor(mod_tmp[:, :, :], mod_raw[b][:, :, :],
                                   silu_c[:, vec:vec + 8].rearrange("p (k o) -> p k o", o=1).to_broadcast([P, KT, 256]),
                                   ALU.mult).then_inc(mod_step, 1)
                pool.wait_ge(mod_step, step + 1)
                pool.tensor_tensor(mod_tmp[:, 0:4, :], mod_tmp[:, 0:4, :], mod_tmp[:, 4:8, :], ALU.add).then_inc(mod_step, 1)
                pool.wait_ge(mod_step, step + 2)
                pool.tensor_tensor(mod_tmp[:, 0:2, :], mod_tmp[:, 0:2, :], mod_tmp[:, 2:4, :], ALU.add).then_inc(mod_step, 1)
                pool.wait_ge(mod_step, step + 3)
                pool.tensor_tensor(acc[:, at(col, 256)].rearrange("p (o n) -> p o n", o=1), mod_tmp[:, 0:1, :],
                                   mod_tmp[:, 1:2, :], ALU.add).then_inc(mod_step, 1)
                pool.wait_ge(mod_step, step + 4)

            def mod_chunk(acc, c, step, b, both, col, load):
                pool.wait_ge(mod_in[b], c * 8 + (16 if b == 0 else 8))
                mod_sum(acc, step, b, 0, col)
                if both:
                    mod_sum(acc, step + 4, b, 8, col + 1024)
                if load is not None:
                    mod_load(b, load)

            mod_load(0, 0)
            mod_load(1, 256)
            for group, (first, cols, both) in enumerate(MOD_GROUPS):
                acc = mod_acc[group % 2]
                if group == 1:
                    pool.wait_ge(hlo, 3 * KT)
                if group >= 2:
                    pool.wait_ge(mod_ps, group - 1)
                n, per = cols // 256, 8 if both else 4
                with pool.Fori(0, n // 2 - 1, 1) as i:
                    for b in range(2):
                        mod_chunk(acc, i * 2 + (first // 256 + b), i * (2 * per) + (32 * group + per * b), b, both,
                                  i * 512 + 256 * b, i * 512 + (first + 512 + 256 * b))
                for b in range(2):
                    c = n - 2 + b
                    mod_chunk(acc, first // 256 + c, 32 * group + per * c, b, both, 256 * c,
                              first + cols + 256 * b if group < 3 else None)

            b, n, _, _ = tab["na_qkv"]
            for i in range(4):
                pool.wait_ge(evac, b + 8 + i + 1)
                pool.dma_start(v_scr[2 * i:2 * i + 2].rearrange("t p n -> p t n"), v_out[:, :, :]).then_inc(v_spill, 16)

            def build_bias(head, kind):
                if kind == 0:
                    pool.wait_ge(gb_in[head % 2], 16 * (head // 2 + 1))
                w = cst[:, C_WIN + 32 * kind:C_WIN + 32 * kind + 32].rearrange("p (o j) -> p o j", o=1).to_broadcast([P, 8, 32])
                x0 = 16 - 8 * kind
                r = pool.tensor_tensor(bias[head % 2][:, kind, :, :], gb[head % 2][:, :, x0:x0 + 32], w, ALU.add)
                if kind == 2:
                    r.then_inc(bias_done, 1)

            for head in range(2):
                for kind in range(3):
                    build_bias(head, kind)

            def window_values(a, tau):
                pool.tensor_copy(vw[:, tau, :, :], grid(vp[a % 2][:, 0:SEQ])[:, :, span[tau]:span[tau] + 32]).then_inc(vw_done, 1)

            def normalise(g):
                pool.wait_ge(ns_rden, g + 1)
                pool.tensor_tensor(sc[:, g % 4, :], sc[:, g % 4, :], na_rden[:, g % 4:g % 4 + 1].to_broadcast([P, 512]),
                                   ALU.mult).then_inc(ns_norm, 1)

            normalise(0)
            for g in range(4 * NA_HEADS):
                if g + 1 < 4 * NA_HEADS:
                    normalise(g + 1)
                head, tau = divmod(g, 4)
                if tau and head + 2 < NA_HEADS:
                    if tau == 1:
                        pool.wait_ge(ns_max, 4 * head + 4)
                    build_bias(head + 2, tau - 1)
                a, st = divmod(g, 8)
                if st == 0 and a + 1 < NA_HEADS // 2:
                    if a == 0:
                        pool.wait_ge(v_spill, 64)
                    pool.wait_ge(nv_ps, 3 * (a + 1))
                    pool.wait_ge(vp_in[(a + 1) % 2], 16 * ((a + 1) // 2 + 1))
                if st in (0, 2, 3, 4) and a + 1 < NA_HEADS // 2:
                    window_values(a + 1, (0, 2, 3, 4).index(st))


_OUT_SHAPE = (1, SEQ, D)


def kernel(**inputs):
    import concourse.bacc as bacc
    from concourse.bass_utils import run_bass_kernel_spmd

    nc = bacc.Bacc("TRN2", target_bir_lowering=False, num_devices=1)
    arrays, t = {}, {}
    for name in INPUTS:
        a = np.ascontiguousarray(inputs[name])
        arrays[f"in_{name}"] = a
        t[name] = nc.dram_tensor(f"in_{name}", a.shape, mybir.dt.from_np(a.dtype), kind="ExternalInput").ap()
    arrays["in_consts"] = constants()
    consts = nc.dram_tensor("in_consts", (P, C_ALL), F32, kind="ExternalInput").ap()
    out = nc.dram_tensor("out", _OUT_SHAPE, F32, kind="ExternalOutput").ap()
    program(nc, t, consts, out)
    r = run_bass_kernel_spmd(nc, [arrays], core_ids=[0])
    return r.results[0]["out"]
```
